# Optimizing a Trainium2 kernel written in Bass

```python
import math
import jax
import jax.numpy as jnp
from jax import lax
import numpy as np

D_MODEL = 1024
BATCH = 1
SEQ = 1024
DEPTH = 2
DEC_BATCH = 8
DEC_SEQ = 8
PAST_LEN = 4096
PAGE_SIZE = 128

HEAD_DIM = 64
NSA_HEADS = 12
NSA_KV_HEADS = 2
NSA_GROUP = NSA_HEADS // NSA_KV_HEADS
NSA_WIDTH = NSA_HEADS * HEAD_DIM
NSA_KV_WIDTH = NSA_KV_HEADS * HEAD_DIM
CMP_BLOCK = 64
CMP_HIDDEN = 128
SLC_BLOCK = CMP_BLOCK
SLC_TOPN = 16
WINDOW = 512
Q_CHUNK = 64
FORCED_SCORE = 1e4
XATTN_HEADS = 4
XATTN_WIDTH = XATTN_HEADS * HEAD_DIM
N_MEM = 256
POOL_WINDOWS = (2, 4, 8, 16)
POOL_GROUPS = len(POOL_WINDOWS)
POOL_GROUP_DIM = 192
POOL_WIDTH = POOL_GROUPS * POOL_GROUP_DIM
POOL_STATE = max(POOL_WINDOWS) - 1
MIX_WIDTH = NSA_WIDTH + XATTN_WIDTH
NSA_IN_WIDTH = NSA_WIDTH + 6 * NSA_KV_WIDTH + 3 * NSA_HEADS + XATTN_WIDTH
POOL_IN_WIDTH = POOL_WIDTH + XATTN_WIDTH
D_FF = 2816
CONV_WIDTH = 3
REL_BUCKETS = 32
REL_MAX_DIST = 128
N_NSA_LAYERS = (DEPTH + 1) // 2
N_POOL_LAYERS = DEPTH // 2
EPS = 1e-6
NEG_INF = -1e30

kernel_name = 'nsa_pool_hybrid_decode_step'

def rmsnorm(x, g):
    xf = x.astype(jnp.float32)
    y = xf * lax.rsqrt(jnp.mean(xf * xf, axis=-1, keepdims=True) + EPS)
    return (y * g.astype(jnp.float32)).astype(x.dtype)

def rel_bucket(dist):
    n = jnp.maximum(dist, 0)
    max_exact = REL_BUCKETS // 2
    nf = jnp.maximum(n, 1).astype(jnp.float32)
    large = max_exact + (jnp.log(nf / max_exact) / math.log(REL_MAX_DIST / max_exact)
                         * (REL_BUCKETS - max_exact)).astype(jnp.int32)
    large = jnp.minimum(large, REL_BUCKETS - 1)
    return jnp.where(n < max_exact, n, large)

def masked_softmax(logits, mask):
    p = jax.nn.softmax(jnp.where(mask, logits, NEG_INF), axis=-1)
    return jnp.where(mask, p, 0.0)

def compress(rows, pos, w1, b1, w2, b2):
    b, lc, g, dh = rows.shape
    blk = rows.reshape(b, lc // CMP_BLOCK, CMP_BLOCK, g, dh) + pos[None, None, :, None, :]
    h = jax.nn.gelu(jnp.einsum('bclgd,ldh->bcgh', blk, w1) + b1)
    return jnp.einsum('bcgh,hd->bcgd', h, w2) + b2

def nsa_sources(full, k_gain, cmp_params):
    cpos, cw1, cb1, cw2, cb2 = cmp_params
    b, l, _, g, dh = full.shape
    nc = l // CMP_BLOCK
    rc = full[:, :nc * CMP_BLOCK]
    kc = rmsnorm(compress(rc[:, :, 0], cpos[0], cw1[0], cb1[0], cw2[0], cb2[0]), k_gain)
    vc = compress(rc[:, :, 1], cpos[1], cw1[1], cb1[1], cw2[1], cb2[1])
    c_end = jnp.arange(nc, dtype=jnp.int32) * CMP_BLOCK + (CMP_BLOCK - 1)
    nb = -(-l // SLC_BLOCK)
    sel = jnp.pad(full[:, :, 2:4], ((0, 0), (0, nb * SLC_BLOCK - l), (0, 0), (0, 0), (0, 0)))
    sel = sel.reshape(b, nb, SLC_BLOCK, 2, g, dh)
    return kc, vc, c_end, sel[:, :, :, 0], sel[:, :, :, 1]

def nsa_attend(q, q_pos, gates, kc, vc, c_end, ks_blk, vs_blk, kw, vw, kw_pos, rel_bias):
    b, nq, g, r, dh = q.shape
    scale = dh ** -0.5
    nb = ks_blk.shape[1]
    nc = kc.shape[1]
    d_c = q_pos[:, None] - c_end[None, :]
    bias_c = rel_bias[rel_bucket(d_c)].transpose(2, 0, 1).reshape(g, r, nq, nc)
    l_c = jnp.einsum('bqgrd,bcgd->bgrqc', q, kc).astype(jnp.float32) * scale + bias_c
    p_c = masked_softmax(l_c, d_c >= 0)
    o_c = jnp.einsum('bgrqc,bcgd->bqgrd', p_c.astype(vc.dtype), vc)
    blk = jnp.arange(nb, dtype=jnp.int32)[None, :]
    cur = (q_pos // SLC_BLOCK)[:, None]
    valid = blk * SLC_BLOCK <= q_pos[:, None]
    forced = (blk == 0) | (blk == cur) | (blk == cur - 1)
    imp = jnp.pad(p_c.sum(axis=2), ((0, 0), (0, 0), (0, 0), (0, nb - nc)))
    score = jnp.where(valid, jnp.where(forced, FORCED_SCORE, imp), -1.0)
    top_val, top_idx = lax.top_k(score, min(SLC_TOPN, nb))
    n_sel = top_idx.shape[-1]
    bi = jnp.arange(b)[:, None, None, None]
    gi = jnp.arange(g)[None, :, None, None]
    k_sel = ks_blk.transpose(0, 3, 1, 2, 4)[bi, gi, top_idx]
    v_sel = vs_blk.transpose(0, 3, 1, 2, 4)[bi, gi, top_idx]
    pos_sel = top_idx[..., None] * SLC_BLOCK + jnp.arange(SLC_BLOCK, dtype=jnp.int32)
    d_s = q_pos[None, None, :, None, None] - pos_sel
    m_s = ((d_s >= 0) & (top_val >= 0.0)[..., None]).reshape(b, g, 1, nq, n_sel * SLC_BLOCK)
    rb = rel_bias.reshape(REL_BUCKETS, g, r)
    bias_s = jnp.moveaxis(rb[rel_bucket(d_s), gi[..., None]], -1, 2).reshape(b, g, r, nq, n_sel * SLC_BLOCK)
    l_s = jnp.einsum('bqgrd,bgqkld->bgrqkl', q, k_sel).astype(jnp.float32)
    l_s = l_s.reshape(b, g, r, nq, n_sel * SLC_BLOCK) * scale + bias_s
    p_s = masked_softmax(l_s, m_s)
    o_s = jnp.einsum('bgrqn,bgqnd->bqgrd', p_s.astype(v_sel.dtype),
                     v_sel.reshape(b, g, nq, n_sel * SLC_BLOCK, dh))
    d_w = q_pos[:, None] - kw_pos[None, :]
    m_w = (d_w >= 0) & (d_w <= WINDOW) & (kw_pos >= 0)[None, :]
    bias_w = rel_bias[rel_bucket(d_w)].transpose(2, 0, 1).reshape(g, r, nq, kw_pos.shape[0])
    l_w = jnp.einsum('bqgrd,bwgd->bgrqw', q, kw).astype(jnp.float32) * scale + bias_w
    p_w = masked_softmax(l_w, m_w)
    o_w = jnp.einsum('bgrqw,bwgd->bqgrd', p_w.astype(vw.dtype), vw)
    o = gates[..., 0:1] * o_c + gates[..., 1:2] * o_s + gates[..., 2:3] * o_w
    return o.reshape(b, nq, g * r * dh)

def nsa_mix(z, q_gain, k_gain, cmp_params, rel_bias, past_rows, win_buf):
    b, l, _ = z.shape
    o1 = NSA_WIDTH + 6 * NSA_KV_WIDTH
    q = rmsnorm(z[..., :NSA_WIDTH].reshape(b, l, NSA_HEADS, HEAD_DIM), q_gain)
    q = q.reshape(b, l, NSA_KV_HEADS, NSA_GROUP, HEAD_DIM)
    kv = z[..., NSA_WIDTH:o1].reshape(b, l, 6, NSA_KV_HEADS, HEAD_DIM)
    gates = jax.nn.sigmoid(z[..., o1:o1 + 3 * NSA_HEADS]).reshape(b, l, NSA_KV_HEADS, NSA_GROUP, 3)
    k_slc = rmsnorm(kv[:, :, 2], k_gain)
    k_win = rmsnorm(kv[:, :, 4], k_gain)
    new_rows = jnp.stack([kv[:, :, 0], kv[:, :, 1], k_slc, kv[:, :, 3]], axis=2)
    win_rows = jnp.stack([k_win, kv[:, :, 5]], axis=2)
    if past_rows is None:
        pos0 = 0
        full = new_rows
    else:
        pos0 = past_rows.shape[1]
        full = jnp.concatenate([past_rows, new_rows], axis=1)
    kc, vc, c_end, ks_blk, vs_blk = nsa_sources(full, k_gain, cmp_params)
    if win_buf is None:
        win_pad = jnp.pad(win_rows, ((0, 0), (WINDOW, 0), (0, 0), (0, 0), (0, 0)))

        def chunk(i):
            s0 = i * Q_CHUNK
            qc = lax.dynamic_slice_in_dim(q, s0, Q_CHUNK, axis=1)
            gc = lax.dynamic_slice_in_dim(gates, s0, Q_CHUNK, axis=1)
            wc = lax.dynamic_slice_in_dim(win_pad, s0, WINDOW + Q_CHUNK, axis=1)
            q_pos = s0 + jnp.arange(Q_CHUNK, dtype=jnp.int32)
            kw_pos = s0 - WINDOW + jnp.arange(WINDOW + Q_CHUNK, dtype=jnp.int32)
            return nsa_attend(qc, q_pos, gc, kc, vc, c_end, ks_blk, vs_blk,
                              wc[:, :, 0], wc[:, :, 1], kw_pos, rel_bias)

        outs = lax.map(chunk, jnp.arange(l // Q_CHUNK, dtype=jnp.int32))
        out = outs.transpose(1, 0, 2, 3).reshape(b, l, NSA_WIDTH)
        new_win = win_rows[:, -min(WINDOW, l):]
    else:
        wb = win_buf.shape[1]
        wall = jnp.concatenate([win_buf, win_rows], axis=1)
        q_pos = pos0 + jnp.arange(l, dtype=jnp.int32)
        kw_pos = pos0 - wb + jnp.arange(wb + l, dtype=jnp.int32)
        out = nsa_attend(q, q_pos, gates, kc, vc, c_end, ks_blk, vs_blk,
                         wall[:, :, 0], wall[:, :, 1], kw_pos, rel_bias)
        new_win = wall[:, -wb:]
    return out, new_rows, new_win

def pool_mix(u, pos0, prev, w_grp, scale):
    b, l, _ = u.shape
    ext = jnp.concatenate([prev, u], axis=1).astype(jnp.float32)
    cs = jnp.cumsum(jnp.pad(ext, ((0, 0), (1, 0), (0, 0))), axis=1)
    pos = pos0 + jnp.arange(l, dtype=jnp.int32)
    e0 = POOL_STATE + 1
    outs = []
    for gidx, w in enumerate(POOL_WINDOWS):
        sl = slice(gidx * POOL_GROUP_DIM, (gidx + 1) * POOL_GROUP_DIM)
        s = cs[:, e0:e0 + l, sl] - cs[:, e0 - w:e0 - w + l, sl]
        cnt = jnp.minimum(w, pos + 1).astype(jnp.float32)[None, :, None]
        outs.append(s / cnt)
    pooled = (jnp.concatenate(outs, axis=-1) - u.astype(jnp.float32)).astype(u.dtype)
    mixed = jnp.einsum('blgc,gcd->blgd', pooled.reshape(b, l, POOL_GROUPS, POOL_GROUP_DIM), w_grp)
    return mixed.reshape(b, l, POOL_WIDTH) * scale, ext[:, -POOL_STATE:].astype(u.dtype)

def memory_kv(mem, g_mem, w_mem_kv, xk_gain):
    b, m, _ = mem.shape
    kv = (rmsnorm(mem, g_mem) @ w_mem_kv).reshape(b, m, 2, XATTN_HEADS, HEAD_DIM)
    return jnp.stack([rmsnorm(kv[:, :, 0], xk_gain), kv[:, :, 1]], axis=2)

def memory_attend(zq, xq_gain, mkv):
    b, l, _ = zq.shape
    q = rmsnorm(zq.reshape(b, l, XATTN_HEADS, HEAD_DIM), xq_gain)
    logits = jnp.einsum('blhd,bmhd->bhlm', q, mkv[:, :, 0]).astype(jnp.float32) * HEAD_DIM ** -0.5
    p = jax.nn.softmax(logits, axis=-1).astype(mkv.dtype)
    return jnp.einsum('bhlm,bmhd->blhd', p, mkv[:, :, 1]).reshape(b, l, XATTN_WIDTH)

def conv_ffn(h, prev, w_up, conv_w, conv_b, w_down):
    l = h.shape[1]
    u = h @ w_up
    ext = jnp.concatenate([prev, u], axis=1)
    y = conv_b + sum(conv_w[k] * ext[:, k:k + l] for k in range(CONV_WIDTH))
    a, v = jnp.split(y, 2, axis=-1)
    return (jax.nn.silu(a) * v) @ w_down, ext[:, -(CONV_WIDTH - 1):]

def setup_inputs(seed: int = 0) -> dict:
    key = jax.random.key(seed)
    keys = iter(jax.random.split(key, 48))

    def nrm(shape, scale):
        return jax.random.normal(next(keys), shape, jnp.float32) * scale

    n_pages = PAST_LEN // PAGE_SIZE
    n_used = DEC_BATCH * n_pages
    n_phys = n_used + (n_used + 3) // 4
    wb = min(WINDOW, PAST_LEN)
    page_table = jax.random.permutation(next(keys), n_phys)[:n_used].reshape(DEC_BATCH, n_pages).astype(jnp.int32)
    return {
        'x_prompt': nrm((BATCH, SEQ, D_MODEL), 1.0),
        'x_sample': nrm((DEC_BATCH, DEC_SEQ, D_MODEL), 1.0),
        'cache_nsa_kv': nrm((N_NSA_LAYERS, n_phys, PAGE_SIZE, 4, NSA_KV_HEADS, HEAD_DIM), 1.0),
        'cache_nsa_win': nrm((N_NSA_LAYERS, DEC_BATCH, wb, 2, NSA_KV_HEADS, HEAD_DIM), 1.0),
        'cache_mem_kv': nrm((DEPTH, DEC_BATCH, N_MEM, 2, XATTN_HEADS, HEAD_DIM), 1.0),
        'state_pool': nrm((N_POOL_LAYERS, DEC_BATCH, POOL_STATE, POOL_WIDTH), 1.0),
        'state_ffn_conv': nrm((DEPTH, DEC_BATCH, CONV_WIDTH - 1, 2 * D_FF), 1.0),
        'page_table': page_table,
        'mem_prompt': nrm((BATCH, N_MEM, D_MODEL), 1.0),
        'rel_bias': nrm((REL_BUCKETS, NSA_HEADS), 0.5),
        'g_mix': 1.0 + nrm((DEPTH, D_MODEL), 0.05),
        'g_mem': 1.0 + nrm((DEPTH, D_MODEL), 0.05),
        'g_ffn': 1.0 + nrm((DEPTH, D_MODEL), 0.05),
        'w_in_nsa': nrm((N_NSA_LAYERS, D_MODEL, NSA_IN_WIDTH), D_MODEL ** -0.5),
        'q_gain_nsa': 1.0 + nrm((N_NSA_LAYERS, HEAD_DIM), 0.05),
        'k_gain_nsa': 1.0 + nrm((N_NSA_LAYERS, HEAD_DIM), 0.05),
        'cmp_pos': nrm((N_NSA_LAYERS, 2, CMP_BLOCK, HEAD_DIM), 0.1),
        'cmp_w1': nrm((N_NSA_LAYERS, 2, CMP_BLOCK, HEAD_DIM, CMP_HIDDEN), (CMP_BLOCK * HEAD_DIM) ** -0.5),
        'cmp_b1': nrm((N_NSA_LAYERS, 2, CMP_HIDDEN), 0.01),
        'cmp_w2': nrm((N_NSA_LAYERS, 2, CMP_HIDDEN, HEAD_DIM), CMP_HIDDEN ** -0.5),
        'cmp_b2': nrm((N_NSA_LAYERS, 2, HEAD_DIM), 0.01),
        'w_in_pool': nrm((N_POOL_LAYERS, D_MODEL, POOL_IN_WIDTH), D_MODEL ** -0.5),
        'w_pool_grp': nrm((N_POOL_LAYERS, POOL_GROUPS, POOL_GROUP_DIM, POOL_GROUP_DIM), POOL_GROUP_DIM ** -0.5),
        'pool_scale': 1.0 + nrm((N_POOL_LAYERS, POOL_WIDTH), 0.05),
        'w_mem_kv': nrm((DEPTH, D_MODEL, 2 * XATTN_WIDTH), D_MODEL ** -0.5),
        'xq_gain': 1.0 + nrm((DEPTH, HEAD_DIM), 0.05),
        'xk_gain': 1.0 + nrm((DEPTH, HEAD_DIM), 0.05),
        'w_out': nrm((DEPTH, MIX_WIDTH, D_MODEL), MIX_WIDTH ** -0.5),
        'w_up': nrm((DEPTH, D_MODEL, 2 * D_FF), D_MODEL ** -0.5),
        'conv_w': nrm((DEPTH, CONV_WIDTH, 2 * D_FF), CONV_WIDTH ** -0.5),
        'conv_b': nrm((DEPTH, 2 * D_FF), 0.01),
        'w_down': nrm((DEPTH, D_FF, D_MODEL), D_FF ** -0.5),
    }

def reference(x_prompt, x_sample, cache_nsa_kv, cache_nsa_win, cache_mem_kv, state_pool, state_ffn_conv,
              page_table, mem_prompt, rel_bias, g_mix, g_mem, g_ffn, w_in_nsa, q_gain_nsa, k_gain_nsa,
              cmp_pos, cmp_w1, cmp_b1, cmp_w2, cmp_b2, w_in_pool, w_pool_grp, pool_scale, w_mem_kv,
              xq_gain, xk_gain, w_out, w_up, conv_w, conv_b, w_down):
    n_pages = page_table.shape[1]
    past_len = n_pages * PAGE_SIZE
    yp, ys = x_prompt, x_sample
    bp, bs = yp.shape[0], ys.shape[0]
    nsa_kv_p, nsa_kv_s, nsa_win_p, nsa_win_s = [], [], [], []
    mem_kv_p, pool_p, pool_s, conv_p, conv_s = [], [], [], [], []
    for i in range(DEPTH):
        j = i // 2
        xn_p = rmsnorm(yp, g_mix[i])
        xn_s = rmsnorm(ys, g_mix[i])
        mkv_p = memory_kv(mem_prompt, g_mem[i], w_mem_kv[i], xk_gain[i])
        mkv_s = cache_mem_kv[i]
        mem_kv_p.append(mkv_p)
        if i % 2 == 0:
            zp = xn_p @ w_in_nsa[j]
            zs = xn_s @ w_in_nsa[j]
            cmp_params = (cmp_pos[j], cmp_w1[j], cmp_b1[j], cmp_w2[j], cmp_b2[j])
            past_rows = cache_nsa_kv[j, page_table].reshape(bs, past_len, 4, NSA_KV_HEADS, HEAD_DIM)
            mix_p, rows_p, win_p = nsa_mix(zp, q_gain_nsa[j], k_gain_nsa[j], cmp_params, rel_bias, None, None)
            mix_s, rows_s, win_s = nsa_mix(zs, q_gain_nsa[j], k_gain_nsa[j], cmp_params, rel_bias,
                                           past_rows, cache_nsa_win[j])
            nsa_kv_p.append(rows_p)
            nsa_kv_s.append(rows_s)
            nsa_win_p.append(win_p)
            nsa_win_s.append(win_s)
        else:
            zp = xn_p @ w_in_pool[j]
            zs = xn_s @ w_in_pool[j]
            mix_p, st_p = pool_mix(zp[..., :POOL_WIDTH], 0, jnp.zeros((bp, POOL_STATE, POOL_WIDTH), zp.dtype),
                                   w_pool_grp[j], pool_scale[j])
            mix_s, st_s = pool_mix(zs[..., :POOL_WIDTH], past_len, state_pool[j], w_pool_grp[j], pool_scale[j])
            pool_p.append(st_p)
            pool_s.append(st_s)
        att_p = memory_attend(zp[..., -XATTN_WIDTH:], xq_gain[i], mkv_p)
        att_s = memory_attend(zs[..., -XATTN_WIDTH:], xq_gain[i], mkv_s)
        yp = yp + jnp.concatenate([mix_p, att_p], axis=-1) @ w_out[i]
        ys = ys + jnp.concatenate([mix_s, att_s], axis=-1) @ w_out[i]
        f_p, c_p = conv_ffn(rmsnorm(yp, g_ffn[i]), jnp.zeros((bp, CONV_WIDTH - 1, 2 * D_FF), yp.dtype),
                            w_up[i], conv_w[i], conv_b[i], w_down[i])
        f_s, c_s = conv_ffn(rmsnorm(ys, g_ffn[i]), state_ffn_conv[i], w_up[i], conv_w[i], conv_b[i], w_down[i])
        yp = yp + f_p
        ys = ys + f_s
        conv_p.append(c_p)
        conv_s.append(c_s)
    return (yp, ys, jnp.stack(nsa_kv_p), jnp.stack(nsa_kv_s), jnp.stack(nsa_win_p), jnp.stack(nsa_win_s),
            jnp.stack(mem_kv_p), jnp.stack(pool_p), jnp.stack(pool_s), jnp.stack(conv_p), jnp.stack(conv_s))


_drawn_inputs = setup_inputs


def setup_inputs(seed=0):
    import zlib

    import numpy as np

    out = dict(_drawn_inputs(seed))
    spreads = {}
    factors = {'q_gain_nsa': 8.0, 'cmp_b1': 8.0, 'cmp_b2': 8.0, 'xq_gain': 8.0, 'conv_b': 5.962}
    for name, (base, spread) in spreads.items():
        noise = np.random.default_rng([zlib.crc32(name.encode()), seed]).standard_normal(out[name].shape)
        drawn = base * np.exp(spread * noise) if base else spread * noise
        out[name] = jnp.asarray(drawn.astype(out[name].dtype))
    for name, factor in factors.items():
        out[name] = (out[name] * factor).astype(out[name].dtype)
    return out
```

```python
from contextlib import ExitStack

import numpy as np
import concourse.bass as bass
from concourse import mybir

F32 = mybir.dt.float32
I32 = mybir.dt.int32
ALU = mybir.AluOpType
ACT = mybir.ActivationFunctionType
X = mybir.AxisListType.X

P = 128
D_MODEL = 1024
KC = D_MODEL // P
SEQ = 1024
B, L = 8, 8
TS = B * L
T = SEQ + TS
QT = SEQ // P
PAST = 4096
PAGE = 128
PAGES = PAST // PAGE
HD = 64
G, R = 2, 6
H = G * R
ROWS = H * L
GR = R * L
CB = 64
L2 = CB // 2
NCP = SEQ // CB
NCS = PAST // CB
NBS = NCS + 1
WINDOW = 512
XH = 4
NMEM = 256
DFF = 2816
FC = DFF // P
HALVES = 2
FH = FC // HALVES
PG = 192
PCH = 96
NPC = 8
POOLW = (2, 4, 8, 16)
PST = 15
BUCKETS = 32
RW = 384
NEG = -1e30
FORCED = 1e4
SCALE = HD ** -0.5
LOWEST = -3e38
TAIL = P + L
NT = ((0, 512), (512, 512), (1024, 64))

Z_Q, Z_KS, Z_KW, Z_XQ, Z_KC, Z_VC, Z_VS, Z_VW, Z_GATE = 0, 6, 7, 8, 10, 11, 12, 13, 14
NZ = 15
NORMED = 10
WHOLE = NORMED + 2


def pairs(eng, n, body):
    if n // 2:
        with eng.Fori(0, n // 2) as j:
            body(j * 2, j, 0)
            body(j * 2 + 1, j, 1)
    if n % 2:
        body(n - 1, n // 2, 0)


class Kernel:

    def __init__(self, nc, ctx, ins, outs):
        self.nc, self.ctx, self.ins, self.outs = nc, ctx, ins, outs
        self.made = 0
        self.sems_of, self.sems = None, []
        self.cleared = []

    def sb(self, ctx, name, shape, dtype=F32):
        self.made += 1
        return ctx.enter_context(self.nc.sbuf_tensor(f"{name}_{self.made}", shape, dtype))

    def retire(self, sems):
        for s in self.cleared:
            self.nc.release_semaphore(s)
        for s in sems:
            self.nc.gpsimd.sem_clear(s)
        self.cleared = sems

    def sem(self, ctx, name):
        if self.sems_of is not ctx:
            self.sems_of, self.sems = ctx, []
            ctx.callback(self.retire, self.sems)
        self.made += 1
        self.sems.append(self.nc.alloc_semaphore(f"{name}_{self.made}"))
        return self.sems[-1]


def wait_apart(k, eng, sem, value):
    eng.wait_ge(sem, value)
    eng.sem_inc(k.passed, 1)


LOOKUP = 8


def load_pages(k, sp, b, pages, dst, loaded):
    with sp.Fori(0, PAGES // LOOKUP) as i:
        _, found = k.nc.values_load_multi_w_load_instructions(
            k.cst["page_table"][0:1, bass.ds(b * PAGES + i * LOOKUP, LOOKUP)], engines=(mybir.EngineType.SP,),
            min_val=0, max_val=k.n_pages - 1)
        for x in range(LOOKUP):
            sp.dma_start(dst[:, bass.ds(i * LOOKUP + x, 1), :].rearrange("p a n -> p (a n)"), pages[found[x]]).then_inc(loaded, 16)


def bank_set(k, s):
    return k.ps[:, 3 * s:3 * s + 3, :].rearrange("p b n -> p (b n)")[:, 0:T]


def samples(ap):
    return ap[:, SEQ:T].rearrange("p (b q) -> p b q", b=B)


def load_constants(k, octx, names):
    for n in names:
        k.cst[n] = k.sb(octx, n, CONSTANTS[n], I32 if n in SMALL_INTEGERS else F32)
    with ExitStack() as ctx:
        loaded = k.sem(ctx, "constants_loaded")
        block = ctx.enter_context(k.nc.Block())

        @block.sync
        def _(sp):
            for n in names:
                sp.dma_start(k.cst[n][:], k.ins[n]).then_inc(loaded, 16)
            sp.wait_ge(loaded, 16 * len(names))


def bias_tables(k):
    nc, c = k.nc, k.cst
    with ExitStack() as ctx:
        load_constants(k, ctx, TABLES)
        row = k.sb(ctx, "bias_row", [H, RW])
        hank = k.sb(ctx, "bias_hankel", [P, H, 256])
        row_ready = k.sem(ctx, "bias_row_product")
        row_read = k.sem(ctx, "bias_row_read")
        row_stored = k.sem(ctx, "bias_row_stored")
        tables_loaded = k.sem(ctx, "tables_loaded")
        flipped = k.sem(ctx, "tables_flipped")
        block = ctx.enter_context(nc.Block())

        @block.tensor
        def _(pe):
            pe.matmul(k.ps[0:H, 0, 0:RW], c["relx"][:, :], c["onehot"][:, :], start=True, stop=True).then_inc(row_ready, 1)
            pe.wait_ge(tables_loaded, 16 * (1 + 2 * L))
            for i in range(6):
                last = pe.matmul(k.ps[:, i, :], c["flip"][:, :], hank[:, 2 * i:2 * i + 2, :], start=True, stop=True)
            last.then_inc(flipped, 1)

        @block.vector
        def _(dve):
            dve.wait_ge(row_ready, 1)
            dve.tensor_copy(row[:], k.ps[0:H, 0, 0:RW]).then_inc(row_read, 1)
            dve.wait_ge(flipped, 1)
            dve.tensor_copy(k.near_bias[:], k.ps[:, 0:6, :].rearrange("p i (h n) -> p (i h) n", h=2))
            dve.memset(k.block_bias[:], NEG)
            dve.drain()
            dve.tensor_copy(k.block_bias[:, :, 14:18], k.near_bias[:, :, CB - 1:256:CB])
            dve.tensor_copy(k.block_bias[:, :, 0:14], k.near_bias[:, :, 0:1].broadcast_to([P, H, 14]))
            far = k.row_far[:, 0:1]
            dve.tensor_copy(k.row_blocks[:, 0:NCS - 2], far.broadcast_to([ROWS, NCS - 2]))
            dve.tensor_copy(k.row_blocks[:, NCS - 2:NCS - 1], k.row_tail[:, 63:64])
            dve.tensor_copy(k.row_blocks[:, NCS - 1:NCS], k.row_tail[:, 127:128])
            dve.memset(k.row_select[:], 0.0)
            dve.drain()
            dve.tensor_copy(k.row_select[:, 0:NCS - 2], far.broadcast_to([ROWS, NCS - 2]))
            dve.tensor_copy(k.row_window[:, 0:WINDOW - P], far.broadcast_to([ROWS, WINDOW - P]))
            dve.tensor_copy(k.row_window[:, WINDOW - P:WINDOW + L], k.row_tail[:, :])
            dve.drain()
            dve.tensor_tensor(k.row_window[:, 0:L], k.row_window[:, 0:L], c["win_mask"][:, :], ALU.add)

        @block.sync
        def _(sp):
            sp.wait_ge(row_read, 1)
            sp.dma_start(k.row_dram, row[:]).then_inc(row_stored, 16)
            sp.wait_ge(row_stored, 16)
            sp.dma_start(hank[:], bass.AP(k.row_dram.tensor, 0, [[1, P], [RW, H], [1, 256]])).then_inc(tables_loaded, 16)
            for q in range(L):
                sp.dma_start(k.row_tail[q:ROWS:L, :], k.row_dram[:, 127 - q:127 - q + TAIL]).then_inc(tables_loaded, 16)
                sp.dma_start(k.row_far[q:ROWS:L, :], k.row_dram[:, 0:2]).then_inc(tables_loaded, 16)
            sp.wait_ge(tables_loaded, 16 * (1 + 2 * L))


def load_x(k, x, src):
    with ExitStack() as ctx:
        loaded = k.sem(ctx, "x_loaded")
        block = ctx.enter_context(k.nc.Block())

        @block.sync
        def _(sp):
            sp.dma_start(x[:], src.rearrange("k p t -> p k t")).then_inc(loaded, 16)
            sp.wait_ge(loaded, 16)


def rms_norm(k, x, out, gain, n):
    c = k.cst
    cuts = [(a, min(512, n - a)) for a in range(0, n, 512)]
    with ExitStack() as ctx:
        sq = k.sb(ctx, "squares", [P, 2, n])
        rms = k.sb(ctx, "rms", [P, n])
        rstd = k.sb(ctx, "rstd", [P, n])
        squared = k.sem(ctx, "squared")
        summed = k.sem(ctx, "squares_summed")
        rooted = k.sem(ctx, "rooted")
        block = ctx.enter_context(k.nc.Block())
        total = k.ps[:, 0:3, :].rearrange("p b n -> p (b n)")[:, 0:n]

        @block.scalar
        def _(act):
            for i in range(KC):
                if i >= 2:
                    act.wait_ge(summed, i - 1)
                act.activation(sq[:, i % 2, :], x[:, i, :], ACT.Square).then_inc(squared, 1)
            act.wait_ge(summed, KC)
            act.activation(rms[:], total, ACT.Sqrt, bias=c["norm_bias"][:, WHOLE:WHOLE + 1],
                           scale=c["norm_scale"][:, WHOLE:WHOLE + 1]).then_inc(rooted, 1)

        @block.tensor
        def _(pe):
            for i in range(KC):
                pe.wait_ge(squared, i + 1)
                for a, w in cuts:
                    last = pe.matmul(total[:, a:a + w], c["ones"][:, :], sq[:, i % 2, a:a + w],
                                     start=i == 0, stop=i == KC - 1)
                last.then_inc(summed, 1)

        @block.vector
        def _(dve):
            dve.wait_ge(rooted, 1)
            dve.reciprocal(rstd[:], rms[:])
            dve.drain()
            for i in range(KC):
                dve.scalar_tensor_tensor(out=out[:, i, :], in0=x[:, i, :], scalar=gain[:, i:i + 1],
                                         in1=rstd[:], op0=ALU.mult, op1=ALU.mult)


def project(k, name, w_src, n, terms, read, width=P):
    with ExitStack() as ctx:
        w = k.sb(ctx, name + "_weights", [P, 2, len(terms), width])
        w_loaded = [k.sem(ctx, f"{name}_weights_loaded{s}") for s in range(2)]
        multiplied = k.sem(ctx, name + "_multiplied")
        taken = k.sem(ctx, name + "_taken")
        block = ctx.enter_context(k.nc.Block())

        @block.sync
        def _(sp):
            def load(m, j, s):
                sp.wait_ge(multiplied, m + 1)
                sp.dma_start(w[:, s, :, :], w_src[m]).then_inc(w_loaded[s], 16)
            pairs(sp, n, load)

        @block.tensor
        def _(pe):
            pe.sem_inc(multiplied, 2)

            def multiply(m, j, s):
                pe.wait_ge(w_loaded[s], j * 16 + 16)
                pe.wait_ge(taken, m + 1)
                out = bank_set(k, s)
                for a, cols in NT:
                    for kk, (rows, moving) in enumerate(terms):
                        last = pe.matmul(out[0:width, a:a + cols], w[0:rows, s, kk, :], moving[:, a:a + cols],
                                         start=kk == 0, stop=kk == len(terms) - 1)
                last.then_inc(multiplied, 1)
            pairs(pe, n, multiply)

        @block.vector
        def _(dve):
            dve.sem_inc(taken, 2)

            def take(m, j, s):
                dve.wait_ge(multiplied, m + 3)
                read(dve, m, bank_set(k, s)).then_inc(taken, 1)
            pairs(dve, n, take)


def head_norms(k, z, n, first):
    c = k.cst
    with ExitStack() as ctx:
        sq = k.sb(ctx, "head_squares", [P, 2, T])
        rms = k.sb(ctx, "head_rms", [P, 2, T])
        rstd = k.sb(ctx, "head_rstd", [P, T])
        squared = k.sem(ctx, "head_squared")
        summed = k.sem(ctx, "head_summed")
        rooted = k.sem(ctx, "head_rooted")
        inverted = k.sem(ctx, "head_inverted")
        block = ctx.enter_context(k.nc.Block())

        @block.vector
        def _(dve):
            dve.sem_inc(inverted, 2)

            def normalise(m, j, s):
                dve.wait_ge(rooted, m + 1)
                dve.reciprocal(rstd[:], rms[:, s, :]).then_inc(inverted, 1)
                dve.drain()
                dve.scalar_tensor_tensor(out=z[:, m, :], in0=z[:, m, :], scalar=k.cst["gains"][:, bass.ds(m + first, 1)],
                                         in1=rstd[:], op0=ALU.mult, op1=ALU.mult)
                dve.drain()
            pairs(dve, n, normalise)

        @block.scalar
        def _(act):
            def square(m, j, s):
                act.activation(sq[:, s, :], z[:, m, :], ACT.Square).then_inc(squared, 1)
                act.wait_ge(summed, m + 1)
                act.wait_ge(inverted, m + 1)
                act.activation(rms[:, s, :], bank_set(k, s), ACT.Sqrt,
                               bias=c["norm_bias"][:, bass.ds(m + first, 1)],
                               scale=c["norm_scale"][:, bass.ds(m + first, 1)]).then_inc(rooted, 1)
            pairs(act, n, square)

        @block.tensor
        def _(pe):
            def add(m, j, s):
                pe.wait_ge(squared, m + 1)
                pe.wait_ge(rooted, m)
                for a, cols in NT:
                    last = pe.matmul(bank_set(k, s)[:, a:a + cols], c["halves"][:, :], sq[:, s, a:a + cols],
                                     start=True, stop=True)
                last.then_inc(summed, 1)
            pairs(pe, n, add)


def memory_kv(k, layer, mem, memn):
    c = k.cst
    rms_norm(k, mem, memn, c["g_mem"][:, layer, :], NMEM)
    with ExitStack() as ctx:
        w = k.sb(ctx, "mem_weights", [P, KC, 4 * P])
        sq = k.sb(ctx, "mem_squares", [P, 2, NMEM])
        rms = k.sb(ctx, "mem_rms", [P, 2 * NMEM])
        keys = k.mem_k[:, layer, :, :]
        loaded = k.sem(ctx, "mem_weights_loaded")
        multiplied = k.sem(ctx, "mem_multiplied")
        squared = k.sem(ctx, "mem_squared")
        summed = k.sem(ctx, "mem_summed")
        rooted = k.sem(ctx, "mem_rooted")
        written = k.sem(ctx, "mem_written")
        stored = k.sem(ctx, "mem_stored")
        block = ctx.enter_context(k.nc.Block())

        @block.sync
        def _(sp):
            sp.dma_start(w[:], k.ins["w_mem"][layer]).then_inc(loaded, 16)
            sp.wait_ge(written, 1)
            sp.dma_start(k.outs["mem_k"][layer], keys).then_inc(stored, 16)
            sp.dma_start(k.outs["mem_v"][layer], k.mem_v[:, layer, :, :]).then_inc(stored, 16)
            sp.wait_ge(stored, 32)

        @block.tensor
        def _(pe):
            pe.wait_ge(loaded, 16)
            for ch in range(2):
                for kk in range(KC):
                    pe.matmul(k.ps[:, ch, 0:NMEM], w[:, kk, ch * P:(ch + 1) * P], memn[:, kk, :],
                              start=kk == 0, stop=kk == KC - 1)
            for mt in range(2):
                for kk in range(KC):
                    last = pe.matmul(k.ps[:, 2 + mt, 0:NMEM], memn[:, kk, mt * P:(mt + 1) * P], w[:, kk, 2 * P:4 * P],
                                     start=kk == 0, stop=kk == KC - 1)
            last.then_inc(multiplied, 1)
            pe.wait_ge(squared, 1)
            pe.matmul(k.ps[:, 4, :], c["halves"][:, :], sq[:, :, :], start=True, stop=True).then_inc(summed, 1)

        @block.scalar
        def _(act):
            act.wait_ge(multiplied, 1)
            act.activation(sq[:, :, :], k.ps[:, 0:2, 0:NMEM], ACT.Square).then_inc(squared, 1)
            act.wait_ge(summed, 1)
            act.activation(rms[:], k.ps[:, 4, :], ACT.Sqrt, bias=c["norm_bias"][:, Z_KS:Z_KS + 1],
                           scale=c["norm_scale"][:, Z_KS:Z_KS + 1]).then_inc(rooted, 1)

        @block.vector
        def _(dve):
            dve.wait_ge(multiplied, 1)
            dve.tensor_copy(k.mem_v[:, layer, :, :], k.ps[:, 2:4, 0:NMEM])
            dve.wait_ge(rooted, 1)
            dve.reciprocal(rms[:], rms[:])
            dve.drain()
            dve.scalar_tensor_tensor(out=keys, in0=k.ps[:, 0:2, 0:NMEM], scalar=c["xk_gain"][:, layer:layer + 1],
                                     in1=rms[:].rearrange("p (c n) -> p c n", c=2), op0=ALU.mult, op1=ALU.mult)
            dve.drain().then_inc(written, 1)


def token_major_values(k, z, vals):
    with ExitStack() as ctx:
        turned = k.sem(ctx, "values_turned")
        copied = k.sem(ctx, "values_copied")
        block = ctx.enter_context(k.nc.Block())

        @block.tensor
        def _(pe):
            for i in range(4):
                if i >= 2:
                    pe.wait_ge(copied, i - 1)
                for t in range(4):
                    last = pe.transpose(k.ps[:, i % 2, t * P:(t + 1) * P],
                                        z[:, Z_VS + i // 2, (4 * (i % 2) + t) * P:(4 * (i % 2) + t + 1) * P],
                                        k.cst["ident"][:, :])
                last.then_inc(turned, 1)

        @block.vector
        def _(dve):
            for i in range(4):
                dve.wait_ge(turned, i + 1)
                dve.tensor_copy(vals[:, i // 2, 4 * (i % 2):4 * (i % 2) + 4, :],
                                k.ps[:, i % 2, :].rearrange("p (t n) -> p t n", t=4)).then_inc(copied, 1)


def compress(k, z, spare, comp_k, comp_v):
    nc, c = k.nc, k.cst
    QP = PAGES * 2 * G
    with ExitStack() as ctx:
        load_constants(k, ctx, COMPRESSION)
        w1 = k.sb(ctx, "cmp_w1", [P, 2, L2, P])
        row_len = 2 * L2 * G * 2
        rows = [spare[:, :, :].rearrange("p a n -> p (a n)")[:, 0:PAGES * row_len].rearrange("p (a n) -> p a n", a=PAGES),
                k.sb(ctx, "cmp_rows", [P, PAGES, row_len])[:, :, :]]
        own = rows[0][:, 0:8, :].rearrange("p a n -> p (a n)")
        bias = k.sb(ctx, "cmp_bias", [P, 2])
        hid = k.sb(ctx, "cmp_hidden", [P, 2, QP])
        kc = k.sb(ctx, "cmp_keys", [P, NCS])
        sq = k.sb(ctx, "cmp_squares", [P, NCS])
        rms = k.sb(ctx, "cmp_rms", [P, NCS])
        w_loaded = k.sem(ctx, "cmp_weights_loaded")
        rows_loaded = [k.sem(ctx, f"cmp_rows_loaded{s}") for s in range(2)]
        pos_summed = k.sem(ctx, "cmp_pos_summed")
        bias_ready = k.sem(ctx, "cmp_bias_ready")
        hidden = k.sem(ctx, "cmp_hidden_summed")
        active = k.sem(ctx, "cmp_activated")
        mapped = k.sem(ctx, "cmp_mapped")
        squared = k.sem(ctx, "cmp_squared")
        summed = k.sem(ctx, "cmp_squares_summed")
        rooted = k.sem(ctx, "cmp_rooted")
        own_moved = k.sem(ctx, "cmp_own_moved")
        own_written = k.sem(ctx, "cmp_own_written")
        block = ctx.enter_context(nc.Block())

        def row_view(s, kv, l2, n):
            v = rows[s][:, 0:n // (2 * G), :].rearrange("p a (k l c) -> p k l a c", k=2, l=L2)
            return v[:, kv, l2, :, :]

        @block.sync
        def _(sp):
            sp.dma_start(w1[:], k.ins["cmp_w1"]).then_inc(w_loaded, 16)

            def load(b, j, s):
                wait_apart(k, sp, hidden, b + 1)
                load_pages(k, sp, b, k.ins["cmp_pages"], rows[s], rows_loaded[s])
            pairs(sp, B, load)

        def second(pe, kv, b, cols):
            v = hid[:, kv, 0:cols].rearrange("p (g n) -> p g n", g=G)
            for g in range(G):
                if kv == 0:
                    last = pe.matmul(k.ps[g * HD:(g + 1) * HD, 2, 0:cols // G], c["cmp_w2"][:, 0, :], v[:, g, :],
                                     start=True, stop=True)
                else:
                    last = pe.matmul(k.ps[0:cols // G, 4, g * HD:(g + 1) * HD], v[:, g, :], c["cmp_w2"][:, 1, :],
                                     start=True, stop=True)
            return last

        def one(pe, b, s, cols, view):
            for kv in range(2):
                for l2 in range(L2):
                    last = pe.matmul(k.ps[:, kv, 0:cols], w1[:, kv, l2, :], view(kv, l2), start=l2 == 0, stop=l2 == L2 - 1)
            last.then_inc(hidden, 1)
            pe.wait_ge(active, b + 1)
            second(pe, 0, b, cols)
            second(pe, 1, b, cols).then_inc(mapped, 1)
            pe.wait_ge(squared, b + 1)
            pe.matmul(k.ps[:, 3, 0:cols // G], c["halves"][:, :], sq[:, 0:cols // G], start=True, stop=True).then_inc(summed, 1)

        @block.tensor
        def _(pe):
            pe.sem_inc(hidden, 2)
            pe.wait_ge(w_loaded, 16)
            for kv in range(2):
                for l2 in range(L2):
                    last = pe.matmul(k.ps[:, 5 + kv, 0:1], w1[:, kv, l2, :], c["cmp_pos"][:, kv, l2:l2 + 1],
                                     start=l2 == 0, stop=l2 == L2 - 1)
            last.then_inc(pos_summed, 1)

            def sample(b, j, s):
                pe.wait_ge(rows_loaded[s], (j + 1) * (16 * PAGES))
                one(pe, b, s, QP, lambda kv, l2: row_view(s, kv, l2, QP))
            pairs(pe, B, sample)
            for kv in range(2):
                for g in range(G):
                    if kv or g:
                        pe.wait_ge(own_written, 2 * kv + g)
                    for lp in range(2):
                        src = z[:, Z_KC + kv, 0:SEQ].rearrange("p (n l) -> p l n", l=2)[:, lp, :]
                        last = pe.matmul(k.ps[:, 7, :], c["shift"][:, g, lp, :], src, start=lp == 0, stop=lp == 1)
                    last.then_inc(own_moved, 1)
            pe.wait_ge(own_written, 4)
            ov = own.rearrange("p (k l n) -> p k l n", k=2, l=L2)
            one(pe, B, 0, NCP * G, lambda kv, l2: ov[:, kv, l2, :])

        def finish(dve, b, cols):
            n = cols // G
            dve.wait_ge(mapped, b + 1)
            dve.tensor_scalar(kc[:, 0:n], k.ps[:, 2, 0:n], c["cmp_b2k"][:, 0:1], None, ALU.add)
            dve.tensor_tensor(comp_v[0:n, b, :], k.ps[0:n, 4, 0:P], c["cmp_b2v"][0:n, :], ALU.add)
            dve.drain()
            dve.tensor_tensor(sq[:, 0:n], kc[:, 0:n], kc[:, 0:n], ALU.mult).then_inc(squared, 1)
            dve.wait_ge(rooted, b + 1)
            dve.reciprocal(rms[:, 0:n], rms[:, 0:n])
            dve.drain()
            dve.scalar_tensor_tensor(out=comp_k[:, b, 0:n], in0=kc[:, 0:n], scalar=c["gains"][:, Z_KS:Z_KS + 1],
                                     in1=rms[:, 0:n], op0=ALU.mult, op1=ALU.mult)
            dve.drain()

        @block.vector
        def _(dve):
            dve.wait_ge(pos_summed, 1)
            dve.tensor_tensor(bias[:, 0:2], k.ps[:, 5:7, 0:1].rearrange("p a b -> p (a b)"), c["cmp_b1"][:, :], ALU.add).then_inc(bias_ready, 1)

            def sample(b, j, s):
                finish(dve, b, QP)
            pairs(dve, B, sample)
            ov = own.rearrange("p (k l a g c) -> p k l a g c", k=2, l=L2, g=G, c=2)
            for kv in range(2):
                for g in range(G):
                    dve.wait_ge(own_moved, 2 * kv + g + 1)
                    dve.tensor_copy(ov[:, kv, :, :, g, :], k.ps[:, 7, :].rearrange("p (a c l) -> p l a c", l=L2, c=2)).then_inc(own_written, 1)
            finish(dve, B, NCP * G)

        @block.scalar
        def _(act):
            act.wait_ge(bias_ready, 1)

            def gelu(b, cols):
                act.wait_ge(hidden, b + 3)
                for kv in range(2):
                    last = act.activation(hid[:, kv, 0:cols].rearrange("p (g a c) -> p a g c", g=G, c=2),
                                          k.ps[:, kv, 0:cols].rearrange("p (a g c) -> p a g c", g=G, c=2), ACT.Gelu_apprx_tanh, bias=bias[:, kv:kv + 1])
                last.then_inc(active, 1)
                act.wait_ge(summed, b + 1)
                act.activation(rms[:, 0:cols // G], k.ps[:, 3, 0:cols // G], ACT.Sqrt,
                               bias=c["norm_bias"][:, Z_KS:Z_KS + 1], scale=c["norm_scale"][:, Z_KS:Z_KS + 1]).then_inc(rooted, 1)
            pairs(act, B, lambda b, j, s: gelu(b, QP))
            gelu(B, NCP * G)


def prompt_attention(k, z, zs, vals, comp_k, comp_v, mix):
    nc, c = k.nc, k.cst
    UN = QT * G
    WK = WINDOW + P
    with ExitStack() as ctx:
        q = k.sb(ctx, "pair_queries", [P, SEQ])
        far = k.sb(ctx, "pair_bias", [P, G, SEQ])
        win = k.sb(ctx, "pair_window_bias", [P, G, WK])
        cbias = k.sb(ctx, "pair_block_bias", [P, G, 32])
        gates = k.sb(ctx, "gates", [P, QT, 3, H])
        gate_x = z[:, Z_GATE, :]
        pair_gates = k.sb(ctx, "pair_gates", [P, QT, 3, G])
        ls = k.sb(ctx, "logits_selected", [P, 2, SEQ])
        lw = k.sb(ctx, "logits_window", [P, 2, WK])
        lc = k.sb(ctx, "logits_blocks", [P, 2, NCP])
        mx = k.sb(ctx, "maxima", [P, 2, 4])
        nmx = k.sb(ctx, "negated_maxima", [P, 2, 4])
        sums = k.sb(ctx, "sums", [P, 2, 4])
        coef = k.sb(ctx, "coefficients", [P, 2, 4])
        pt = k.sb(ctx, "probs_turned", [P, 4, 512])
        o = k.sb(ctx, "pair_out", [P, 2, P])
        gates_turned = k.sem(ctx, "gates_turned")
        gates_on = k.sem(ctx, "gates_sigmoid")
        gates_read = k.sem(ctx, "gates_read")
        pair_ready = k.sem(ctx, "pair_ready")
        scored = k.sem(ctx, "scored")
        biased = k.sem(ctx, "biased")
        exped = k.sem(ctx, "exped")
        turned = k.sem(ctx, "turned")
        copied = [k.sem(ctx, f"turned_copied{x}") for x in range(2)]
        probs_c = k.sem(ctx, "probs_unmasked")
        valued = k.sem(ctx, "valued")
        combined = k.sem(ctx, "combined")
        mixed = k.sem(ctx, "mixed_turned")
        mix_read = k.sem(ctx, "mixed_read")
        block = ctx.enter_context(nc.Block())

        def turns(t):
            lo = max(0, t - 4)
            sel = [("s", i * P, P, i) for i in range(t + 1)]
            w = [("w", (i - t + 4) * P, P, i) for i in range(lo, t + 1)]
            blocks = [("c", 0, NCP, 0)]
            allt = sel + w + blocks
            return [allt[i:i + 4] for i in range(0, len(allt), 4)]

        units = [(t, g) for t in range(QT) for g in range(G)]
        banks_before = [0]
        for t, g in units:
            banks_before.append(banks_before[-1] + len(turns(t)))
        BANKS = banks_before[-1]
        assert BANKS % 4 == 0

        S_SEL = k.ps[:, 0:2, :].rearrange("p b n -> p (b n)")
        S_WIN = k.ps[:, 2:4, :].rearrange("p b n -> p (b n)")
        S_CMP = k.ps[:, 3, 256:256 + NCP]
        OUT = k.ps[:, 6, :]
        MIXT = k.ps[:, 7, 0:P]

        def score(pe, i, u):
            t, g = units[u]
            rows = slice(g * HD, (g + 1) * HD)
            pe.wait_ge(biased, i * UN + u + 1)
            lhs = q[rows, t * P:(t + 1) * P]
            for a in range(0, (t + 1) * P, 512):
                w = min(512, (t + 1) * P - a)
                pe.matmul(S_SEL[:, a:a + w], lhs, z[rows, Z_KS, a:a + w], start=True, stop=True)
            lo = max(0, t - 4)
            off = (lo - t + 4) * P
            for a, b_ in ((off, 512), (512, WK)):
                if a < b_:
                    pe.matmul(S_WIN[:, a:b_], lhs, z[rows, Z_KW, (t - 4) * P + a:(t - 4) * P + b_], start=True, stop=True)
            pe.matmul(S_CMP, lhs, comp_k[rows, B, 0:NCP], start=True, stop=True).then_inc(scored, 1)

        @block.tensor
        def _(pe):
            for t in range(QT):
                last = pe.transpose(k.ps[:, t // 4, (t % 4) * P:(t % 4 + 1) * P], gate_x[:, t * P:(t + 1) * P], c["ident"][:, :]) if t else None
                if t == 0:
                    pe.wait_ge(gates_on, 1)
                    last = pe.transpose(k.ps[:, 0, 0:P], gate_x[:, 0:P], c["ident"][:, :])
            last.then_inc(gates_turned, 1)
            pe.wait_ge(gates_read, 1)
            with pe.Fori(0, R) as i:
                pe.wait_ge(pair_ready, i + 1)
                score(pe, i, 0)
                for u, (t, g) in enumerate(units):
                    if u + 1 < UN:
                        score(pe, i, u + 1)
                    pe.wait_ge(exped, i * UN + u + 1)
                    groups = turns(t)
                    for n in range(len(groups) + 1):
                        if n < len(groups):
                            at = banks_before[u] + n
                            pe.wait_ge(copied[at % 2], i * (BANKS // 2) + (at // 2 + 1))
                            bank = 4 + (banks_before[u] + n) % 2
                            for s, (what, col, w, tile) in enumerate(groups[n]):
                                src = {"s": ls, "w": lw, "c": lc}[what]
                                last = pe.transpose(k.ps[0:w, bank, s * P:(s + 1) * P], src[:, u % 2, col:col + w], c["ident"][:, :])
                            last.then_inc(turned, 1)
                        if n >= 1:
                            at = banks_before[u] + n - 1
                            pe.wait_ge(copied[at % 2], i * (BANKS // 2) + (at // 2 + 2))
                            if n == 1:
                                pe.wait_ge(combined, i * UN + u + 1)
                            lo = max(0, t - 4)
                            slot = (banks_before[u] + n - 1) % 4
                            for s, (what, col, w, tile) in enumerate(groups[n - 1]):
                                moving = {"s": vals[:, 0, tile, g * HD:(g + 1) * HD],
                                          "w": vals[:, 1, tile, g * HD:(g + 1) * HD],
                                          "c": comp_v[0:NCP, B, g * HD:(g + 1) * HD]}[what]
                                first = {"s": 0, "w": lo, "c": 0}[what]
                                end = {"s": t, "w": t, "c": 0}[what]
                                at_o = {"s": 0, "w": 1, "c": 2}[what] * HD
                                last = pe.matmul(OUT[:, at_o:at_o + HD], pt[0:w, slot, s * P:(s + 1) * P], moving,
                                                 start=tile == first, stop=tile == end)
                    last.then_inc(valued, 1)
                    if g == 1:
                        pe.wait_ge(combined, i * UN + u + 2)
                        pe.wait_ge(mix_read, i * QT + t + 1)
                        pe.transpose(MIXT, o[:, t % 2, :], c["ident"][:, :]).then_inc(mixed, 1)

        def copy_turned(eng, i, u, n):
            t, g = units[u]
            group = turns(t)[n]
            at = i * BANKS + (banks_before[u] + n)
            eng.wait_ge(turned, at + 1)
            bank, slot = 4 + (banks_before[u] + n) % 2, (banks_before[u] + n) % 4
            full = [x for x in group if x[0] != "c"]
            ops = []
            if full:
                w = len(full) * P
                ops.append((pt[:, slot, 0:w], k.ps[:, bank, 0:w]))
            if len(full) < len(group):
                a = len(full) * P
                ops.append((pt[0:NCP, slot, a:a + P], k.ps[0:NCP, bank, a:a + P]))
            for x, (dst, src) in enumerate(ops):
                if eng is k.nc.scalar:
                    last = eng.activation(dst, src, ACT.Copy)
                else:
                    last = eng.tensor_copy(dst, src)
            last.then_inc(copied[(banks_before[u] + n) % 2], 1)

        def copies_act(u, n):
            return (banks_before[u] + n) % 2 == 1

        @block.vector
        def _(dve):
            dve.sem_inc(biased, 1)
            dve.sem_inc(combined, 1)
            dve.sem_inc(copied[0], 1)
            dve.wait_ge(gates_turned, 1)
            for j in range(3):
                last = dve.tensor_copy(gates[:, :, j, :], k.ps[:, 0:2, :].rearrange("p b (t n) -> p (b t) n", t=4)[:, :, 32 * j:32 * j + H])
            last.then_inc(gates_read, 1)
            dve.drain()

            def bias(u):
                t, g = units[u]
                s = u % 2
                w = (t + 1) * P
                off = (max(0, t - 4) - t + 4) * P
                dve.tensor_tensor_reduce(ls[:, s, 0:w], S_SEL[:, 0:w], far[:, g, SEQ - w:SEQ], 1.0, LOWEST, ALU.add, ALU.max, mx[:, s, 0:1])
                dve.tensor_tensor_reduce(lw[:, s, off:WK], S_WIN[:, off:WK], win[:, g, off:WK], 1.0, LOWEST, ALU.add, ALU.max, mx[:, s, 1:2])
                dve.tensor_tensor_reduce(lc[:, s, :], S_CMP, cbias[:, g, 16 - 2 * t:32 - 2 * t], 1.0, LOWEST, ALU.add, ALU.max, mx[:, s, 2:3])
                dve.drain()
                dve.tensor_scalar(nmx[:, s, 0:3], mx[:, s, 0:3], -1.0, None, ALU.mult).then_inc(biased, 1)

            with dve.Fori(0, R) as i:
                dve.tensor_copy(q[:], z[:, i, 0:SEQ])
                for g in range(G):
                    h = i + g * R
                    b31 = k.near_bias[:, h, 0:1]
                    table = k.near_bias[:, h, :]
                    dve.tensor_copy(far[:, g, 0:SEQ - 256], b31.broadcast_to([P, SEQ - 256]))
                    dve.tensor_copy(far[:, g, SEQ - 256:SEQ], table)
                    dve.tensor_copy(win[:, g, P:WK - 256], b31.broadcast_to([P, WK - 256 - P]))
                    dve.tensor_copy(win[:, g, WK - 256:WK], table)
                    dve.tensor_scalar(win[:, g, 0:P], c["edge_mask"][:, :], b31, None, ALU.add)
                    dve.tensor_copy(cbias[:, g, :], k.block_bias[:, h, :])
                    dve.tensor_copy(pair_gates[:, :, :, g], gates[:, :, :, h])
                dve.drain().then_inc(pair_ready, 1)
                wait_apart(k, dve, scored, i * UN + 1)
                bias(0)
                for u, (t, g) in enumerate(units):
                    s = u % 2
                    if u + 1 < UN:
                        wait_apart(k, dve, scored, i * UN + u + 2)
                        if u >= 1:
                            wait_apart(k, dve, valued, i * UN + u)
                        bias(u + 1)
                    dve.wait_ge(exped, i * UN + u + 1)
                    dve.reciprocal(coef[:, s, 0:3], sums[:, s, 0:3])
                    dve.drain()
                    for col, j in ((0, 1), (1, 2), (2, 0)):
                        dve.tensor_tensor(coef[:, s, col:col + 1], coef[:, s, col:col + 1], pair_gates[:, t, j, g:g + 1], ALU.mult)
                    dve.drain()
                    for n in range(len(turns(t))):
                        if not copies_act(u, n):
                            copy_turned(dve, i, u, n)
                    dve.wait_ge(valued, i * UN + u + 1)
                    ov = o[:, t % 2, g * HD:(g + 1) * HD]
                    dve.tensor_scalar(ov, OUT[:, 0:HD], coef[:, s, 0:1], None, ALU.mult)
                    dve.drain()
                    dve.scalar_tensor_tensor(out=ov, in0=OUT[:, HD:2 * HD], scalar=coef[:, s, 1:2], in1=ov, op0=ALU.mult, op1=ALU.add)
                    dve.drain()
                    dve.scalar_tensor_tensor(out=ov, in0=OUT[:, 2 * HD:3 * HD], scalar=coef[:, s, 2:3], in1=ov, op0=ALU.mult, op1=ALU.add).then_inc(combined, 1)

        @block.scalar
        def _(act):
            act.activation(gate_x, gate_x, ACT.Sigmoid).then_inc(gates_on, 1)
            act.sem_inc(copied[1], 1)
            act.sem_inc(mix_read, 1)
            with act.Fori(0, R) as i:
                for u, (t, g) in enumerate(units):
                    s = u % 2
                    w = (t + 1) * P
                    off = (max(0, t - 4) - t + 4) * P
                    act.wait_ge(biased, i * UN + u + 2)
                    if u >= 2:
                        act.wait_ge(combined, i * UN + u)
                    act.activation(ls[:, s, 0:w], ls[:, s, 0:w], ACT.Exp, bias=nmx[:, s, 0:1], accum_out=sums[:, s, 0:1])
                    act.activation(lw[:, s, off:WK], lw[:, s, off:WK], ACT.Exp, bias=nmx[:, s, 1:2], accum_out=sums[:, s, 1:2])
                    act.activation(lc[:, s, :], lc[:, s, :], ACT.Exp, bias=nmx[:, s, 2:3], accum_out=sums[:, s, 2:3])
                    act.drain().then_inc(probs_c, 1)
                    for n in range(len(turns(t))):
                        if copies_act(u, n):
                            copy_turned(act, i, u, n)
                    if g == 1:
                        act.wait_ge(mixed, i * QT + t + 1)
                        act.activation(mix[:, i, t * P:(t + 1) * P], MIXT, ACT.Copy).then_inc(mix_read, 1)

        @block.gpsimd
        def _(pool):
            pool.wait_ge(gates_on, 1)
            pool.tensor_copy(zs[:, :, :], z[:, :, SEQ:T])
            with pool.Fori(0, R) as i:
                for u, (t, g) in enumerate(units):
                    pool.wait_ge(probs_c, i * UN + u + 1)
                    pool.tensor_tensor(lc[:, u % 2, :], lc[:, u % 2, :], c["block_mask"][:, 16 - 2 * t:32 - 2 * t], ALU.mult).then_inc(exped, 1)


def sample_attention(k, zs, comp_k, comp_v, mix):
    nc, c = k.nc, k.cst
    WIN = WINDOW + L
    KEYS = PAST + L
    KCH = PAGES + 1
    groups = [list(range(a, min(a + 4, KCH))) for a in range(0, KCH, 4)]
    with ExitStack() as ctx:
        kv = k.sb(ctx, "past_rows", [P, 2, PAGES, 2 * P])
        wk = k.sb(ctx, "window_keys", [P, 2, WINDOW])
        wv = k.sb(ctx, "window_values", [P, 2, 4, P])
        qd = k.sb(ctx, "block_diagonal_queries", [P, ROWS])
        new = k.sb(ctx, "new_rows", [P, 4, L])
        newv = k.sb(ctx, "new_values", [L, 2, P])
        ls = k.sb(ctx, "row_logits", [ROWS, KEYS])
        lw = k.sb(ctx, "row_window_logits", [ROWS, WIN])
        lc = k.sb(ctx, "row_block_logits", [ROWS, NCS])
        mx = k.sb(ctx, "row_maxima", [ROWS, 16])
        mm = k.sb(ctx, "row_max", [ROWS, 4])
        nm = k.sb(ctx, "row_neg_max", [ROWS, 4])
        sums = k.sb(ctx, "row_sums", [ROWS, 4])
        rs = k.sb(ctx, "row_rsums", [ROWS, 4])
        co = k.sb(ctx, "row_coef", [ROWS, 4])
        imp = k.sb(ctx, "importance", [G * L, 4, NBS])
        top = k.sb(ctx, "top8", [G * L, 2, 8])
        neg = k.sb(ctx, "unselected", [G * L, NBS])
        negr = k.sb(ctx, "row_unselected", [ROWS, NBS])
        pt = k.sb(ctx, "row_probs_turned", [P, 4, 4, ROWS])
        gd = k.sb(ctx, "gate_diagonals", [P, H, L])
        os_ = k.sb(ctx, "row_out", [ROWS, P])
        s_kv = [k.sem(ctx, f"past_loaded{s}") for s in range(2)]
        s_new = k.sem(ctx, "new_rows_copied")
        s_newt = k.sem(ctx, "new_values_turned")
        s_newv = k.sem(ctx, "new_values_copied")
        s_cs = k.sem(ctx, "block_scores")
        s_cb = k.sem(ctx, "block_logits")
        s_ce = k.sem(ctx, "block_probs")
        s_cn = k.sem(ctx, "block_probs_normed")
        s_imp = k.sem(ctx, "importance_summed")
        s_sel = k.sem(ctx, "blocks_selected")
        s_neg = k.sem(ctx, "mask_spread")
        s_negc = k.sem(ctx, "mask_copied")
        s_ks = k.sem(ctx, "key_scores")
        s_kb = k.sem(ctx, "key_logits")
        s_wb = k.sem(ctx, "window_logits")
        s_we = k.sem(ctx, "window_probs")
        s_lm = k.sem(ctx, "logit_max")
        s_e = k.sem(ctx, "key_probs")
        s_t = k.sem(ctx, "turned")
        s_tc = [k.sem(ctx, f"turned_copied{x}") for x in range(2)]
        s_o = k.sem(ctx, "outputs_summed")
        s_os = k.sem(ctx, "outputs_combined")
        s_ot = k.sem(ctx, "outputs_turned")
        s_mix = k.sem(ctx, "outputs_placed")
        block = ctx.enter_context(nc.Block())

        turn_list = [[("w", a * P, P, KCH + 1 + a) for a in range(4)],
                     [("w", 4 * P, L, KCH + 5), ("c", 0, NCS, KCH)]]
        turn_list += [[("s", a * P, P if a < PAGES else L, a) for a in g] for g in groups]
        if len(turn_list) % 2:
            turn_list[2:4] = [turn_list[2][:2], turn_list[2][2:], turn_list[3]]
        NTURN = len(turn_list)
        assert NTURN % 2 == 0
        OC, OS, OW = (k.ps[0:ROWS, 7, x * P:(x + 1) * P] for x in range(3))
        NKS = 9

        def tokens(b):
            return bass.ds(b * L + SEQ, L)

        @block.sync
        def _(sp):
            def load(b, j, s):
                wait_apart(k, sp, s_o, b + 1)
                sp.dma_start(wk[:, s, :], k.ins["win_k"][b]).then_inc(s_kv[s], 16)
                sp.dma_start(wv[:, s, :, :], k.ins["win_v"][b].rearrange("(a p) n -> p a n", p=P)).then_inc(s_kv[s], 16)
                load_pages(k, sp, b, k.ins["kv_pages"], kv[:, s, :, :], s_kv[s])
            pairs(sp, B, load)

        @block.tensor
        def _(pe):
            ident = c["ident"]
            pe.sem_inc(s_o, 2)

            def sample(b, j, slot):
                pe.wait_ge(s_new, b + 1)
                pe.transpose(k.ps[0:L, 2, 0:P], new[:, 2, :], ident[:, :])
                pe.transpose(k.ps[0:L, 2, P:2 * P], new[:, 3, :], ident[:, :]).then_inc(s_newt, 1)
                pe.matmul(k.ps[0:ROWS, 3, 0:NCS], qd[:, :], comp_k[:, b, :], start=True, stop=True)
                pe.matmul(k.ps[0:ROWS, 3, 256:260], gd[:, :, :].rearrange("p h q -> p (h q)"), c["branch"][:, :], start=True, stop=True)
                pe.wait_ge(s_kv[slot], (j + 1) * (16 * (PAGES + 2)))
                pe.matmul(k.ps[0:ROWS, 6, 0:WINDOW], qd[:, :], wk[:, slot, :], start=True, stop=True)
                pe.matmul(k.ps[0:ROWS, 3, 128:128 + L], qd[:, :], new[:, 1, :], start=True, stop=True).then_inc(s_cs, 1)
                pe.wait_ge(s_cn, b + 1)
                pe.matmul(k.ps[0:G * L, 2, 256:256 + NCS], c["sum_heads"][:, :], lc[:, :], start=True, stop=True).then_inc(s_imp, 1)
                pe.wait_ge(s_sel, b + 1)
                pe.matmul(k.ps[0:ROWS, 2, 384:384 + NBS], c["spread_heads"][:, :], neg[:, :], start=True, stop=True).then_inc(s_neg, 1)
                for n in range(NKS):
                    pe.wait_ge(s_kb, b * NKS + (n + 1))
                    if n < NKS - 1:
                        last = pe.matmul(k.ps[0:ROWS, n % 2, :], qd[:, :], kv[:, slot, 4 * n:4 * n + 4, 0:P], start=True, stop=True)
                    else:
                        last = pe.matmul(k.ps[0:ROWS, n % 2, 0:L], qd[:, :], new[:, 0, :], start=True, stop=True)
                    last.then_inc(s_ks, 1)
                pe.wait_ge(s_os, b)
                for n in range(NTURN + 1):
                    if n < NTURN:
                        if n == 0:
                            pe.wait_ge(s_we, b + 1)
                        if n == 2:
                            pe.wait_ge(s_e, b + 1)
                        pe.wait_ge(s_tc[n % 2], b * (NTURN // 2) + (n // 2 + 1))
                        for s, (what, col, w, tile) in enumerate(turn_list[n]):
                            src = {"s": ls, "w": lw, "c": lc}[what]
                            last = pe.transpose(k.ps[0:w, 4 + n % 2, s * ROWS:(s + 1) * ROWS], src[:, col:col + w], ident[0:ROWS, 0:ROWS])
                        last.then_inc(s_t, 1)
                    if n >= 1:
                        pe.wait_ge(s_tc[(n - 1) % 2], b * (NTURN // 2) + ((n - 1) // 2 + 2))
                        if n == 1:
                            pe.wait_ge(s_newv, b + 1)
                        for s, (what, col, w, tile) in enumerate(turn_list[n - 1]):
                            if what == "c":
                                o, mv, st, sp_ = OC, comp_v[:, b, :], True, True
                            elif what == "w":
                                a = tile - KCH - 1
                                o, st, sp_ = OW, a == 0, a == 4
                                mv = wv[:, slot, a, :] if a < 4 else newv[:, 1, :]
                            else:
                                o, st, sp_ = OS, tile == 0, tile == PAGES
                                mv = kv[:, slot, tile, P:2 * P] if tile < PAGES else newv[:, 0, :]
                            last = pe.matmul(o, pt[0:w, (n - 1) % 4, s, :], mv, start=st, stop=sp_)
                last.then_inc(s_o, 1)
                pe.wait_ge(s_os, b + 1)
                pe.wait_ge(s_mix, b)
                pe.transpose(k.ps[:, 3, 384:384 + ROWS], os_[:, :], ident[0:ROWS, 0:ROWS]).then_inc(s_ot, 1)
            pairs(pe, B, sample)

        def copies(eng, b, parity):
            for n in range(parity, NTURN, 2):
                eng.wait_ge(s_t, b * NTURN + (n + 1))
                group = turn_list[n]
                runs = []
                for s, (what, col, w, tile) in enumerate(group):
                    if runs and runs[-1][2] == w and runs[-1][1] + runs[-1][3] == tile:
                        runs[-1][3] += 1
                    else:
                        runs.append([s, tile, w, 1])
                for s, tile, w, count in runs:
                    dst = pt[0:w, n % 4, s:s + count, :]
                    src = k.ps[0:w, 4 + n % 2, s * ROWS:(s + count) * ROWS].rearrange("p (a n) -> p a n", a=count)
                    if eng is k.nc.scalar:
                        last = eng.activation(dst, src, ACT.Copy)
                    else:
                        last = eng.tensor_copy(dst, src)
                last.then_inc(s_tc[n % 2], 1)

        @block.scalar
        def _(act):
            act.sem_inc(s_tc[1], 1)
            with act.Fori(0, B) as b:
                act.wait_ge(s_cb, b + 1)
                act.activation(lc[:, :], lc[:, :], ACT.Exp, bias=nm[:, 0:1], accum_out=sums[:, 0:1]).then_inc(s_ce, 1)
                act.wait_ge(s_wb, b + 1)
                act.activation(lw[:, :], lw[:, :], ACT.Exp, bias=nm[:, 2:3], accum_out=sums[:, 2:3]).then_inc(s_we, 1)
                act.wait_ge(s_lm, b + 1)
                act.activation(ls[:, :], ls[:, :], ACT.Exp, bias=nm[:, 1:2], accum_out=sums[:, 1:2]).then_inc(s_e, 1)
                copies(act, b, 1)

        @block.vector
        def _(dve):
            dve.sem_inc(s_tc[0], 1)
            dve.sem_inc(s_kb, 2)
            dve.memset(qd[:], 0.0)
            dve.memset(imp[:], FORCED)
            dve.drain()
            with dve.Fori(0, B) as b:
                for g in range(G):
                    rows = slice(g * HD, (g + 1) * HD)
                    dve.tensor_copy(qd[rows, g * GR:(g + 1) * GR].rearrange("p (r q) -> p r q", r=R), zs[rows, 0:R, bass.ds(b * L, L)])
                for n, ch in enumerate((Z_KS, Z_KW, Z_VS, Z_VW)):
                    dve.tensor_copy(new[:, n, :], zs[:, ch, bass.ds(b * L, L)])
                dve.tensor_tensor(gd[:, :, :], c["diag"][:, :].rearrange("p (h o) -> p h o", o=1).broadcast_to([P, H, L]),
                                  zs[:, bass.ds(Z_GATE, 1), bass.ds(b * L, L)].broadcast_to([P, H, L]), ALU.mult)
                dve.drain().then_inc(s_new, 1)
                dve.wait_ge(s_newt, b + 1)
                dve.tensor_copy(newv[:, :, :], k.ps[0:L, 2, 0:2 * P].rearrange("p (a n) -> p a n", a=2)).then_inc(s_newv, 1)
                wait_apart(k, dve, s_cs, b + 1)
                dve.tensor_tensor_reduce(lc[:, :], k.ps[0:ROWS, 3, 0:NCS], k.row_blocks[:, :], 1.0, LOWEST, ALU.add, ALU.max, mm[:, 0:1])
                dve.drain()
                dve.tensor_scalar(nm[:, 0:1], mm[:, 0:1], -1.0, None, ALU.mult).then_inc(s_cb, 1)
                dve.tensor_tensor_reduce(lw[:, 0:WINDOW], k.ps[0:ROWS, 6, 0:WINDOW], k.row_window[:, 0:WINDOW], 1.0, LOWEST, ALU.add, ALU.max, mx[:, 12:13])
                dve.tensor_tensor_reduce(lw[:, WINDOW:WIN], k.ps[0:ROWS, 3, 128:128 + L], k.row_window[:, WINDOW:WIN], 1.0, LOWEST, ALU.add, ALU.max, mx[:, 13:14])
                dve.tensor_copy(co[:, 0:3], k.ps[0:ROWS, 3, 256:259])
                dve.drain()
                dve.tensor_tensor(mm[:, 2:3], mx[:, 12:13], mx[:, 13:14], ALU.max)
                dve.drain()
                dve.tensor_scalar(nm[:, 2:3], mm[:, 2:3], -1.0, None, ALU.mult).then_inc(s_wb, 1)
                dve.wait_ge(s_ce, b + 1)
                dve.reciprocal(rs[:, 0:1], sums[:, 0:1])
                dve.drain()
                dve.tensor_scalar(lc[:, :], lc[:, :], rs[:, 0:1], None, ALU.mult).then_inc(s_cn, 1)
                dve.wait_ge(s_imp, b + 1)
                dve.tensor_copy(imp[:, 0, 1:NCS - 1], k.ps[0:G * L, 2, 257:256 + NCS - 1])
                dve.drain()
                for step in range(2):
                    dve.max(top[:, step, :], imp[:, step, :])
                    dve.drain()
                    dve.match_replace(imp[:, step + 1, :], top[:, step, :], imp[:, step, :], -5.0)
                    dve.drain()
                dve.tensor_scalar(neg[:, :], imp[:, 2, :], -1.0, NEG, ALU.is_ge, ALU.mult).then_inc(s_sel, 1)
                dve.wait_ge(s_neg, b + 1)
                dve.tensor_tensor(negr[:, :], k.ps[0:ROWS, 2, 384:384 + NBS], k.row_select[:, :], ALU.add)
                dve.drain()
                for n in range(NKS):
                    wait_apart(k, dve, s_ks, b * NKS + (n + 1))
                    if n < NKS - 2:
                        dve.tensor_tensor_reduce(ls[:, n * 512:(n + 1) * 512].rearrange("p (a n) -> p a n", n=CB),
                                                 k.ps[0:ROWS, n % 2, :].rearrange("p (a n) -> p a n", n=CB),
                                                 negr[:, 8 * n:8 * n + 8].rearrange("p (a o) -> p a o", o=1).broadcast_to([ROWS, 8, CB]),
                                                 1.0, LOWEST, ALU.add, ALU.max, mx[:, n:n + 1]).then_inc(s_kb, 1)
                    elif n == NKS - 2:
                        dve.tensor_tensor(ls[:, n * 512:(n + 1) * 512].rearrange("p (a n) -> p a n", n=CB),
                                          k.ps[0:ROWS, n % 2, :].rearrange("p (a n) -> p a n", n=CB),
                                          negr[:, 8 * n:8 * n + 8].rearrange("p (a o) -> p a o", o=1).broadcast_to([ROWS, 8, CB]),
                                          ALU.add).then_inc(s_kb, 1)
                    else:
                        dve.tensor_scalar(ls[:, PAST:KEYS], k.ps[0:ROWS, n % 2, 0:L], negr[:, NCS:NBS], None, ALU.add).then_inc(s_kb, 1)
                dve.drain()
                dve.tensor_tensor(ls[:, KEYS - TAIL:KEYS], ls[:, KEYS - TAIL:KEYS], k.row_tail[:, :], ALU.add)
                dve.drain()
                dve.tensor_reduce(mx[:, 7:8], ls[:, (NKS - 2) * 512:KEYS], X, ALU.max)
                dve.drain()
                dve.tensor_reduce(mm[:, 1:2], mx[:, 0:8], X, ALU.max)
                dve.drain()
                dve.tensor_scalar(nm[:, 1:2], mm[:, 1:2], -1.0, None, ALU.mult).then_inc(s_lm, 1)
                copies(dve, b, 0)
                dve.wait_ge(s_e, b + 1)
                dve.wait_ge(s_o, b + 3)
                dve.reciprocal(rs[:, 1:3], sums[:, 1:3])
                dve.drain()
                dve.tensor_tensor(co[:, 1:3], co[:, 1:3], rs[:, 1:3], ALU.mult)
                dve.drain()
                dve.tensor_scalar(os_[:, :], OC, co[:, 0:1], None, ALU.mult)
                dve.drain()
                dve.scalar_tensor_tensor(out=os_[:, :], in0=OS, scalar=co[:, 1:2], in1=os_[:, :], op0=ALU.mult, op1=ALU.add)
                dve.drain()
                dve.scalar_tensor_tensor(out=os_[:, :], in0=OW, scalar=co[:, 2:3], in1=os_[:, :], op0=ALU.mult, op1=ALU.add).then_inc(s_os, 1)
                dve.wait_ge(s_ot, b + 1)
                for g in range(G):
                    rows = slice(g * HD, (g + 1) * HD)
                    last = dve.tensor_copy(mix[rows, 0:R, tokens(b)],
                                           k.ps[rows, 3, 384 + g * GR:384 + (g + 1) * GR].rearrange("p (r q) -> p r q", r=R))
                last.then_inc(s_mix, 1)


def memory_attention(k, layer, xq, mix_out):
    nc, c = k.nc, k.cst
    NB4 = 4
    STEPS = QT + B // NB4
    with ExitStack() as ctx:
        keys = k.sb(ctx, "sample_mem_keys", [P, B, 2, NMEM])
        vals = k.sb(ctx, "sample_mem_values", [P, B, 2, 2 * P])
        qd = k.sb(ctx, "mem_queries_diagonal", [P, 2, B, XH, L])
        pr = k.sb(ctx, "mem_probs", [P, 2, XH * NMEM])
        mx = k.sb(ctx, "mem_maxima", [P, 2, XH])
        sums = k.sb(ctx, "mem_sums", [P, 2, XH])
        rs = k.sb(ctx, "mem_rsums", [P, 2, XH])
        pt = k.sb(ctx, "mem_probs_turned", [P, 2, 512])
        o = k.sb(ctx, "mem_out", [P, 2 * P])
        loaded = k.sem(ctx, "mem_rows_loaded")
        placed = k.sem(ctx, "mem_queries_placed")
        scored = k.sem(ctx, "mem_scored")
        maxed = k.sem(ctx, "mem_maxed")
        exped = k.sem(ctx, "mem_exped")
        turned = k.sem(ctx, "mem_turned")
        copied = k.sem(ctx, "mem_copied")
        valued = k.sem(ctx, "mem_valued")
        normed = k.sem(ctx, "mem_normed")
        back = k.sem(ctx, "mem_turned_back")
        stored = k.sem(ctx, "mem_mixed")
        block = ctx.enter_context(nc.Block())

        @block.sync
        def _(sp):
            sp.dma_start(keys[:], k.ins["cmem_k"][layer].rearrange("b p n -> p b n").rearrange("p b (c n) -> p b c n", c=2)).then_inc(loaded, 16)
            sp.dma_start(vals[:], k.ins["cmem_v"][layer].rearrange("b p n -> p b n").rearrange("p b (c n) -> p b c n", c=2)).then_inc(loaded, 16)

        def score_view(n):
            return k.ps[:, 2 * (n % 2):2 * (n % 2) + 2, :].rearrange("p b n -> p (b n)")

        def head_at(y):
            return 2 * (y % 2) + y // 2

        def n_turn(n):
            return 2 if n < QT else 1

        turn_before = [0]
        for n in range(STEPS):
            turn_before.append(turn_before[-1] + n_turn(n))

        @block.tensor
        def _(pe):
            pe.wait_ge(placed, 1)
            pe.wait_ge(loaded, 32)

            def score(n):
                if n >= 2:
                    pe.wait_ge(exped, n - 1)
                sv = score_view(n)
                if n < QT:
                    for y in range(XH):
                        h = head_at(y)
                        rows = slice((h % 2) * HD, (h % 2 + 1) * HD)
                        last = pe.matmul(sv[:, y * NMEM:(y + 1) * NMEM], xq[rows, h // 2, n * P:(n + 1) * P],
                                         k.mem_k[rows, layer, h // 2, :], start=True, stop=True)
                else:
                    for x in range(NB4):
                        b = (n - QT) * NB4 + x
                        for ch in range(2):
                            last = pe.matmul(sv[32 * x:32 * x + 32, 0:NMEM], qd[:, ch, b, :, :].rearrange("p h q -> p (h q)"),
                                             keys[:, b, ch, :], start=ch == 0, stop=ch == 1)
                last.then_inc(scored, 1)
            score(0)
            for n in range(STEPS):
                if n + 1 < STEPS:
                    score(n + 1)
                pe.wait_ge(exped, n + 1)
                for x in range(n_turn(n)):
                    at = turn_before[n] + x
                    if at >= 1:
                        pe.wait_ge(copied, at)
                    cols = 4 if n < QT else 2
                    for y in range(cols):
                        last = pe.transpose(k.ps[:, 4, y * P:(y + 1) * P], pr[:, n % 2, (4 * x + y) * P:(4 * x + y + 1) * P], c["ident"][:, :])
                    last.then_inc(turned, 1)
                    pe.wait_ge(copied, at + 1)
                    if x == 0 and n >= 1:
                        pe.wait_ge(normed, n)
                    if n < QT:
                        for hh in range(2):
                            h = head_at(2 * x + hh)
                            for mt in range(2):
                                last = pe.matmul(k.ps[:, 5, h * HD:(h + 1) * HD], pt[:, at % 2, (2 * hh + mt) * P:(2 * hh + mt + 1) * P],
                                                 k.mem_v[:, layer, mt, h * HD:(h + 1) * HD], start=mt == 0, stop=mt == 1)
                    else:
                        for xx in range(NB4):
                            b = (n - QT) * NB4 + xx
                            for mt in range(2):
                                last = pe.matmul(k.ps[32 * xx:32 * xx + 32, 5, 0:2 * P], pt[:, at % 2, mt * P + 32 * xx:mt * P + 32 * xx + 32],
                                                 vals[:, b, mt, :], start=mt == 0, stop=mt == 1)
                last.then_inc(valued, 1)
                pe.wait_ge(normed, n + 1)
                if n >= 1:
                    pe.wait_ge(stored, n)
                for ch in range(2):
                    last = pe.transpose(k.ps[:, 6, ch * P:(ch + 1) * P], o[:, ch * P:(ch + 1) * P], c["ident"][:, :])
                last.then_inc(back, 1)

        @block.vector
        def _(dve):
            dve.memset(qd[:], 0.0)
            dve.drain()
            for h in range(XH):
                rows = slice((h % 2) * HD, (h % 2 + 1) * HD)
                dve.tensor_copy(qd[rows, h // 2, :, h, :], samples(xq[rows, h // 2, :]))
            dve.drain().then_inc(placed, 1)

            def maximum(n):
                dve.wait_ge(scored, n + 1)
                heads = XH if n < QT else 1
                if n >= 2:
                    dve.wait_ge(exped, n - 1)
                dve.tensor_reduce(mx[:, n % 2, 0:heads], score_view(n)[:, 0:heads * NMEM].rearrange("p (h n) -> p h n", h=heads), X, ALU.max)
                dve.drain()
                dve.tensor_scalar(mx[:, n % 2, 0:heads], mx[:, n % 2, 0:heads], -1.0, None, ALU.mult).then_inc(maxed, 1)
            maximum(0)
            for n in range(STEPS):
                heads = XH if n < QT else 1
                if n + 1 < STEPS:
                    maximum(n + 1)
                dve.wait_ge(exped, n + 1)
                dve.reciprocal(rs[:, n % 2, 0:heads], sums[:, n % 2, 0:heads])
                for x in range(n_turn(n)):
                    at = turn_before[n] + x
                    w = 512 if n < QT else 256
                    dve.wait_ge(turned, at + 1)
                    dve.tensor_copy(pt[:, at % 2, 0:w], k.ps[:, 4, 0:w]).then_inc(copied, 1)
                dve.drain()
                dve.wait_ge(valued, n + 1)
                if n >= 1:
                    dve.wait_ge(back, n)
                if n < QT:
                    dve.tensor_tensor(o[:, :].rearrange("p (a b d) -> p a b d", a=2, b=2), k.ps[:, 5, 0:2 * P].rearrange("p (a b d) -> p a b d", a=2, b=2),
                                      rs[:, n % 2, :].rearrange("p (b a o) -> p a b o", a=2, o=1).broadcast_to([P, 2, 2, HD]), ALU.mult).then_inc(normed, 1)
                else:
                    dve.tensor_scalar(o[:, :], k.ps[:, 5, 0:2 * P], rs[:, n % 2, 0:1], None, ALU.mult).then_inc(normed, 1)

        @block.scalar
        def _(act):
            def place(n):
                act.wait_ge(back, n + 1)
                if n < QT:
                    last = act.activation(mix_out[:, :, n * P:(n + 1) * P], k.ps[:, 6, 0:2 * P].rearrange("p (c n) -> p c n", c=2), ACT.Copy)
                else:
                    for h in range(XH):
                        rows = slice((h % 2) * HD, (h % 2 + 1) * HD)
                        src = k.ps[rows, 6, (h // 2) * P:(h // 2 + 1) * P].rearrange("p (b h q) -> p b h q", b=NB4, h=XH)[:, :, h, :]
                        b0 = (n - QT) * NB4
                        last = act.activation(samples(mix_out[rows, h // 2, :])[:, b0:b0 + NB4, :], src, ACT.Copy)
                last.then_inc(stored, 1)

            for n in range(STEPS):
                heads = XH if n < QT else 1
                act.wait_ge(maxed, n + 1)
                if n >= 2:
                    act.wait_ge(normed, n - 1)
                for h in range(heads):
                    last = act.activation(pr[:, n % 2, h * NMEM:(h + 1) * NMEM], score_view(n)[:, h * NMEM:(h + 1) * NMEM],
                                          ACT.Exp, bias=mx[:, n % 2, h:h + 1], accum_out=sums[:, n % 2, h:h + 1])
                last.then_inc(exped, 1)
                if n >= 1:
                    place(n - 1)
            place(STEPS - 1)


def pool_mixer(k, z, mix):
    nc, c = k.nc, k.cst
    EP, ES = PST + SEQ, PST + L
    W = EP + B * ES
    with ExitStack() as ctx:
        load_constants(k, ctx, POOLING)
        ext = k.sb(ctx, "pool_ext", [PCH, 2, W])
        sa = k.sb(ctx, "pool_sums_a", [PCH, W])
        sb_ = k.sb(ctx, "pool_sums_b", [PCH, W])
        state = k.sb(ctx, "pool_state", [PCH, NPC, B * PST])
        pooled = k.sb(ctx, "pooled", [PCH, NPC, T])
        tails = k.sb(ctx, "pool_tails", [PCH, NPC, PST * (1 + B)])
        w = k.sb(ctx, "pool_weights", [PCH, NPC, PG])
        loaded = k.sem(ctx, "pool_loaded")
        done = k.sem(ctx, "pooled_ready")
        multiplied = k.sem(ctx, "pool_multiplied")
        scaled = k.sem(ctx, "pool_scaled")
        stored = k.sem(ctx, "pool_stored")
        block = ctx.enter_context(nc.Block())

        @block.sync
        def _(sp):
            sp.dma_start(state[:], k.ins["pool_state"]).then_inc(loaded, 16)
            sp.dma_start(w[:], k.ins["w_grp"]).then_inc(loaded, 16)
            sp.wait_ge(done, NPC)
            sp.dma_start(k.outs["pool"], tails[:]).then_inc(stored, 16)
            sp.wait_ge(stored, 16)

        def parts(buf, lo):
            s = buf[:, EP:W].rearrange("p (b n) -> p b n", b=B)
            return buf[:, lo:EP], s[:, :, lo:ES]

        @block.vector
        def _(dve):
            dve.wait_ge(loaded, 32)
            for ch in range(NPC):
                e = ext[:, ch % 2, :]
                pw = POOLW[ch // 2]
                ep, es = parts(e, 0)
                dve.memset(ep[:, 0:PST], 0.0)
                dve.tensor_copy(ep[:, PST:EP], z[0:PCH, ch, 0:SEQ])
                dve.tensor_copy(es[:, :, 0:PST], state[:, ch, :].rearrange("p (b n) -> p b n", b=B))
                dve.tensor_copy(es[:, :, PST:ES], samples(z[0:PCH, ch, :]))
                dve.drain()
                dve.tensor_copy(tails[:, ch, 0:PST], ep[:, SEQ:EP])
                dve.tensor_copy(tails[:, ch, PST:].rearrange("p (b n) -> p b n", b=B), es[:, :, L:ES])
                cur, span = e, 1
                while span < pw:
                    nxt = sa if cur is not sa else sb_
                    nxt_ap = nxt[:, :]
                    lo = 2 * span - 1
                    cp, cs = parts(cur if cur is e else cur[:, :], 0)
                    np_, ns = parts(nxt_ap, 0)
                    dve.tensor_tensor(np_[:, lo:EP], cp[:, lo:EP], cp[:, lo - span:EP - span], ALU.add)
                    dve.tensor_tensor(ns[:, :, lo:ES], cs[:, :, lo:ES], cs[:, :, lo - span:ES - span], ALU.add)
                    dve.drain()
                    cur, span = nxt, 2 * span
                cp, cs = parts(cur[:, :], 0)
                dve.tensor_tensor(cp[:, PST:PST + 16], cp[:, PST:PST + 16], c["pool_counts"][0:PCH, ch // 2, :], ALU.mult)
                dve.drain()
                dve.scalar_tensor_tensor(out=pooled[:, ch, 0:SEQ], in0=cp[:, PST:EP], scalar=1.0 / pw, in1=ep[:, PST:EP],
                                         op0=ALU.mult, op1=ALU.subtract)
                dve.scalar_tensor_tensor(out=samples(pooled[:, ch, :]), in0=cs[:, :, PST:ES], scalar=1.0 / pw, in1=es[:, :, PST:ES],
                                         op0=ALU.mult, op1=ALU.subtract)
                dve.drain().then_inc(done, 1)

        @block.tensor
        def _(pe):
            for m in range(NPC):
                g = m // 2
                pe.wait_ge(done, 2 * g + 2)
                if m >= 2:
                    pe.wait_ge(scaled, m - 1)
                for a, cols in NT:
                    for kk in range(2):
                        last = pe.matmul(bank_set(k, m % 2)[0:PCH, a:a + cols], w[:, 2 * g + kk, (m % 2) * PCH:(m % 2 + 1) * PCH],
                                         pooled[:, 2 * g + kk, a:a + cols], start=kk == 0, stop=kk == 1)
                last.then_inc(multiplied, 1)

        @block.scalar
        def _(act):
            for m in range(NPC):
                act.wait_ge(multiplied, m + 1)
                act.activation(mix[0:PCH, m, :], bank_set(k, m % 2)[0:PCH, :], ACT.Copy, scale=c["pool_scale"][0:PCH, m:m + 1]).then_inc(scaled, 1)


def conv_ffn(k, layer, xn, x):
    nc, c = k.nc, k.cst
    EP, ES = SEQ + 2, L + 2
    W = EP + B * ES
    with ExitStack() as octx:
        load_constants(k, octx, CONVOLUTION)
        gated = k.sb(octx, "gated", [P, FH, T])
        tails = k.sb(octx, "conv_tails", [P, 2 * FC, 2 * (1 + B)])
        for half in range(HALVES):
            with ExitStack() as ctx:
                w = k.sb(ctx, "up_weights", [P, 2, 2, KC, P])
                ext = k.sb(ctx, "conv_ext", [P, 2, W])
                y = k.sb(ctx, "conv_out", [P, 2, T])
                silu = k.sb(ctx, "silu", [P, T])
                loaded = [k.sem(ctx, f"up_loaded{s}") for s in range(2)]
                multiplied = k.sem(ctx, "up_multiplied")
                copied = k.sem(ctx, "up_copied")
                convolved = k.sem(ctx, "convolved")
                silued = k.sem(ctx, "silued")
                gate_done = k.sem(ctx, "gated_ready")
                stated = k.sem(ctx, "conv_states_placed")
                tailed = k.sem(ctx, "conv_tails_taken")
                block = ctx.enter_context(nc.Block())
                base = half * FH

                @block.sync
                def _(sp):
                    def load(m, j, s):
                        sp.wait_ge(multiplied, m * 2 + 2)
                        sp.dma_start(w[:, s, 0, :, :], k.ins["w_up"][layer, m + base]).then_inc(loaded[s], 16)
                        sp.dma_start(w[:, s, 1, :, :], k.ins["w_up"][layer, m + (base + FC)]).then_inc(loaded[s], 16)
                    pairs(sp, FH, load)

                @block.tensor
                def _(pe):
                    pe.sem_inc(multiplied, 4)

                    def multiply(m, j, s):
                        pe.wait_ge(loaded[s], j * 32 + 32)
                        for av in range(2):
                            pe.wait_ge(copied, m * 2 + (av + 1))
                            for a, cols in NT:
                                for kk in range(KC):
                                    last = pe.matmul(bank_set(k, av)[:, a:a + cols], w[:, s, av, kk, :], xn[:, kk, a:a + cols],
                                                     start=kk == 0, stop=kk == KC - 1)
                            last.then_inc(multiplied, 1)
                    pairs(pe, FH, multiply)

                def ext_parts(av):
                    return ext[:, av, 0:EP], ext[:, av, EP:W].rearrange("p (b n) -> p b n", b=B)

                @block.scalar
                def _(act):
                    act.sem_inc(copied, 2)

                    def one(m, j, s):
                        for av in range(2):
                            act.wait_ge(multiplied, m * 2 + (av + 5))
                            ep, es = ext_parts(av)
                            bs = bank_set(k, av)
                            ch = m + (base + av * FC)
                            act.wait_ge(gate_done, m)
                            act.wait_ge(tailed, m)
                            act.activation(y[:, av, :], bs, ACT.Identity, bias=c["conv_b"][:, layer, bass.ds(ch, 1)],
                                           scale=c["conv_w"][:, layer, 2, bass.ds(ch, 1)])
                            act.activation(ep[:, 2:EP], bs[:, 0:SEQ], ACT.Copy)
                            act.activation(es[:, :, 2:ES], samples(bs), ACT.Copy).then_inc(copied, 1)
                        act.wait_ge(convolved, m + 1)
                        act.activation(silu[:, :], y[:, 0, :], ACT.Silu).then_inc(silued, 1)
                    pairs(act, FH, one)

                @block.gpsimd
                def _(pool):
                    pool.memset(ext[:, :, 0:2], 0.0)

                    def one(m, j, s):
                        pool.wait_ge(gate_done, m)
                        for av in range(2):
                            ep, es = ext_parts(av)
                            ch = m + (base + av * FC)
                            last = pool.tensor_copy(es[:, :, 0:2], c["conv_state"][:, layer, bass.ds(ch, 1), :].rearrange("p a (b n) -> p (a b) n", b=B))
                        pool.drain().then_inc(stated, 1)
                        pool.wait_ge(copied, m * 2 + 4)
                        for av in range(2):
                            ep, es = ext_parts(av)
                            ch = m + (base + av * FC)
                            tail = tails[:, bass.ds(ch, 1), :].rearrange("p a n -> p (a n)")
                            pool.tensor_copy(tail[:, 0:2], ep[:, SEQ:EP])
                            pool.tensor_copy(tail[:, 2:].rearrange("p (b n) -> p b n", b=B), es[:, :, L:ES])
                        pool.drain().then_inc(tailed, 1)
                    pairs(pool, FH, one)

                @block.vector
                def _(dve):
                    def one(m, j, s):
                        dve.wait_ge(stated, m + 1)
                        for av in range(2):
                            dve.wait_ge(copied, m * 2 + (av + 3))
                            ep, es = ext_parts(av)
                            ch = m + (base + av * FC)
                            for tap in (1, 0):
                                wt = c["conv_w"][:, layer, tap, bass.ds(ch, 1)]
                                dve.scalar_tensor_tensor(out=y[:, av, 0:SEQ], in0=ep[:, tap:tap + SEQ], scalar=wt, in1=y[:, av, 0:SEQ],
                                                         op0=ALU.mult, op1=ALU.add)
                                dve.scalar_tensor_tensor(out=samples(y[:, av, :]), in0=es[:, :, tap:tap + L], scalar=wt, in1=samples(y[:, av, :]),
                                                         op0=ALU.mult, op1=ALU.add)
                                dve.drain()
                        dve.drain().then_inc(convolved, 1)
                        dve.wait_ge(silued, m + 1)
                        dve.tensor_tensor(gated[:, m, :], silu[:, :], y[:, 1, :], ALU.mult).then_inc(gate_done, 1)
                    pairs(dve, FH, one)

            def add(dve, m, banks):
                return dve.tensor_tensor(x[:, m, :], x[:, m, :], banks, ALU.add)
            project(k, "down", k.ins["w_down"][layer, half], KC, [(P, gated[:, kk, :]) for kk in range(FH)], add)
        with ExitStack() as ctx:
            stored = k.sem(ctx, "conv_tails_stored")
            block = ctx.enter_context(nc.Block())

            @block.sync
            def _(sp):
                sp.dma_start(k.outs["conv"][layer], tails[:]).then_inc(stored, 16)
                sp.wait_ge(stored, 16)


def store(k, pairs_):
    with ExitStack() as ctx:
        stored = k.sem(ctx, "stored")
        block = ctx.enter_context(k.nc.Block())

        @block.sync
        def _(sp):
            for dst, src in pairs_:
                sp.dma_start(dst, src).then_inc(stored, 16)
            sp.wait_ge(stored, 16 * len(pairs_))


CONSTANTS = dict(
    page_table=[1, B * PAGES],
    ident=[P, P], ones=[P, P], halves=[P, P], flip=[P, P], edge_mask=[P, P], block_mask=[P, 32],
    win_mask=[ROWS, L], sum_heads=[ROWS, G * L], spread_heads=[G * L, ROWS], diag=[P, H], branch=[P, 4],
    shift=[P, G, 2, P], norm_bias=[P, WHOLE + 1], norm_scale=[P, WHOLE + 1], onehot=[BUCKETS + 1, RW],
    relx=[BUCKETS + 1, H], gains=[P, NORMED + 2], xk_gain=[P, 2], g_mix=[P, 2, KC], g_mem=[P, 2, KC],
    g_ffn=[P, 2, KC], cmp_pos=[P, 2, L2], cmp_b1=[P, 2], cmp_w2=[P, 2, HD], cmp_b2k=[P, 1], cmp_b2v=[P, P],
    pool_scale=[P, NPC], pool_counts=[P, 4, 16], conv_b=[P, 2, 2 * FC], conv_w=[P, 2, 3, 2 * FC],
    conv_state=[P, 2, 2 * FC, 2 * B],
)


SMALL_INTEGERS = ("page_table",)
TABLES = ["onehot", "relx", "flip"]
COMPRESSION = ["shift", "cmp_pos", "cmp_b1", "cmp_w2", "cmp_b2k", "cmp_b2v"]
ATTENTION = ["edge_mask", "block_mask", "win_mask", "sum_heads", "spread_heads", "diag", "branch"]
POOLING = ["pool_scale", "pool_counts"]
CONVOLUTION = ["conv_b", "conv_w", "conv_state"]
COMMON = [n for n in CONSTANTS if n not in TABLES + COMPRESSION + ATTENTION + POOLING + CONVOLUTION]


def decoder(nc, ins, outs, n_pages):
    with ExitStack() as ctx:
        k = Kernel(nc, ctx, ins, outs)
        k.n_pages = n_pages
        k.ps = ctx.enter_context(nc.psum_tensor("banks", [P, 8, 512], F32))
        k.cst = {}
        k.passed = ctx.enter_context(nc.semaphore("passed"))
        k.row_dram = nc.dram_tensor("bias_row_scratch", [H, RW], F32, kind="Internal").ap()
        act_ = k.sb(ctx, "activations", [P, KC + 2, T])
        k.mem_k = k.sb(ctx, "mem_keys", [P, 2, 2, NMEM])
        k.mem_v = k.sb(ctx, "mem_values", [P, 2, 2, 2 * P])
        xn = act_[:, 0:KC, :]
        load_constants(k, ctx, COMMON)
        with ExitStack() as m:
            mem = k.sb(m, "memory", [P, KC, NMEM])
            memn = k.sb(m, "memory_normed", [P, KC, NMEM])
            load_x(k, mem, ins["mem"])
            for layer in range(2):
                memory_kv(k, layer, mem, memn)
        with ExitStack() as l0:
            comp_k = k.sb(l0, "compressed_keys", [P, B + 1, NCS])
            comp_v = k.sb(l0, "compressed_values", [NCS, B + 1, P])
            zs = k.sb(l0, "z_samples", [P, NZ, TS])
            load_constants(k, l0, ATTENTION)
            k.row_tail = k.sb(l0, "row_tail_bias", [ROWS, TAIL])
            k.row_far = k.sb(l0, "row_far_bias", [ROWS, 2])
            k.row_blocks = k.sb(l0, "row_block_bias", [ROWS, NCS])
            k.row_select = k.sb(l0, "row_select_bias", [ROWS, NBS])
            k.row_window = k.sb(l0, "row_window_bias", [ROWS, WINDOW + L])
            lz = l0.enter_context(ExitStack())
            z = k.sb(lz, "z", [P, NZ, T])
            with ExitStack() as n:
                x0 = k.sb(n, "x_first", [P, KC, T])
                load_x(k, x0, ins["x"])
                rms_norm(k, x0, xn, k.cst["g_mix"][:, 0, :], T)
            project(k, "in0", ins["w_in0"], NZ, [(P, xn[:, kk, :]) for kk in range(KC)],
                    lambda dve, m, banks: dve.tensor_copy(z[:, m, :], banks))
            head_norms(k, z, NORMED, 0)
            store(k, [(outs["rows"], z[:, Z_KS:Z_GATE, :]),
                      (outs["win_k"][:, :, 0:WINDOW - L], ins["win_k"][:, :, L:WINDOW]),
                      (outs["win_v"][:, 0:WINDOW - L, :], ins["win_v"][:, L:WINDOW, :])])
            compress(k, z, act_, comp_k, comp_v)
            with ExitStack() as n:
                k.near_bias = k.sb(n, "near_bias", [P, H, 256])
                k.block_bias = k.sb(n, "block_bias", [P, H, 32])
                bias_tables(k)
                vals = k.sb(n, "prompt_values", [P, 2, QT, P])
                token_major_values(k, z, vals)
                prompt_attention(k, z, zs, vals, comp_k, comp_v, act_)
            memory_attention(k, 0, z[:, Z_XQ:Z_XQ + 2, :], act_[:, R:R + 2, :])
            lz.close()
            sample_attention(k, zs, comp_k, comp_v, act_)
        x = k.sb(ctx, "x", [P, KC, T])

        def add(dve, m, banks):
            return dve.tensor_tensor(x[:, m, :], x[:, m, :], banks, ALU.add)
        load_x(k, x, ins["x"])
        project(k, "out0", ins["w_out0"], KC, [(P, act_[:, kk, :]) for kk in range(R + 2)], add)
        rms_norm(k, x, xn, k.cst["g_ffn"][:, 0, :], T)
        conv_ffn(k, 0, xn, x)
        rms_norm(k, x, xn, k.cst["g_mix"][:, 1, :], T)
        with ExitStack() as l1:
            z = k.sb(l1, "z_pool", [P, NPC + 2, T])
            project(k, "in1", ins["w_in1"], NPC + 2, [(P, xn[:, kk, :]) for kk in range(KC)],
                    lambda dve, m, banks: dve.tensor_copy(z[:, m, :], banks))
            head_norms(k, z[:, NPC:NPC + 2, :], 2, NORMED)
            pool_mixer(k, z, act_)
            memory_attention(k, 1, z[:, NPC:NPC + 2, :], act_[:, NPC:NPC + 2, :])
        project(k, "out1", ins["w_out1"], KC,
                [(PCH, act_[0:PCH, kk, :]) for kk in range(NPC)] + [(P, act_[:, NPC + kk, :]) for kk in range(2)], add)
        rms_norm(k, x, xn, k.cst["g_ffn"][:, 1, :], T)
        conv_ffn(k, 1, xn, x)
        store(k, [(outs["y"], x[:])])


def rel_buckets(dist):
    exact = BUCKETS // 2
    n = np.maximum(dist, 0)
    nf = np.maximum(n, 1).astype(np.float32)
    large = exact + (np.log(nf / np.float32(exact)) / np.float32(np.log(128 / exact)) * np.float32(BUCKETS - exact)).astype(np.int32)
    return np.where(n < exact, n, np.minimum(large, BUCKETS - 1))


def shape_constants():
    f = np.float32
    eye = np.eye(P, dtype=f)
    out = dict(ident=eye, ones=np.ones((P, P), f), halves=np.kron(np.eye(2), np.ones((HD, HD))).astype(f),
               flip=eye[::-1].copy())
    q, kk = np.arange(P)[:, None], np.arange(P)[None, :]
    out["edge_mask"] = np.where(kk >= q, 0, NEG).astype(f)
    m = np.arange(32)[None, :] - 16
    out["block_mask"] = (q - 63 - CB * m >= 0).astype(f)
    row_q = (np.arange(ROWS) % L)[:, None]
    out["win_mask"] = np.where(np.arange(L)[None, :] >= row_q, 0, NEG).astype(f)
    rows = np.arange(ROWS)
    gq = rows // GR * L + rows % L
    out["sum_heads"] = (gq[:, None] == np.arange(G * L)[None, :]).astype(f)
    out["spread_heads"] = out["sum_heads"].T.copy()
    diag = np.zeros((P, H), f)
    for j in range(3):
        diag[32 * j + np.arange(H), np.arange(H)] = 1
    out["diag"] = diag
    out["branch"] = np.zeros((P, 4), f)
    for j in range(3):
        out["branch"][32 * j:32 * j + H, j] = 1
    shift = np.zeros((P, G, 2, P), f)
    for g in range(G):
        for lp in range(2):
            shift[g * HD + np.arange(HD), g, lp, lp * HD + np.arange(HD)] = 1
    out["shift"] = shift
    eps = 1e-6
    is_q = np.array([i not in (Z_KS, Z_KW) for i in range(WHOLE)])
    scale = np.where(is_q, 1.0 / HD / SCALE ** 2, 1.0 / HD)
    bias = np.where(is_q, eps / SCALE ** 2, eps)
    out["norm_scale"] = np.broadcast_to(np.append(scale, 1.0 / D_MODEL), (P, WHOLE + 1)).astype(f)
    out["norm_bias"] = np.broadcast_to(np.append(bias, eps), (P, WHOLE + 1)).astype(f)
    dist = 255 - np.arange(RW)
    onehot = np.zeros((BUCKETS + 1, RW), f)
    onehot[np.where(dist >= 0, rel_buckets(dist), BUCKETS), np.arange(RW)] = 1
    out["onehot"] = onehot
    pos = np.arange(16)
    counts = np.stack([w / np.minimum(w, pos + 1) for w in POOLW])
    out["pool_counts"] = np.broadcast_to(counts, (P, 4, 16)).astype(f)
    return out


def lay_out(a):
    f = np.float32
    con = np.ascontiguousarray
    d = shape_constants()

    def chunks(w, cols=None, m=P, kchunks=None):
        kk = w.shape[0] // P
        return con(w.reshape(kk, P, -1, m).transpose(2, 1, 0, 3))

    def feature(g):
        return con(g.reshape(g.shape[0], -1, P).transpose(2, 0, 1))

    x = np.concatenate([a["x_prompt"][0], a["x_sample"].reshape(TS, D_MODEL)], 0)
    d["x"] = con(x.T.reshape(KC, P, T))
    d["mem"] = con(a["mem_prompt"][0].T.reshape(KC, P, NMEM))
    d["relx"] = np.concatenate([a["rel_bias"], np.full((1, H), NEG, f)], 0)
    wi = a["w_in_nsa"][0]
    qw = wi[:, :H * HD].reshape(D_MODEL, G, R, HD).transpose(0, 2, 1, 3).reshape(D_MODEL, H * HD)
    kvw = wi[:, H * HD:H * HD + 6 * P].reshape(D_MODEL, 6, P)
    gw = wi[:, H * HD + 6 * P:H * HD + 6 * P + 3 * H].reshape(D_MODEL, H, 3)
    gate = np.zeros((D_MODEL, 4, 32), f)
    gate[:, 0:3, 0:H] = gw.transpose(0, 2, 1)
    xq = wi[:, H * HD + 6 * P + 3 * H:]
    w0 = np.concatenate([qw, kvw[:, 2], kvw[:, 4], xq, kvw[:, 0], kvw[:, 1], kvw[:, 3], kvw[:, 5], gate.reshape(D_MODEL, P)], 1)
    d["w_in0"] = chunks(w0)
    w1 = a["w_in_pool"][0]
    pool = np.zeros((D_MODEL, NPC, P), f)
    pool[:, :, 0:PCH] = w1[:, :NPC * PCH].reshape(D_MODEL, NPC, PCH)
    d["w_in1"] = chunks(np.concatenate([pool.reshape(D_MODEL, NPC * P), w1[:, NPC * PCH:]], 1))
    wo = a["w_out"][0]
    wo0 = np.concatenate([wo[:H * HD].reshape(G, R, HD, D_MODEL).transpose(1, 0, 2, 3).reshape(H * HD, D_MODEL), wo[H * HD:]], 0)
    d["w_out0"] = chunks(wo0)
    wo = a["w_out"][1]
    wp = np.zeros((NPC, P, D_MODEL), f)
    wp[:, 0:PCH] = wo[:NPC * PCH].reshape(NPC, PCH, D_MODEL)
    d["w_out1"] = chunks(np.concatenate([wp.reshape(NPC * P, D_MODEL), wo[NPC * PCH:]], 0))
    d["w_mem"] = con(a["w_mem_kv"].reshape(2, KC, P, 4 * P).transpose(0, 2, 1, 3))
    d["w_up"] = con(a["w_up"].reshape(2, KC, P, 2 * FC, P).transpose(0, 3, 2, 1, 4))
    d["w_down"] = con(a["w_down"].reshape(2, HALVES, FH, P, KC, P).transpose(0, 1, 4, 3, 2, 5))
    twice = lambda g: np.concatenate([g, g], -1)
    qg, kg, xqg = twice(a["q_gain_nsa"][0]), twice(a["k_gain_nsa"][0]), twice(a["xq_gain"])
    d["gains"] = con(np.stack([qg] * R + [kg] * 2 + [xqg[0]] * 2 + [xqg[1]] * 2, 1))
    d["xk_gain"] = con(twice(a["xk_gain"]).T)
    for n in ("g_mix", "g_mem", "g_ffn"):
        d[n] = feature(a[n])
    d["cmp_pos"] = con(a["cmp_pos"][0].reshape(2, L2, 2, HD).transpose(2, 3, 0, 1).reshape(P, 2, L2))
    d["cmp_w1"] = con(a["cmp_w1"][0].reshape(2, L2, 2, HD, P).transpose(2, 3, 0, 1, 4).reshape(P, 2, L2, P))
    d["cmp_b1"] = con(a["cmp_b1"][0].T)
    d["cmp_w2"] = con(a["cmp_w2"][0].transpose(1, 0, 2))
    d["cmp_b2k"] = con(twice(a["cmp_b2"][0, 0])[:, None])
    d["cmp_b2v"] = con(np.broadcast_to(twice(a["cmp_b2"][0, 1]), (P, P)))
    ps = np.zeros((P, NPC), f)
    ps[0:PCH] = a["pool_scale"][0].reshape(NPC, PCH).T
    d["pool_scale"] = ps
    d["conv_b"] = feature(a["conv_b"])
    d["conv_w"] = con(a["conv_w"].reshape(2, 3, 2 * FC, P).transpose(3, 0, 1, 2))
    d["conv_state"] = con(a["state_ffn_conv"].reshape(2, B, 2, 2 * FC, P).transpose(4, 0, 3, 1, 2).reshape(P, 2, 2 * FC, 2 * B))
    d["pool_state"] = con(a["state_pool"][0].reshape(B, PST, NPC, PCH).transpose(3, 2, 0, 1).reshape(PCH, NPC, B * PST))
    d["w_grp"] = con(a["w_pool_grp"][0].reshape(4, 2, PCH, PG).transpose(2, 0, 1, 3).reshape(PCH, NPC, PG))
    cache = a["cache_nsa_kv"][0]
    n = cache.shape[0]
    cmp_rows = cache[:, :, 0:2].reshape(n, 2, L2, 2, 2, G, HD)
    d["cmp_pages"] = con(cmp_rows.transpose(0, 3, 6, 4, 2, 5, 1).reshape(n, P, 2 * L2 * G * 2))
    d["kv_pages"] = np.concatenate([cache[:, :, 2].reshape(n, PAGE, P).transpose(0, 2, 1), cache[:, :, 3].reshape(n, PAGE, P)], 2)
    win = a["cache_nsa_win"][0]
    d["win_k"] = con(win[:, :, 0].reshape(B, WINDOW, P).transpose(0, 2, 1))
    d["win_v"] = con(win[:, :, 1].reshape(B, WINDOW, P))
    cm = a["cache_mem_kv"]
    d["cmem_k"] = con(cm[:, :, :, 0].reshape(2, B, NMEM, 2, P).transpose(0, 1, 4, 3, 2).reshape(2, B, P, 2 * NMEM))
    d["cmem_v"] = con(cm[:, :, :, 1].reshape(2, B, 2, P, 2 * P).transpose(0, 1, 3, 2, 4).reshape(2, B, P, 4 * P))
    d["page_table"] = con(a["page_table"].astype(np.int32).reshape(1, B * PAGES))
    return {name: con(v) for name, v in d.items()}


_OUTS = dict(y=[P, KC, T], rows=[P, Z_GATE - Z_KS, T], win_k=[B, P, WINDOW], win_v=[B, WINDOW, P],
             mem_k=[2, P, 2, NMEM], mem_v=[2, P, 2, 2 * P], pool=[PCH, NPC, PST * (1 + B)],
             conv=[2, P, 2 * FC, 2 * (1 + B)])


def kernel(**inputs):
    import concourse.bacc as bacc
    from concourse.bass_utils import run_bass_kernel_spmd

    a = {n: np.asarray(v) for n, v in inputs.items()}
    arrays = lay_out(a)
    nc = bacc.Bacc("TRN2", target_bir_lowering=False, num_devices=1)
    ins = {n: nc.dram_tensor(f"in_{n}", v.shape, mybir.dt.from_np(v.dtype), kind="ExternalInput").ap() for n, v in arrays.items()}
    outs = {n: nc.dram_tensor(f"out_{n}", s, F32, kind="ExternalOutput").ap() for n, s in _OUTS.items()}
    decoder(nc, ins, outs, a["cache_nsa_kv"].shape[1])
    r = run_bass_kernel_spmd(nc, [{f"in_{n}": v for n, v in arrays.items()}], core_ids=[0]).results[0]
    o = {n: r[f"out_{n}"] for n in _OUTS}

    y = o["y"].transpose(2, 1, 0).reshape(T, D_MODEL)
    y_prompt, y_sample = y[None, :SEQ], y[SEQ:].reshape(B, L, D_MODEL)
    at = {s: c - Z_KS for s, c in enumerate((Z_KC, Z_VC, Z_KS, Z_VS, Z_KW, Z_VW))}
    rows = np.stack([o["rows"][:, at[s], :].T.reshape(T, G, HD) for s in range(6)], 1)
    kv_p = rows[None, None, :SEQ, 0:4]
    kv_s = rows[SEQ:, 0:4].reshape(1, B, L, 4, G, HD)
    win_p = rows[None, None, SEQ - WINDOW:SEQ, 4:6]
    new = rows[SEQ:, 4:6].reshape(B, L, 2, G, HD)
    old = np.stack([o["win_k"].transpose(0, 2, 1), o["win_v"]], 2)[:, :WINDOW - L].reshape(B, WINDOW - L, 2, G, HD)
    win_s = np.concatenate([old, new], 1)[None]
    mk = o["mem_k"].transpose(0, 3, 2, 1).reshape(2, NMEM, XH, HD)
    mv = o["mem_v"].transpose(0, 2, 1, 3).reshape(2, NMEM, XH, HD)
    mem_kv = np.stack([mk, mv], 2)[:, None]
    pool = o["pool"].reshape(PCH, NPC, 1 + B, PST).transpose(2, 3, 1, 0).reshape(1 + B, PST, NPC * PCH)
    conv = o["conv"].reshape(2, P, 2 * FC, 1 + B, 2).transpose(0, 3, 4, 2, 1).reshape(2, 1 + B, 2, 2 * DFF)
    got = (y_prompt, y_sample, kv_p, kv_s, win_p, win_s, mem_kv, pool[None, :1], pool[None, 1:], conv[:, :1], conv[:, 1:])
    return tuple(np.ascontiguousarray(v, dtype=np.float32) for v in got)
```

```python
from contextlib import ExitStack

import numpy as np
import concourse.bass as bass
from concourse import mybir

F32 = mybir.dt.float32
F32R = mybir.dt.float32r
I32 = mybir.dt.int32
ALU = mybir.AluOpType
ACT = mybir.ActivationFunctionType
X = mybir.AxisListType.X

P = 128
D_MODEL = 1024
KC = D_MODEL // P
SEQ = 1024
B, L = 8, 8
TS = B * L
T = SEQ + TS
QT = SEQ // P
PAST = 4096
PAGE = 128
PAGES = PAST // PAGE
HD = 64
G, R = 2, 6
H = G * R
ROWS = H * L
GR = R * L
CB = 64
L2 = CB // 2
NCP = SEQ // CB
NCS = PAST // CB
NBS = NCS + 1
WINDOW = 512
XH = 4
NMEM = 256
DFF = 2816
FC = DFF // P
PARTS = (6, 6, 5, 5)
PG = 192
PCH = 96
NPC = 8
POOLW = (2, 4, 8, 16)
PST = 15
BUCKETS = 32
RW = 384
NEG = -1e30
FORCED = 1e4
SCALE = HD ** -0.5
LOWEST = -3e38
TAIL = P + L
NT = ((0, 512), (512, 512), (1024, 64))

Z_Q, Z_KS, Z_KW, Z_XQ, Z_KC, Z_VC, Z_VS, Z_VW, Z_GATE = 0, 6, 7, 8, 10, 11, 12, 13, 14
NZ = 15
NORMED = 10
WHOLE = NORMED + 2


def pairs(eng, n, body):
    if n // 2:
        with eng.Fori(0, n // 2) as j:
            body(j * 2, j, 0)
            body(j * 2 + 1, j, 1)
    if n % 2:
        body(n - 1, n // 2, 0)


class Kernel:

    def __init__(self, nc, ctx, ins, outs):
        self.nc, self.ctx, self.ins, self.outs = nc, ctx, ins, outs
        self.made = 0
        self.sems_of, self.sems = None, []
        self.cleared = []

    def sb(self, ctx, name, shape, dtype=F32):
        self.made += 1
        return ctx.enter_context(self.nc.sbuf_tensor(f"{name}_{self.made}", shape, dtype))

    def retire(self, sems):
        for s in self.cleared:
            self.nc.release_semaphore(s)
        for s in sems:
            self.nc.gpsimd.sem_clear(s)
        self.cleared = sems

    def sem(self, ctx, name):
        if self.sems_of is not ctx:
            self.sems_of, self.sems = ctx, []
            ctx.callback(self.retire, self.sems)
        self.made += 1
        self.sems.append(self.nc.alloc_semaphore(f"{name}_{self.made}"))
        return self.sems[-1]


def wait_apart(k, eng, sem, value):
    eng.wait_ge(sem, value)
    eng.sem_inc(k.passed, 1)


LOOKUP = 8


def load_pages(k, sp, b, pages, dst, loaded):
    with sp.Fori(0, PAGES // LOOKUP) as i:
        _, found = k.nc.values_load_multi_w_load_instructions(
            k.cst["page_table"][0:1, bass.ds(b * PAGES + i * LOOKUP, LOOKUP)], engines=(mybir.EngineType.SP,),
            min_val=0, max_val=k.n_pages - 1)
        for x in range(LOOKUP):
            sp.dma_start(dst[:, bass.ds(i * LOOKUP + x, 1), :].rearrange("p a n -> p (a n)"), pages[found[x]]).then_inc(loaded, 16)


def bank_set(k, s):
    return k.ps[:, 3 * s:3 * s + 3, :].rearrange("p b n -> p (b n)")[:, 0:T]


def samples(ap):
    return ap[:, SEQ:T].rearrange("p (b q) -> p b q", b=B)


def load_constants(k, octx, names):
    for n in names:
        k.cst[n] = k.sb(octx, n, CONSTANTS[n], I32 if n in SMALL_INTEGERS else F32)
    with ExitStack() as ctx:
        loaded = k.sem(ctx, "constants_loaded")
        block = ctx.enter_context(k.nc.Block())

        @block.sync
        def _(sp):
            for n in names:
                sp.dma_start(k.cst[n][:], k.ins[n]).then_inc(loaded, 16)
            sp.wait_ge(loaded, 16 * len(names))


def bias_tables(k):
    nc, c = k.nc, k.cst
    with ExitStack() as ctx:
        load_constants(k, ctx, TABLES)
        row = k.sb(ctx, "bias_row", [H, RW])
        hank = k.sb(ctx, "bias_hankel", [P, H, 256])
        row_ready = k.sem(ctx, "bias_row_product")
        row_read = k.sem(ctx, "bias_row_read")
        row_stored = k.sem(ctx, "bias_row_stored")
        tables_loaded = k.sem(ctx, "tables_loaded")
        flipped = k.sem(ctx, "tables_flipped")
        block = ctx.enter_context(nc.Block())

        @block.tensor
        def _(pe):
            pe.matmul(k.ps[0:H, 0, 0:RW], c["relx"][:, :], c["onehot"][:, :], start=True, stop=True).then_inc(row_ready, 1)
            pe.wait_ge(tables_loaded, 16 * (1 + 2 * L))
            for i in range(6):
                last = pe.matmul(k.ps[:, i, :], c["flip"][:, :], hank[:, 2 * i:2 * i + 2, :], start=True, stop=True)
            last.then_inc(flipped, 1)

        @block.vector
        def _(dve):
            dve.wait_ge(row_ready, 1)
            dve.tensor_copy(row[:], k.ps[0:H, 0, 0:RW]).then_inc(row_read, 1)
            dve.wait_ge(flipped, 1)
            dve.tensor_copy(k.near_bias[:], k.ps[:, 0:6, :].rearrange("p i (h n) -> p (i h) n", h=2))
            dve.memset(k.block_bias[:], NEG)
            dve.drain()
            dve.tensor_copy(k.block_bias[:, :, 14:18], k.near_bias[:, :, CB - 1:256:CB])
            dve.tensor_copy(k.block_bias[:, :, 0:14], k.near_bias[:, :, 0:1].broadcast_to([P, H, 14]))
            far = k.row_far[:, 0:1]
            dve.tensor_copy(k.row_blocks[:, 0:NCS - 2], far.broadcast_to([ROWS, NCS - 2]))
            dve.tensor_copy(k.row_blocks[:, NCS - 2:NCS - 1], k.row_tail[:, 63:64])
            dve.tensor_copy(k.row_blocks[:, NCS - 1:NCS], k.row_tail[:, 127:128])
            dve.memset(k.row_select[:], 0.0)
            dve.drain()
            dve.tensor_copy(k.row_select[:, 0:NCS - 2], far.broadcast_to([ROWS, NCS - 2]))
            dve.tensor_copy(k.row_window[:, 0:WINDOW - P], far.broadcast_to([ROWS, WINDOW - P]))
            dve.tensor_copy(k.row_window[:, WINDOW - P:WINDOW + L], k.row_tail[:, :])
            dve.drain()
            dve.tensor_tensor(k.row_window[:, 0:L], k.row_window[:, 0:L], c["win_mask"][:, :], ALU.add)

        @block.sync
        def _(sp):
            sp.wait_ge(row_read, 1)
            sp.dma_start(k.row_dram, row[:]).then_inc(row_stored, 16)
            sp.wait_ge(row_stored, 16)
            sp.dma_start(hank[:], bass.AP(k.row_dram.tensor, 0, [[1, P], [RW, H], [1, 256]])).then_inc(tables_loaded, 16)
            for q in range(L):
                sp.dma_start(k.row_tail[q:ROWS:L, :], k.row_dram[:, 127 - q:127 - q + TAIL]).then_inc(tables_loaded, 16)
                sp.dma_start(k.row_far[q:ROWS:L, :], k.row_dram[:, 0:2]).then_inc(tables_loaded, 16)
            sp.wait_ge(tables_loaded, 16 * (1 + 2 * L))


def load_x(k, x, src):
    with ExitStack() as ctx:
        loaded = k.sem(ctx, "x_loaded")
        block = ctx.enter_context(k.nc.Block())

        @block.sync
        def _(sp):
            sp.dma_start(x[:], src.rearrange("k p t -> p k t")).then_inc(loaded, 16)
            sp.wait_ge(loaded, 16)


def rms_norm(k, x, out, gain, n):
    c = k.cst
    cuts = [(a, min(512, n - a)) for a in range(0, n, 512)]
    parts = isinstance(out, tuple)
    with ExitStack() as ctx:
        sq = k.sb(ctx, "squares", [P, 2, n])
        acc = k.sb(ctx, "squares_added", [P, n])
        rms = k.sb(ctx, "rms", [P, n])
        whole = sq
        squared = k.sem(ctx, "squared")
        added = k.sem(ctx, "squares_added")
        summed = k.sem(ctx, "squares_summed")
        rooted = k.sem(ctx, "rooted")
        normed = k.sem(ctx, "normed")
        rounded = k.sem(ctx, "rounded")
        split = k.sem(ctx, "split")
        block = ctx.enter_context(k.nc.Block())
        total = k.ps[:, 0:3, :].rearrange("p b n -> p (b n)")[:, 0:n]

        @block.scalar
        def _(act):
            for i in range(KC):
                if i >= 2:
                    act.wait_ge(added, i - 1)
                act.activation(sq[:, i % 2, :], x[:, i, :], ACT.Square).then_inc(squared, 1)
            act.wait_ge(summed, 1)
            act.activation(rms[:], total, ACT.Sqrt, bias=c["norm_bias"][:, WHOLE:WHOLE + 1],
                           scale=c["norm_scale"][:, WHOLE:WHOLE + 1]).then_inc(rooted, 1)
            if parts:
                for i in range(KC):
                    act.wait_ge(normed, i + 1)
                    act.activation(out[0][:, i, :], whole[:, i % 2, :], ACT.Copy).then_inc(rounded, 1)

        @block.gpsimd
        def _(pool):
            for i in range(KC):
                pool.wait_ge(squared, i + 1)
                if i == 1:
                    pool.tensor_tensor(acc[:], sq[:, 0, :], sq[:, 1, :], ALU.add).then_inc(added, 2)
                elif i > 1:
                    pool.tensor_tensor(acc[:], acc[:], sq[:, i % 2, :], ALU.add).then_inc(added, 1)
                pool.drain()
            if parts:
                for i in range(KC):
                    pool.wait_ge(rounded, i + 1)
                    pool.tensor_tensor(out[1][:, i, :], whole[:, i % 2, :], out[0][:, i, :].bitcast(F32), ALU.subtract).then_inc(split, 1)

        @block.tensor
        def _(pe):
            pe.wait_ge(added, KC)
            for a, w in cuts:
                last = pe.matmul(total[:, a:a + w], c["ones"][:, :], acc[:, a:a + w], start=True, stop=True)
            last.then_inc(summed, 1)

        @block.vector
        def _(dve):
            dve.wait_ge(rooted, 1)
            dve.reciprocal(rms[:], rms[:])
            dve.drain()
            for i in range(KC):
                if parts and i >= 2:
                    dve.wait_ge(split, i - 1)
                dve.scalar_tensor_tensor(out=whole[:, i % 2, :] if parts else out[:, i, :], in0=x[:, i, :], scalar=gain[:, i:i + 1],
                                         in1=rms[:], op0=ALU.mult, op1=ALU.mult).then_inc(normed, 1)


def split_tokens(k, src, out, chunks):
    with ExitStack() as ctx:
        rounded = k.sem(ctx, "rounded")
        block = ctx.enter_context(k.nc.Block())

        @block.scalar
        def _(act):
            for rows, i in chunks:
                act.activation(out[0][0:rows, i, :], src[0:rows, i, :], ACT.Copy).then_inc(rounded, 1)

        @block.vector
        def _(dve):
            for n, (rows, i) in enumerate(chunks):
                dve.wait_ge(rounded, n + 1)
                dve.tensor_tensor(out[1][0:rows, i, :], src[0:rows, i, :], out[0][0:rows, i, :].bitcast(F32), ALU.subtract)


class Weights:

    def __init__(self, k, ctx, name, cols):
        self.whole = k.sb(ctx, name + "_whole", [P, 2, cols])
        self.high = k.sb(ctx, name + "_high", [P, 2, cols], F32R)
        self.low = k.sb(ctx, name + "_low", [P, 2, cols], F32R)
        self.loaded = [k.sem(ctx, f"{name}_loaded{s}") for s in range(2)]
        self.split = k.sem(ctx, name + "_split")
        self.multiplied = k.sem(ctx, name + "_multiplied")

    def load(self, sp, t, s, src, cols):
        sp.wait_ge(self.split, t + 1)
        sp.dma_start(self.whole[:, s, 0:cols], src).then_inc(self.loaded[s], 16)

    def part(self, k, pool, t, j, s, cols):
        whole, high, low = (x[:, s, 0:cols] for x in (self.whole, self.high, self.low))
        pool.wait_ge(self.loaded[s], j * 16 + 16)
        wait_apart(k, pool, self.multiplied, t + 1)
        pool.tensor_scalar(high, whole, 1.0, None, ALU.mult)
        pool.drain()
        pool.tensor_tensor(low, whole, high.bitcast(F32), ALU.subtract).then_inc(self.split, 1)

    def multiply(self, pe, t, s, terms, out, width=P):
        pe.wait_ge(self.split, t + 3)
        for a, cols in NT:
            for kk, (rows, high, low) in enumerate(terms):
                wh = self.high[0:rows, s, kk * P:kk * P + width]
                wl = self.low[0:rows, s, kk * P:kk * P + width]
                o = out[0:width, a:a + cols]
                pe.matmul(o, wh, high[:, a:a + cols], start=kk == 0, stop=False)
                pe.matmul(o, wh, low[:, a:a + cols], start=False, stop=False)
                last = pe.matmul(o, wl, high[:, a:a + cols], start=False, stop=kk == len(terms) - 1)
        last.then_inc(self.multiplied, 1)


def project(k, name, w_src, n, terms, read):
    cols = len(terms) * P
    with ExitStack() as ctx:
        w = Weights(k, ctx, name, cols)
        taken = k.sem(ctx, name + "_taken")
        block = ctx.enter_context(k.nc.Block())

        @block.sync
        def _(sp):
            pairs(sp, n, lambda m, j, s: w.load(sp, m, s, w_src[m], cols))

        @block.gpsimd
        def _(pool):
            pool.sem_inc(w.split, 2)
            pairs(pool, n, lambda m, j, s: w.part(k, pool, m, j, s, cols))

        @block.tensor
        def _(pe):
            pe.sem_inc(w.multiplied, 2)

            def multiply(m, j, s):
                pe.wait_ge(taken, m + 1)
                w.multiply(pe, m, s, terms, bank_set(k, s))
            pairs(pe, n, multiply)

        @block.vector
        def _(dve):
            dve.sem_inc(taken, 2)

            def take(m, j, s):
                dve.wait_ge(w.multiplied, m + 3)
                read(dve, m, bank_set(k, s)).then_inc(taken, 1)
            pairs(dve, n, take)


def head_norms(k, z, n, first):
    c = k.cst
    with ExitStack() as ctx:
        sq = k.sb(ctx, "head_squares", [P, 2, T])
        rms = k.sb(ctx, "head_rms", [P, 2, T])
        rstd = k.sb(ctx, "head_rstd", [P, T])
        squared = k.sem(ctx, "head_squared")
        summed = k.sem(ctx, "head_summed")
        rooted = k.sem(ctx, "head_rooted")
        inverted = k.sem(ctx, "head_inverted")
        block = ctx.enter_context(k.nc.Block())

        @block.vector
        def _(dve):
            dve.sem_inc(inverted, 2)

            def normalise(m, j, s):
                dve.wait_ge(rooted, m + 2)
                dve.reciprocal(rstd[:], rms[:, s, :]).then_inc(inverted, 1)
                dve.drain()
                dve.scalar_tensor_tensor(out=z[:, m, :], in0=z[:, m, :], scalar=k.cst["gains"][:, bass.ds(m + first, 1)],
                                         in1=rstd[:], op0=ALU.mult, op1=ALU.mult)
                dve.drain()
            pairs(dve, n, normalise)

        @block.scalar
        def _(act):
            act.sem_inc(rooted, 1)

            def square(m, j, s):
                act.activation(sq[:, s, :], z[:, m, :], ACT.Square).then_inc(squared, 1)
                act.wait_ge(summed, m + 1)
                act.wait_ge(inverted, m + 1)
                act.activation(rms[:, s, :], bank_set(k, s), ACT.Sqrt,
                               bias=c["norm_bias"][:, bass.ds(m + first, 1)],
                               scale=c["norm_scale"][:, bass.ds(m + first, 1)]).then_inc(rooted, 1)
            pairs(act, n, square)

        @block.tensor
        def _(pe):
            def add(m, j, s):
                pe.wait_ge(squared, m + 1)
                pe.wait_ge(rooted, m + 1)
                for a, cols in NT:
                    last = pe.matmul(bank_set(k, s)[:, a:a + cols], c["halves"][:, :], sq[:, s, a:a + cols],
                                     start=True, stop=True)
                last.then_inc(summed, 1)
            pairs(pe, n, add)


def memory_kv(k, layer, mem, memn):
    c = k.cst
    rms_norm(k, mem, memn, c["g_mem"][:, layer, :], NMEM)
    with ExitStack() as ctx:
        w = k.sb(ctx, "mem_weights", [P, KC, 4 * P])
        sq = k.sb(ctx, "mem_squares", [P, 2, NMEM])
        rms = k.sb(ctx, "mem_rms", [P, 2 * NMEM])
        keys = k.mem_k[:, layer, :, :]
        loaded = k.sem(ctx, "mem_weights_loaded")
        multiplied = k.sem(ctx, "mem_multiplied")
        squared = k.sem(ctx, "mem_squared")
        summed = k.sem(ctx, "mem_summed")
        rooted = k.sem(ctx, "mem_rooted")
        written = k.sem(ctx, "mem_written")
        stored = k.sem(ctx, "mem_stored")
        block = ctx.enter_context(k.nc.Block())

        @block.sync
        def _(sp):
            sp.dma_start(w[:], k.ins["w_mem"][layer]).then_inc(loaded, 16)
            sp.wait_ge(written, 1)
            sp.dma_start(k.outs["mem_k"][layer], keys).then_inc(stored, 16)
            sp.dma_start(k.outs["mem_v"][layer], k.mem_v[:, layer, :, :]).then_inc(stored, 16)
            sp.wait_ge(stored, 32)

        @block.tensor
        def _(pe):
            pe.wait_ge(loaded, 16)
            for ch in range(2):
                for kk in range(KC):
                    pe.matmul(k.ps[:, ch, 0:NMEM], w[:, kk, ch * P:(ch + 1) * P], memn[:, kk, :],
                              start=kk == 0, stop=kk == KC - 1)
            for mt in range(2):
                for kk in range(KC):
                    last = pe.matmul(k.ps[:, 2 + mt, 0:NMEM], memn[:, kk, mt * P:(mt + 1) * P], w[:, kk, 2 * P:4 * P],
                                     start=kk == 0, stop=kk == KC - 1)
            last.then_inc(multiplied, 1)
            pe.wait_ge(squared, 1)
            pe.matmul(k.ps[:, 4, :], c["halves"][:, :], sq[:, :, :], start=True, stop=True).then_inc(summed, 1)

        @block.scalar
        def _(act):
            act.wait_ge(multiplied, 1)
            act.activation(sq[:, :, :], k.ps[:, 0:2, 0:NMEM], ACT.Square).then_inc(squared, 1)
            act.wait_ge(summed, 1)
            act.activation(rms[:], k.ps[:, 4, :], ACT.Sqrt, bias=c["norm_bias"][:, Z_KS:Z_KS + 1],
                           scale=c["norm_scale"][:, Z_KS:Z_KS + 1]).then_inc(rooted, 1)

        @block.vector
        def _(dve):
            dve.wait_ge(multiplied, 1)
            dve.tensor_copy(k.mem_v[:, layer, :, :], k.ps[:, 2:4, 0:NMEM])
            dve.wait_ge(rooted, 1)
            dve.reciprocal(rms[:], rms[:])
            dve.drain()
            dve.scalar_tensor_tensor(out=keys, in0=k.ps[:, 0:2, 0:NMEM], scalar=c["xk_gain"][:, layer:layer + 1],
                                     in1=rms[:].rearrange("p (c n) -> p c n", c=2), op0=ALU.mult, op1=ALU.mult)
            dve.drain().then_inc(written, 1)


def token_major_values(k, z, vals):
    with ExitStack() as ctx:
        turned = k.sem(ctx, "values_turned")
        copied = k.sem(ctx, "values_copied")
        block = ctx.enter_context(k.nc.Block())

        @block.tensor
        def _(pe):
            for i in range(4):
                if i >= 2:
                    pe.wait_ge(copied, i - 1)
                for t in range(4):
                    last = pe.transpose(k.ps[:, i % 2, t * P:(t + 1) * P],
                                        z[:, Z_VS + i // 2, (4 * (i % 2) + t) * P:(4 * (i % 2) + t + 1) * P],
                                        k.cst["ident"][:, :])
                last.then_inc(turned, 1)

        @block.vector
        def _(dve):
            for i in range(4):
                dve.wait_ge(turned, i + 1)
                dve.tensor_copy(vals[:, i // 2, 4 * (i % 2):4 * (i % 2) + 4, :],
                                k.ps[:, i % 2, :].rearrange("p (t n) -> p t n", t=4)).then_inc(copied, 1)


def compress(k, z, spare, comp_k, comp_v):
    nc, c = k.nc, k.cst
    QP = PAGES * 2 * G
    with ExitStack() as ctx:
        load_constants(k, ctx, COMPRESSION)
        w1 = k.sb(ctx, "cmp_w1", [P, 2, L2, P])
        row_len = 2 * L2 * G * 2
        rows = [spare[:, :, :].rearrange("p a n -> p (a n)")[:, 0:PAGES * row_len].rearrange("p (a n) -> p a n", a=PAGES),
                k.sb(ctx, "cmp_rows", [P, PAGES, row_len])[:, :, :]]
        own = rows[0][:, 0:8, :].rearrange("p a n -> p (a n)")
        bias = k.sb(ctx, "cmp_bias", [P, 2])
        hid = k.sb(ctx, "cmp_hidden", [P, 2, QP])
        kc = k.sb(ctx, "cmp_keys", [P, NCS])
        sq = k.sb(ctx, "cmp_squares", [P, NCS])
        rms = k.sb(ctx, "cmp_rms", [P, NCS])
        w_loaded = k.sem(ctx, "cmp_weights_loaded")
        rows_loaded = [k.sem(ctx, f"cmp_rows_loaded{s}") for s in range(2)]
        pos_summed = k.sem(ctx, "cmp_pos_summed")
        bias_ready = k.sem(ctx, "cmp_bias_ready")
        hidden = k.sem(ctx, "cmp_hidden_summed")
        active = k.sem(ctx, "cmp_activated")
        mapped = k.sem(ctx, "cmp_mapped")
        squared = k.sem(ctx, "cmp_squared")
        summed = k.sem(ctx, "cmp_squares_summed")
        rooted = k.sem(ctx, "cmp_rooted")
        own_moved = k.sem(ctx, "cmp_own_moved")
        own_written = k.sem(ctx, "cmp_own_written")
        block = ctx.enter_context(nc.Block())

        def row_view(s, kv, l2, n):
            v = rows[s][:, 0:n // (2 * G), :].rearrange("p a (k l c) -> p k l a c", k=2, l=L2)
            return v[:, kv, l2, :, :]

        @block.sync
        def _(sp):
            sp.dma_start(w1[:], k.ins["cmp_w1"]).then_inc(w_loaded, 16)

            def load(b, j, s):
                wait_apart(k, sp, hidden, b + 1)
                load_pages(k, sp, b, k.ins["cmp_pages"], rows[s], rows_loaded[s])
            pairs(sp, B, load)

        def second(pe, kv, b, cols):
            v = hid[:, kv, 0:cols].rearrange("p (g n) -> p g n", g=G)
            for g in range(G):
                if kv == 0:
                    last = pe.matmul(k.ps[g * HD:(g + 1) * HD, 2, 0:cols // G], c["cmp_w2"][:, 0, :], v[:, g, :],
                                     start=True, stop=True)
                else:
                    last = pe.matmul(k.ps[0:cols // G, 4, g * HD:(g + 1) * HD], v[:, g, :], c["cmp_w2"][:, 1, :],
                                     start=True, stop=True)
            return last

        def one(pe, b, s, cols, view):
            for kv in range(2):
                for l2 in range(L2):
                    last = pe.matmul(k.ps[:, kv, 0:cols], w1[:, kv, l2, :], view(kv, l2), start=l2 == 0, stop=l2 == L2 - 1)
            last.then_inc(hidden, 1)
            pe.wait_ge(active, b + 1)
            second(pe, 0, b, cols)
            second(pe, 1, b, cols).then_inc(mapped, 1)
            pe.wait_ge(squared, b + 1)
            pe.matmul(k.ps[:, 3, 0:cols // G], c["halves"][:, :], sq[:, 0:cols // G], start=True, stop=True).then_inc(summed, 1)

        @block.tensor
        def _(pe):
            pe.sem_inc(hidden, 2)
            pe.wait_ge(w_loaded, 16)
            for kv in range(2):
                for l2 in range(L2):
                    last = pe.matmul(k.ps[:, 5 + kv, 0:1], w1[:, kv, l2, :], c["cmp_pos"][:, kv, l2:l2 + 1],
                                     start=l2 == 0, stop=l2 == L2 - 1)
            last.then_inc(pos_summed, 1)

            def sample(b, j, s):
                pe.wait_ge(rows_loaded[s], (j + 1) * (16 * PAGES))
                one(pe, b, s, QP, lambda kv, l2: row_view(s, kv, l2, QP))
            pairs(pe, B, sample)
            for kv in range(2):
                for g in range(G):
                    if kv or g:
                        pe.wait_ge(own_written, 2 * kv + g)
                    for lp in range(2):
                        src = z[:, Z_KC + kv, 0:SEQ].rearrange("p (n l) -> p l n", l=2)[:, lp, :]
                        last = pe.matmul(k.ps[:, 7, :], c["shift"][:, g, lp, :], src, start=lp == 0, stop=lp == 1)
                    last.then_inc(own_moved, 1)
            pe.wait_ge(own_written, 4)
            ov = own.rearrange("p (k l n) -> p k l n", k=2, l=L2)
            one(pe, B, 0, NCP * G, lambda kv, l2: ov[:, kv, l2, :])

        def finish(dve, b, cols):
            n = cols // G
            dve.wait_ge(mapped, b + 1)
            dve.tensor_scalar(kc[:, 0:n], k.ps[:, 2, 0:n], c["cmp_b2k"][:, 0:1], None, ALU.add)
            dve.tensor_tensor(comp_v[0:n, b, :], k.ps[0:n, 4, 0:P], c["cmp_b2v"][0:n, :], ALU.add)
            dve.drain()
            dve.tensor_tensor(sq[:, 0:n], kc[:, 0:n], kc[:, 0:n], ALU.mult).then_inc(squared, 1)
            dve.wait_ge(rooted, b + 1)
            dve.reciprocal(rms[:, 0:n], rms[:, 0:n])
            dve.drain()
            dve.scalar_tensor_tensor(out=comp_k[:, b, 0:n], in0=kc[:, 0:n], scalar=c["gains"][:, Z_KS:Z_KS + 1],
                                     in1=rms[:, 0:n], op0=ALU.mult, op1=ALU.mult)
            dve.drain()

        @block.vector
        def _(dve):
            dve.wait_ge(pos_summed, 1)
            dve.tensor_tensor(bias[:, 0:2], k.ps[:, 5:7, 0:1].rearrange("p a b -> p (a b)"), c["cmp_b1"][:, :], ALU.add).then_inc(bias_ready, 1)

            def sample(b, j, s):
                finish(dve, b, QP)
            pairs(dve, B, sample)
            ov = own.rearrange("p (k l a g c) -> p k l a g c", k=2, l=L2, g=G, c=2)
            for kv in range(2):
                for g in range(G):
                    dve.wait_ge(own_moved, 2 * kv + g + 1)
                    dve.tensor_copy(ov[:, kv, :, :, g, :], k.ps[:, 7, :].rearrange("p (a c l) -> p l a c", l=L2, c=2)).then_inc(own_written, 1)
            finish(dve, B, NCP * G)

        @block.scalar
        def _(act):
            act.wait_ge(bias_ready, 1)

            def gelu(b, cols):
                act.wait_ge(hidden, b + 3)
                for kv in range(2):
                    last = act.activation(hid[:, kv, 0:cols].rearrange("p (g a c) -> p a g c", g=G, c=2),
                                          k.ps[:, kv, 0:cols].rearrange("p (a g c) -> p a g c", g=G, c=2), ACT.Gelu_apprx_tanh, bias=bias[:, kv:kv + 1])
                last.then_inc(active, 1)
                act.wait_ge(summed, b + 1)
                act.activation(rms[:, 0:cols // G], k.ps[:, 3, 0:cols // G], ACT.Sqrt,
                               bias=c["norm_bias"][:, Z_KS:Z_KS + 1], scale=c["norm_scale"][:, Z_KS:Z_KS + 1]).then_inc(rooted, 1)
            pairs(act, B, lambda b, j, s: gelu(b, QP))
            gelu(B, NCP * G)


def prompt_attention(k, z, zs, vals, comp_k, comp_v, mix):
    nc, c = k.nc, k.cst
    UN = QT * G
    WK = WINDOW + P
    with ExitStack() as ctx:
        q = k.sb(ctx, "pair_queries", [P, SEQ])
        far = k.sb(ctx, "pair_bias", [P, G, SEQ])
        win = k.sb(ctx, "pair_window_bias", [P, G, WK])
        cbias = k.sb(ctx, "pair_block_bias", [P, G, 32])
        gates = k.sb(ctx, "gates", [P, QT, 3, H])
        gate_x = z[:, Z_GATE, :]
        pair_gates = k.sb(ctx, "pair_gates", [P, QT, 3, G])
        ls = k.sb(ctx, "logits_selected", [P, 3, SEQ])
        lw = k.sb(ctx, "logits_window", [P, 3, WK])
        lc = k.sb(ctx, "logits_blocks", [P, 3, NCP])
        mx = k.sb(ctx, "maxima", [P, 3, 4])
        nmx = k.sb(ctx, "negated_maxima", [P, 3, 4])
        sums = k.sb(ctx, "sums", [P, 3, 4])
        coef = k.sb(ctx, "coefficients", [P, 3, 4])
        pt = k.sb(ctx, "probs_turned", [P, 4, 512])
        o = k.sb(ctx, "pair_out", [P, 2, P])
        gates_turned = k.sem(ctx, "gates_turned")
        gates_on = k.sem(ctx, "gates_sigmoid")
        gates_read = k.sem(ctx, "gates_read")
        pair_ready = k.sem(ctx, "pair_ready")
        scored = k.sem(ctx, "scored")
        biased = k.sem(ctx, "biased")
        exped = k.sem(ctx, "exped")
        turned = k.sem(ctx, "turned")
        copied = k.sem(ctx, "turned_copied")
        probs_c = k.sem(ctx, "probs_unmasked")
        valued = k.sem(ctx, "valued")
        combined = k.sem(ctx, "combined")
        mixed = k.sem(ctx, "mixed_turned")
        mix_read = k.sem(ctx, "mixed_read")
        block = ctx.enter_context(nc.Block())

        def turns(t):
            lo = max(0, t - 4)
            sel = [("s", i * P, P, i) for i in range(t + 1)]
            w = [("w", (i - t + 4) * P, P, i) for i in range(lo, t + 1)]
            blocks = [("c", 0, NCP, 0)]
            allt = sel + w + blocks
            return [allt[i:i + 4] for i in range(0, len(allt), 4)]

        units = [(t, g) for t in range(QT) for g in range(G)]
        banks_before = [0]
        for t, g in units:
            banks_before.append(banks_before[-1] + len(turns(t)))
        BANKS = banks_before[-1]
        assert BANKS % 4 == 0
        SLOTS = 3

        S_SEL = k.ps[:, 0:2, :].rearrange("p b n -> p (b n)")
        S_WIN = k.ps[:, 2:4, :].rearrange("p b n -> p (b n)")
        S_CMP = k.ps[:, 3, 256:256 + NCP]
        OUT = k.ps[:, 6, :]
        MIXT = k.ps[:, 7, 0:P]

        def score(pe, i, u):
            t, g = units[u]
            rows = slice(g * HD, (g + 1) * HD)
            pe.wait_ge(biased, i * UN + u + 1)
            lhs = q[rows, t * P:(t + 1) * P]
            for a in range(0, (t + 1) * P, 512):
                w = min(512, (t + 1) * P - a)
                pe.matmul(S_SEL[:, a:a + w], lhs, z[rows, Z_KS, a:a + w], start=True, stop=True)
            lo = max(0, t - 4)
            off = (lo - t + 4) * P
            for a, b_ in ((off, 512), (512, WK)):
                if a < b_:
                    pe.matmul(S_WIN[:, a:b_], lhs, z[rows, Z_KW, (t - 4) * P + a:(t - 4) * P + b_], start=True, stop=True)
            pe.matmul(S_CMP, lhs, comp_k[rows, B, 0:NCP], start=True, stop=True).then_inc(scored, 1)

        def turn_out(pe, i, t):
            pe.wait_ge(combined, i * UN + (2 * t + 3))
            pe.wait_ge(mix_read, i * QT + t + 1)
            pe.transpose(MIXT, o[:, t % 2, :], c["ident"][:, :]).then_inc(mixed, 1)

        @block.tensor
        def _(pe):
            for t in range(QT):
                last = pe.transpose(k.ps[:, t // 4, (t % 4) * P:(t % 4 + 1) * P], gate_x[:, t * P:(t + 1) * P], c["ident"][:, :]) if t else None
                if t == 0:
                    pe.wait_ge(gates_on, 1)
                    last = pe.transpose(k.ps[:, 0, 0:P], gate_x[:, 0:P], c["ident"][:, :])
            last.then_inc(gates_turned, 1)
            pe.wait_ge(gates_read, 1)
            with pe.Fori(0, R) as i:
                pe.wait_ge(pair_ready, i + 1)
                score(pe, i, 0)
                score(pe, i, 1)
                for u, (t, g) in enumerate(units):
                    if u + 2 < UN:
                        score(pe, i, u + 2)
                    if g == 0 and t:
                        turn_out(pe, i, t - 1)
                    pe.wait_ge(exped, i * UN + u + 1)
                    groups = turns(t)
                    for n in range(len(groups) + 1):
                        if n < len(groups):
                            at = banks_before[u] + n
                            pe.wait_ge(copied, i * BANKS + (at + 1))
                            for s, (what, col, w, tile) in enumerate(groups[n]):
                                src = {"s": ls, "w": lw, "c": lc}[what]
                                last = pe.transpose(k.ps[0:w, 4 + at % 2, s * P:(s + 1) * P], src[:, u % SLOTS, col:col + w], c["ident"][:, :])
                            last.then_inc(turned, 1)
                        if n >= 1:
                            at = banks_before[u] + n - 1
                            pe.wait_ge(copied, i * BANKS + (at + 3))
                            if n == 1:
                                pe.wait_ge(combined, i * UN + u + 1)
                            lo = max(0, t - 4)
                            for s, (what, col, w, tile) in enumerate(groups[n - 1]):
                                moving = {"s": vals[:, 0, tile, g * HD:(g + 1) * HD],
                                          "w": vals[:, 1, tile, g * HD:(g + 1) * HD],
                                          "c": comp_v[0:NCP, B, g * HD:(g + 1) * HD]}[what]
                                first = {"s": 0, "w": lo, "c": 0}[what]
                                end = {"s": t, "w": t, "c": 0}[what]
                                at_o = {"s": 0, "w": 1, "c": 2}[what] * HD
                                last = pe.matmul(OUT[:, at_o:at_o + HD], pt[0:w, at % 4, s * P:(s + 1) * P], moving,
                                                 start=tile == first, stop=tile == end)
                    last.then_inc(valued, 1)
                turn_out(pe, i, QT - 1)

        @block.vector
        def _(dve):
            dve.sem_inc(biased, 1)
            dve.sem_inc(combined, 1)
            dve.wait_ge(gates_turned, 1)
            for j in range(3):
                last = dve.tensor_copy(gates[:, :, j, :], k.ps[:, 0:2, :].rearrange("p b (t n) -> p (b t) n", t=4)[:, :, 32 * j:32 * j + H])
            last.then_inc(gates_read, 1)
            dve.drain()

            def bias(u):
                t, g = units[u]
                s = u % SLOTS
                w = (t + 1) * P
                off = (max(0, t - 4) - t + 4) * P
                dve.tensor_tensor_reduce(ls[:, s, 0:w], S_SEL[:, 0:w], far[:, g, SEQ - w:SEQ], 1.0, LOWEST, ALU.add, ALU.max, mx[:, s, 0:1])
                dve.tensor_tensor_reduce(lw[:, s, off:WK], S_WIN[:, off:WK], win[:, g, off:WK], 1.0, LOWEST, ALU.add, ALU.max, mx[:, s, 1:2])
                dve.tensor_tensor_reduce(lc[:, s, :], S_CMP, cbias[:, g, 16 - 2 * t:32 - 2 * t], 1.0, LOWEST, ALU.add, ALU.max, mx[:, s, 2:3])
                dve.drain()
                dve.tensor_scalar(nmx[:, s, 0:3], mx[:, s, 0:3], -1.0, None, ALU.mult).then_inc(biased, 1)

            with dve.Fori(0, R) as i:
                dve.tensor_copy(q[:], z[:, i, 0:SEQ])
                for g in range(G):
                    h = i + g * R
                    b31 = k.near_bias[:, h, 0:1]
                    table = k.near_bias[:, h, :]
                    dve.tensor_copy(far[:, g, 0:SEQ - 256], b31.broadcast_to([P, SEQ - 256]))
                    dve.tensor_copy(far[:, g, SEQ - 256:SEQ], table)
                    dve.tensor_copy(win[:, g, P:WK - 256], b31.broadcast_to([P, WK - 256 - P]))
                    dve.tensor_copy(win[:, g, WK - 256:WK], table)
                    dve.tensor_scalar(win[:, g, 0:P], c["edge_mask"][:, :], b31, None, ALU.add)
                    dve.tensor_copy(cbias[:, g, :], k.block_bias[:, h, :])
                    dve.tensor_copy(pair_gates[:, :, :, g], gates[:, :, :, h])
                dve.drain().then_inc(pair_ready, 1)
                for u in range(2):
                    wait_apart(k, dve, scored, i * UN + (u + 1))
                    bias(u)
                for u, (t, g) in enumerate(units):
                    s = u % SLOTS
                    if u + 2 < UN:
                        wait_apart(k, dve, scored, i * UN + (u + 3))
                        bias(u + 2)
                    dve.wait_ge(exped, i * UN + u + 1)
                    dve.reciprocal(coef[:, s, 0:3], sums[:, s, 0:3])
                    dve.drain()
                    for col, j in ((0, 1), (1, 2), (2, 0)):
                        dve.tensor_tensor(coef[:, s, col:col + 1], coef[:, s, col:col + 1], pair_gates[:, t, j, g:g + 1], ALU.mult)
                    dve.drain()
                    dve.wait_ge(valued, i * UN + u + 1)
                    ov = o[:, t % 2, g * HD:(g + 1) * HD]
                    dve.tensor_scalar(ov, OUT[:, 0:HD], coef[:, s, 0:1], None, ALU.mult)
                    dve.drain()
                    dve.scalar_tensor_tensor(out=ov, in0=OUT[:, HD:2 * HD], scalar=coef[:, s, 1:2], in1=ov, op0=ALU.mult, op1=ALU.add)
                    dve.drain()
                    dve.scalar_tensor_tensor(out=ov, in0=OUT[:, 2 * HD:3 * HD], scalar=coef[:, s, 2:3], in1=ov, op0=ALU.mult, op1=ALU.add).then_inc(combined, 1)

        @block.scalar
        def _(act):
            act.activation(gate_x, gate_x, ACT.Sigmoid).then_inc(gates_on, 1)
            act.sem_inc(copied, 2)
            act.sem_inc(mix_read, 1)

            def exponentials(i, u):
                t, g = units[u]
                s = u % SLOTS
                w = (t + 1) * P
                off = (max(0, t - 4) - t + 4) * P
                act.wait_ge(biased, i * UN + (u + 2))
                if u >= SLOTS:
                    act.wait_ge(combined, i * UN + (u - 1))
                act.activation(ls[:, s, 0:w], ls[:, s, 0:w], ACT.Exp, bias=nmx[:, s, 0:1], accum_out=sums[:, s, 0:1])
                act.activation(lw[:, s, off:WK], lw[:, s, off:WK], ACT.Exp, bias=nmx[:, s, 1:2], accum_out=sums[:, s, 1:2])
                act.activation(lc[:, s, :], lc[:, s, :], ACT.Exp, bias=nmx[:, s, 2:3], accum_out=sums[:, s, 2:3])
                act.drain().then_inc(probs_c, 1)

            def place(i, t):
                act.wait_ge(mixed, i * QT + (t + 1))
                act.activation(mix[:, i, t * P:(t + 1) * P], MIXT, ACT.Copy).then_inc(mix_read, 1)

            with act.Fori(0, R) as i:
                exponentials(i, 0)
                for u, (t, g) in enumerate(units):
                    if u + 1 < UN:
                        exponentials(i, u + 1)
                    if g == 0 and t:
                        place(i, t - 1)
                    for n, group in enumerate(turns(t)):
                        at = banks_before[u] + n
                        act.wait_ge(turned, i * BANKS + (at + 1))
                        full = sum(x[0] != "c" for x in group) * P
                        if full:
                            last = act.activation(pt[:, at % 4, 0:full], k.ps[:, 4 + at % 2, 0:full], ACT.Copy)
                        if full < len(group) * P:
                            last = act.activation(pt[0:NCP, at % 4, full:full + P], k.ps[0:NCP, 4 + at % 2, full:full + P], ACT.Copy)
                        last.then_inc(copied, 1)
                place(i, QT - 1)

        @block.gpsimd
        def _(pool):
            pool.wait_ge(gates_on, 1)
            pool.tensor_copy(zs[:, :, :], z[:, :, SEQ:T])
            with pool.Fori(0, R) as i:
                for u, (t, g) in enumerate(units):
                    pool.wait_ge(probs_c, i * UN + u + 1)
                    pool.tensor_tensor(lc[:, u % SLOTS, :], lc[:, u % SLOTS, :], c["block_mask"][:, 16 - 2 * t:32 - 2 * t], ALU.mult).then_inc(exped, 1)


def sample_attention(k, zs, comp_k, comp_v, mix):
    nc, c = k.nc, k.cst
    WIN = WINDOW + L
    KEYS = PAST + L
    KCH = PAGES + 1
    groups = [list(range(a, min(a + 4, KCH))) for a in range(0, KCH, 4)]
    with ExitStack() as ctx:
        kv = k.sb(ctx, "past_rows", [P, 2, PAGES, 2 * P])
        wk = k.sb(ctx, "window_keys", [P, 2, WINDOW])
        wv = k.sb(ctx, "window_values", [P, 2, 4, P])
        qd = k.sb(ctx, "block_diagonal_queries", [P, ROWS])
        new = k.sb(ctx, "new_rows", [P, 4, L])
        newv = k.sb(ctx, "new_values", [L, 2, P])
        ls = k.sb(ctx, "row_logits", [ROWS, KEYS])
        lw = k.sb(ctx, "row_window_logits", [ROWS, WIN])
        lc = k.sb(ctx, "row_block_logits", [ROWS, NCS])
        mx = k.sb(ctx, "row_maxima", [ROWS, 16])
        mm = k.sb(ctx, "row_max", [ROWS, 4])
        nm = k.sb(ctx, "row_neg_max", [ROWS, 4])
        sums = k.sb(ctx, "row_sums", [ROWS, 4])
        rs = k.sb(ctx, "row_rsums", [ROWS, 4])
        co = k.sb(ctx, "row_coef", [ROWS, 4])
        imp = k.sb(ctx, "importance", [G * L, 4, NBS])
        top = k.sb(ctx, "top8", [G * L, 2, 8])
        neg = k.sb(ctx, "unselected", [G * L, NBS])
        negr = k.sb(ctx, "row_unselected", [ROWS, NBS])
        pt = k.sb(ctx, "row_probs_turned", [P, 4, 4, ROWS])
        gd = k.sb(ctx, "gate_diagonals", [P, H, L])
        os_ = k.sb(ctx, "row_out", [ROWS, P])
        s_kv = [k.sem(ctx, f"past_loaded{s}") for s in range(2)]
        s_new = k.sem(ctx, "new_rows_copied")
        s_newt = k.sem(ctx, "new_values_turned")
        s_newv = k.sem(ctx, "new_values_copied")
        s_cs = k.sem(ctx, "block_scores")
        s_cb = k.sem(ctx, "block_logits")
        s_ce = k.sem(ctx, "block_probs")
        s_cn = k.sem(ctx, "block_probs_normed")
        s_imp = k.sem(ctx, "importance_summed")
        s_sel = k.sem(ctx, "blocks_selected")
        s_neg = k.sem(ctx, "mask_spread")
        s_negc = k.sem(ctx, "mask_copied")
        s_ks = k.sem(ctx, "key_scores")
        s_kb = k.sem(ctx, "key_logits")
        s_wb = k.sem(ctx, "window_logits")
        s_we = k.sem(ctx, "window_probs")
        s_lm = k.sem(ctx, "logit_max")
        s_e = k.sem(ctx, "key_probs")
        s_t = k.sem(ctx, "turned")
        s_tc = [k.sem(ctx, f"turned_copied{x}") for x in range(2)]
        s_o = k.sem(ctx, "outputs_summed")
        s_os = k.sem(ctx, "outputs_combined")
        s_ot = k.sem(ctx, "outputs_turned")
        s_mix = k.sem(ctx, "outputs_placed")
        block = ctx.enter_context(nc.Block())

        turn_list = [[("w", a * P, P, KCH + 1 + a) for a in range(4)],
                     [("w", 4 * P, L, KCH + 5), ("c", 0, NCS, KCH)]]
        turn_list += [[("s", a * P, P if a < PAGES else L, a) for a in g] for g in groups]
        if len(turn_list) % 2:
            turn_list[2:4] = [turn_list[2][:2], turn_list[2][2:], turn_list[3]]
        NTURN = len(turn_list)
        assert NTURN % 2 == 0
        OC, OS, OW = (k.ps[0:ROWS, 7, x * P:(x + 1) * P] for x in range(3))
        NKS = 9

        def tokens(b):
            return bass.ds(b * L + SEQ, L)

        @block.sync
        def _(sp):
            def load(b, j, s):
                wait_apart(k, sp, s_o, b + 1)
                sp.dma_start(wk[:, s, :], k.ins["win_k"][b]).then_inc(s_kv[s], 16)
                sp.dma_start(wv[:, s, :, :], k.ins["win_v"][b].rearrange("(a p) n -> p a n", p=P)).then_inc(s_kv[s], 16)
                load_pages(k, sp, b, k.ins["kv_pages"], kv[:, s, :, :], s_kv[s])
            pairs(sp, B, load)

        @block.tensor
        def _(pe):
            ident = c["ident"]
            pe.sem_inc(s_o, 2)

            def sample(b, j, slot):
                pe.wait_ge(s_new, b + 1)
                pe.transpose(k.ps[0:L, 2, 0:P], new[:, 2, :], ident[:, :])
                pe.transpose(k.ps[0:L, 2, P:2 * P], new[:, 3, :], ident[:, :]).then_inc(s_newt, 1)
                pe.matmul(k.ps[0:ROWS, 3, 0:NCS], qd[:, :], comp_k[:, b, :], start=True, stop=True)
                pe.matmul(k.ps[0:ROWS, 3, 256:260], gd[:, :, :].rearrange("p h q -> p (h q)"), c["branch"][:, :], start=True, stop=True)
                pe.wait_ge(s_kv[slot], (j + 1) * (16 * (PAGES + 2)))
                pe.matmul(k.ps[0:ROWS, 6, 0:WINDOW], qd[:, :], wk[:, slot, :], start=True, stop=True)
                pe.matmul(k.ps[0:ROWS, 3, 128:128 + L], qd[:, :], new[:, 1, :], start=True, stop=True).then_inc(s_cs, 1)
                pe.wait_ge(s_cn, b + 1)
                pe.matmul(k.ps[0:G * L, 2, 256:256 + NCS], c["sum_heads"][:, :], lc[:, :], start=True, stop=True).then_inc(s_imp, 1)
                pe.wait_ge(s_sel, b + 1)
                pe.matmul(k.ps[0:ROWS, 2, 384:384 + NBS], c["spread_heads"][:, :], neg[:, :], start=True, stop=True).then_inc(s_neg, 1)
                for n in range(NKS):
                    pe.wait_ge(s_kb, b * NKS + (n + 1))
                    if n < NKS - 1:
                        last = pe.matmul(k.ps[0:ROWS, n % 2, :], qd[:, :], kv[:, slot, 4 * n:4 * n + 4, 0:P], start=True, stop=True)
                    else:
                        last = pe.matmul(k.ps[0:ROWS, n % 2, 0:L], qd[:, :], new[:, 0, :], start=True, stop=True)
                    last.then_inc(s_ks, 1)
                pe.wait_ge(s_os, b + 1)
                for n in range(NTURN + 1):
                    if n < NTURN:
                        if n == 0:
                            pe.wait_ge(s_we, b + 1)
                        if n == 2:
                            pe.wait_ge(s_e, b + 1)
                        pe.wait_ge(s_tc[n % 2], b * (NTURN // 2) + (n // 2 + 1))
                        for s, (what, col, w, tile) in enumerate(turn_list[n]):
                            src = {"s": ls, "w": lw, "c": lc}[what]
                            last = pe.transpose(k.ps[0:w, 4 + n % 2, s * ROWS:(s + 1) * ROWS], src[:, col:col + w], ident[0:ROWS, 0:ROWS])
                        last.then_inc(s_t, 1)
                    if n >= 1:
                        pe.wait_ge(s_tc[(n - 1) % 2], b * (NTURN // 2) + ((n - 1) // 2 + 2))
                        if n == 1:
                            pe.wait_ge(s_newv, b + 1)
                        for s, (what, col, w, tile) in enumerate(turn_list[n - 1]):
                            if what == "c":
                                o, mv, st, sp_ = OC, comp_v[:, b, :], True, True
                            elif what == "w":
                                a = tile - KCH - 1
                                o, st, sp_ = OW, a == 0, a == 4
                                mv = wv[:, slot, a, :] if a < 4 else newv[:, 1, :]
                            else:
                                o, st, sp_ = OS, tile == 0, tile == PAGES
                                mv = kv[:, slot, tile, P:2 * P] if tile < PAGES else newv[:, 0, :]
                            last = pe.matmul(o, pt[0:w, (n - 1) % 4, s, :], mv, start=st, stop=sp_)
                last.then_inc(s_o, 1)
                pe.wait_ge(s_os, b + 2)
                pe.wait_ge(s_mix, b + 1)
                pe.transpose(k.ps[:, 3, 384:384 + ROWS], os_[:, :], ident[0:ROWS, 0:ROWS]).then_inc(s_ot, 1)
            pairs(pe, B, sample)

        def copies(eng, b, parity):
            for n in range(parity, NTURN, 2):
                eng.wait_ge(s_t, b * NTURN + (n + 1))
                group = turn_list[n]
                runs = []
                for s, (what, col, w, tile) in enumerate(group):
                    if runs and runs[-1][2] == w and runs[-1][1] + runs[-1][3] == tile:
                        runs[-1][3] += 1
                    else:
                        runs.append([s, tile, w, 1])
                for s, tile, w, count in runs:
                    dst = pt[0:w, n % 4, s:s + count, :]
                    src = k.ps[0:w, 4 + n % 2, s * ROWS:(s + count) * ROWS].rearrange("p (a n) -> p a n", a=count)
                    if eng is k.nc.scalar:
                        last = eng.activation(dst, src, ACT.Copy)
                    else:
                        last = eng.tensor_copy(dst, src)
                last.then_inc(s_tc[n % 2], 1)

        @block.scalar
        def _(act):
            act.sem_inc(s_tc[1], 1)
            with act.Fori(0, B) as b:
                act.wait_ge(s_cb, b + 1)
                act.activation(lc[:, :], lc[:, :], ACT.Exp, bias=nm[:, 0:1], accum_out=sums[:, 0:1]).then_inc(s_ce, 1)
                act.wait_ge(s_wb, b + 1)
                act.activation(lw[:, :], lw[:, :], ACT.Exp, bias=nm[:, 2:3], accum_out=sums[:, 2:3]).then_inc(s_we, 1)
                act.wait_ge(s_lm, b + 1)
                act.activation(ls[:, :], ls[:, :], ACT.Exp, bias=nm[:, 1:2], accum_out=sums[:, 1:2]).then_inc(s_e, 1)
                copies(act, b, 1)

        @block.vector
        def _(dve):
            dve.sem_inc(s_tc[0], 1)
            dve.sem_inc(s_kb, 2)
            dve.sem_inc(s_os, 1)
            dve.sem_inc(s_mix, 1)
            dve.memset(qd[:], 0.0)
            dve.memset(imp[:], FORCED)
            dve.drain()
            with dve.Fori(0, B) as b:
                for g in range(G):
                    rows = slice(g * HD, (g + 1) * HD)
                    dve.tensor_copy(qd[rows, g * GR:(g + 1) * GR].rearrange("p (r q) -> p r q", r=R), zs[rows, 0:R, bass.ds(b * L, L)])
                for n, ch in enumerate((Z_KS, Z_KW, Z_VS, Z_VW)):
                    dve.tensor_copy(new[:, n, :], zs[:, ch, bass.ds(b * L, L)])
                dve.tensor_tensor(gd[:, :, :], c["diag"][:, :].rearrange("p (h o) -> p h o", o=1).broadcast_to([P, H, L]),
                                  zs[:, bass.ds(Z_GATE, 1), bass.ds(b * L, L)].broadcast_to([P, H, L]), ALU.mult)
                dve.drain().then_inc(s_new, 1)
                dve.wait_ge(s_newt, b + 1)
                dve.tensor_copy(newv[:, :, :], k.ps[0:L, 2, 0:2 * P].rearrange("p (a n) -> p a n", a=2)).then_inc(s_newv, 1)
                wait_apart(k, dve, s_cs, b + 1)
                dve.tensor_tensor_reduce(lc[:, :], k.ps[0:ROWS, 3, 0:NCS], k.row_blocks[:, :], 1.0, LOWEST, ALU.add, ALU.max, mm[:, 0:1])
                dve.drain()
                dve.tensor_scalar(nm[:, 0:1], mm[:, 0:1], -1.0, None, ALU.mult).then_inc(s_cb, 1)
                dve.tensor_tensor_reduce(lw[:, 0:WINDOW], k.ps[0:ROWS, 6, 0:WINDOW], k.row_window[:, 0:WINDOW], 1.0, LOWEST, ALU.add, ALU.max, mx[:, 12:13])
                dve.tensor_tensor_reduce(lw[:, WINDOW:WIN], k.ps[0:ROWS, 3, 128:128 + L], k.row_window[:, WINDOW:WIN], 1.0, LOWEST, ALU.add, ALU.max, mx[:, 13:14])
                dve.tensor_copy(co[:, 0:3], k.ps[0:ROWS, 3, 256:259])
                dve.drain()
                dve.tensor_tensor(mm[:, 2:3], mx[:, 12:13], mx[:, 13:14], ALU.max)
                dve.drain()
                dve.tensor_scalar(nm[:, 2:3], mm[:, 2:3], -1.0, None, ALU.mult).then_inc(s_wb, 1)
                dve.wait_ge(s_ce, b + 1)
                dve.reciprocal(rs[:, 0:1], sums[:, 0:1])
                dve.drain()
                dve.tensor_scalar(lc[:, :], lc[:, :], rs[:, 0:1], None, ALU.mult).then_inc(s_cn, 1)
                dve.wait_ge(s_imp, b + 1)
                dve.tensor_copy(imp[:, 0, 1:NCS - 1], k.ps[0:G * L, 2, 257:256 + NCS - 1])
                dve.drain()
                for step in range(2):
                    dve.max(top[:, step, :], imp[:, step, :])
                    dve.drain()
                    dve.match_replace(imp[:, step + 1, :], top[:, step, :], imp[:, step, :], -5.0)
                    dve.drain()
                dve.tensor_scalar(neg[:, :], imp[:, 2, :], -1.0, NEG, ALU.is_ge, ALU.mult).then_inc(s_sel, 1)
                dve.wait_ge(s_neg, b + 1)
                dve.tensor_tensor(negr[:, :], k.ps[0:ROWS, 2, 384:384 + NBS], k.row_select[:, :], ALU.add)
                dve.drain()
                for n in range(NKS):
                    wait_apart(k, dve, s_ks, b * NKS + (n + 1))
                    if n < NKS - 2:
                        dve.tensor_tensor_reduce(ls[:, n * 512:(n + 1) * 512].rearrange("p (a n) -> p a n", n=CB),
                                                 k.ps[0:ROWS, n % 2, :].rearrange("p (a n) -> p a n", n=CB),
                                                 negr[:, 8 * n:8 * n + 8].rearrange("p (a o) -> p a o", o=1).broadcast_to([ROWS, 8, CB]),
                                                 1.0, LOWEST, ALU.add, ALU.max, mx[:, n:n + 1]).then_inc(s_kb, 1)
                    elif n == NKS - 2:
                        dve.tensor_tensor(ls[:, n * 512:(n + 1) * 512].rearrange("p (a n) -> p a n", n=CB),
                                          k.ps[0:ROWS, n % 2, :].rearrange("p (a n) -> p a n", n=CB),
                                          negr[:, 8 * n:8 * n + 8].rearrange("p (a o) -> p a o", o=1).broadcast_to([ROWS, 8, CB]),
                                          ALU.add).then_inc(s_kb, 1)
                    else:
                        dve.tensor_scalar(ls[:, PAST:KEYS], k.ps[0:ROWS, n % 2, 0:L], negr[:, NCS:NBS], None, ALU.add).then_inc(s_kb, 1)
                dve.drain()
                dve.tensor_tensor(ls[:, KEYS - TAIL:KEYS], ls[:, KEYS - TAIL:KEYS], k.row_tail[:, :], ALU.add)
                dve.drain()
                dve.tensor_reduce(mx[:, 7:8], ls[:, (NKS - 2) * 512:KEYS], X, ALU.max)
                dve.drain()
                dve.tensor_reduce(mm[:, 1:2], mx[:, 0:8], X, ALU.max)
                dve.drain()
                dve.tensor_scalar(nm[:, 1:2], mm[:, 1:2], -1.0, None, ALU.mult).then_inc(s_lm, 1)
                copies(dve, b, 0)
                dve.wait_ge(s_e, b + 1)
                dve.wait_ge(s_o, b + 3)
                dve.reciprocal(rs[:, 1:3], sums[:, 1:3])
                dve.drain()
                dve.tensor_tensor(co[:, 1:3], co[:, 1:3], rs[:, 1:3], ALU.mult)
                dve.drain()
                dve.tensor_scalar(os_[:, :], OC, co[:, 0:1], None, ALU.mult)
                dve.drain()
                dve.scalar_tensor_tensor(out=os_[:, :], in0=OS, scalar=co[:, 1:2], in1=os_[:, :], op0=ALU.mult, op1=ALU.add)
                dve.drain()
                dve.scalar_tensor_tensor(out=os_[:, :], in0=OW, scalar=co[:, 2:3], in1=os_[:, :], op0=ALU.mult, op1=ALU.add).then_inc(s_os, 1)
                dve.wait_ge(s_ot, b + 1)
                for g in range(G):
                    rows = slice(g * HD, (g + 1) * HD)
                    last = dve.tensor_copy(mix[rows, 0:R, tokens(b)],
                                           k.ps[rows, 3, 384 + g * GR:384 + (g + 1) * GR].rearrange("p (r q) -> p r q", r=R))
                last.then_inc(s_mix, 1)


def memory_attention(k, layer, xq, mix_out):
    nc, c = k.nc, k.cst
    NB4 = 4
    STEPS = QT + B // NB4
    with ExitStack() as ctx:
        keys = k.sb(ctx, "sample_mem_keys", [P, B, 2, NMEM])
        vals = k.sb(ctx, "sample_mem_values", [P, B, 2, 2 * P])
        qd = k.sb(ctx, "mem_queries_diagonal", [P, 2, B, XH, L])
        pr = k.sb(ctx, "mem_probs", [P, 2, XH * NMEM])
        mx = k.sb(ctx, "mem_maxima", [P, 2, XH])
        sums = k.sb(ctx, "mem_sums", [P, 2, XH])
        rs = k.sb(ctx, "mem_rsums", [P, 2, XH])
        pt = k.sb(ctx, "mem_probs_turned", [P, 2, 512])
        o = k.sb(ctx, "mem_out", [P, 2 * P])
        loaded = k.sem(ctx, "mem_rows_loaded")
        placed = k.sem(ctx, "mem_queries_placed")
        scored = k.sem(ctx, "mem_scored")
        maxed = k.sem(ctx, "mem_maxed")
        exped = k.sem(ctx, "mem_exped")
        turned = k.sem(ctx, "mem_turned")
        copied = k.sem(ctx, "mem_copied")
        valued = k.sem(ctx, "mem_valued")
        normed = k.sem(ctx, "mem_normed")
        back = k.sem(ctx, "mem_turned_back")
        stored = k.sem(ctx, "mem_mixed")
        block = ctx.enter_context(nc.Block())

        @block.sync
        def _(sp):
            sp.dma_start(keys[:], k.ins["cmem_k"][layer].rearrange("b p n -> p b n").rearrange("p b (c n) -> p b c n", c=2)).then_inc(loaded, 16)
            sp.dma_start(vals[:], k.ins["cmem_v"][layer].rearrange("b p n -> p b n").rearrange("p b (c n) -> p b c n", c=2)).then_inc(loaded, 16)

        def score_view(n):
            return k.ps[:, 2 * (n % 2):2 * (n % 2) + 2, :].rearrange("p b n -> p (b n)")

        def head_at(y):
            return 2 * (y % 2) + y // 2

        def n_turn(n):
            return 2 if n < QT else 1

        turn_before = [0]
        for n in range(STEPS):
            turn_before.append(turn_before[-1] + n_turn(n))

        @block.tensor
        def _(pe):
            pe.wait_ge(placed, 1)
            pe.wait_ge(loaded, 32)

            def score(n):
                if n >= 2:
                    pe.wait_ge(exped, n - 1)
                sv = score_view(n)
                if n < QT:
                    for y in range(XH):
                        h = head_at(y)
                        rows = slice((h % 2) * HD, (h % 2 + 1) * HD)
                        last = pe.matmul(sv[:, y * NMEM:(y + 1) * NMEM], xq[rows, h // 2, n * P:(n + 1) * P],
                                         k.mem_k[rows, layer, h // 2, :], start=True, stop=True)
                else:
                    for x in range(NB4):
                        b = (n - QT) * NB4 + x
                        for ch in range(2):
                            last = pe.matmul(sv[32 * x:32 * x + 32, 0:NMEM], qd[:, ch, b, :, :].rearrange("p h q -> p (h q)"),
                                             keys[:, b, ch, :], start=ch == 0, stop=ch == 1)
                last.then_inc(scored, 1)
            score(0)
            for n in range(STEPS):
                if n + 1 < STEPS:
                    score(n + 1)
                pe.wait_ge(exped, n + 1)
                for x in range(n_turn(n)):
                    at = turn_before[n] + x
                    if at >= 1:
                        pe.wait_ge(copied, at)
                    cols = 4 if n < QT else 2
                    for y in range(cols):
                        last = pe.transpose(k.ps[:, 4, y * P:(y + 1) * P], pr[:, n % 2, (4 * x + y) * P:(4 * x + y + 1) * P], c["ident"][:, :])
                    last.then_inc(turned, 1)
                    pe.wait_ge(copied, at + 1)
                    if x == 0 and n >= 1:
                        pe.wait_ge(normed, n)
                    if n < QT:
                        for hh in range(2):
                            h = head_at(2 * x + hh)
                            for mt in range(2):
                                last = pe.matmul(k.ps[:, 5, h * HD:(h + 1) * HD], pt[:, at % 2, (2 * hh + mt) * P:(2 * hh + mt + 1) * P],
                                                 k.mem_v[:, layer, mt, h * HD:(h + 1) * HD], start=mt == 0, stop=mt == 1)
                    else:
                        for xx in range(NB4):
                            b = (n - QT) * NB4 + xx
                            for mt in range(2):
                                last = pe.matmul(k.ps[32 * xx:32 * xx + 32, 5, 0:2 * P], pt[:, at % 2, mt * P + 32 * xx:mt * P + 32 * xx + 32],
                                                 vals[:, b, mt, :], start=mt == 0, stop=mt == 1)
                last.then_inc(valued, 1)
                pe.wait_ge(normed, n + 1)
                if n >= 1:
                    pe.wait_ge(stored, n)
                for ch in range(2):
                    last = pe.transpose(k.ps[:, 6, ch * P:(ch + 1) * P], o[:, ch * P:(ch + 1) * P], c["ident"][:, :])
                last.then_inc(back, 1)

        @block.vector
        def _(dve):
            dve.memset(qd[:], 0.0)
            dve.drain()
            for h in range(XH):
                rows = slice((h % 2) * HD, (h % 2 + 1) * HD)
                dve.tensor_copy(qd[rows, h // 2, :, h, :], samples(xq[rows, h // 2, :]))
            dve.drain().then_inc(placed, 1)

            def maximum(n):
                dve.wait_ge(scored, n + 1)
                heads = XH if n < QT else 1
                if n >= 2:
                    dve.wait_ge(exped, n - 1)
                dve.tensor_reduce(mx[:, n % 2, 0:heads], score_view(n)[:, 0:heads * NMEM].rearrange("p (h n) -> p h n", h=heads), X, ALU.max)
                dve.drain()
                dve.tensor_scalar(mx[:, n % 2, 0:heads], mx[:, n % 2, 0:heads], -1.0, None, ALU.mult).then_inc(maxed, 1)
            maximum(0)
            for n in range(STEPS):
                heads = XH if n < QT else 1
                if n + 1 < STEPS:
                    maximum(n + 1)
                dve.wait_ge(exped, n + 1)
                dve.reciprocal(rs[:, n % 2, 0:heads], sums[:, n % 2, 0:heads])
                for x in range(n_turn(n)):
                    at = turn_before[n] + x
                    w = 512 if n < QT else 256
                    dve.wait_ge(turned, at + 1)
                    dve.tensor_copy(pt[:, at % 2, 0:w], k.ps[:, 4, 0:w]).then_inc(copied, 1)
                dve.drain()
                dve.wait_ge(valued, n + 1)
                if n >= 1:
                    dve.wait_ge(back, n)
                if n < QT:
                    dve.tensor_tensor(o[:, :].rearrange("p (a b d) -> p a b d", a=2, b=2), k.ps[:, 5, 0:2 * P].rearrange("p (a b d) -> p a b d", a=2, b=2),
                                      rs[:, n % 2, :].rearrange("p (b a o) -> p a b o", a=2, o=1).broadcast_to([P, 2, 2, HD]), ALU.mult).then_inc(normed, 1)
                else:
                    dve.tensor_scalar(o[:, :], k.ps[:, 5, 0:2 * P], rs[:, n % 2, 0:1], None, ALU.mult).then_inc(normed, 1)

        @block.scalar
        def _(act):
            def place(n):
                act.wait_ge(back, n + 1)
                if n < QT:
                    last = act.activation(mix_out[:, :, n * P:(n + 1) * P], k.ps[:, 6, 0:2 * P].rearrange("p (c n) -> p c n", c=2), ACT.Copy)
                else:
                    for h in range(XH):
                        rows = slice((h % 2) * HD, (h % 2 + 1) * HD)
                        src = k.ps[rows, 6, (h // 2) * P:(h // 2 + 1) * P].rearrange("p (b h q) -> p b h q", b=NB4, h=XH)[:, :, h, :]
                        b0 = (n - QT) * NB4
                        last = act.activation(samples(mix_out[rows, h // 2, :])[:, b0:b0 + NB4, :], src, ACT.Copy)
                last.then_inc(stored, 1)

            for n in range(STEPS):
                heads = XH if n < QT else 1
                act.wait_ge(maxed, n + 1)
                if n >= 2:
                    act.wait_ge(normed, n - 1)
                for h in range(heads):
                    last = act.activation(pr[:, n % 2, h * NMEM:(h + 1) * NMEM], score_view(n)[:, h * NMEM:(h + 1) * NMEM],
                                          ACT.Exp, bias=mx[:, n % 2, h:h + 1], accum_out=sums[:, n % 2, h:h + 1])
                last.then_inc(exped, 1)
                if n >= 1:
                    place(n - 1)
            place(STEPS - 1)


def pool_mixer(k, z, mix):
    nc, c = k.nc, k.cst
    EP, ES = PST + SEQ, PST + L
    W = EP + B * ES
    with ExitStack() as ctx:
        load_constants(k, ctx, POOLING)
        ext = k.sb(ctx, "pool_ext", [PCH, 2, W])
        sa = k.sb(ctx, "pool_sums_a", [PCH, W])
        sb_ = k.sb(ctx, "pool_sums_b", [PCH, W])
        state = k.sb(ctx, "pool_state", [PCH, NPC, B * PST])
        pooled = k.sb(ctx, "pooled", [PCH, NPC, T])
        tails = k.sb(ctx, "pool_tails", [PCH, NPC, PST * (1 + B)])
        w = k.sb(ctx, "pool_weights", [PCH, NPC, PG])
        loaded = k.sem(ctx, "pool_loaded")
        done = k.sem(ctx, "pooled_ready")
        multiplied = k.sem(ctx, "pool_multiplied")
        scaled = k.sem(ctx, "pool_scaled")
        stored = k.sem(ctx, "pool_stored")
        block = ctx.enter_context(nc.Block())

        @block.sync
        def _(sp):
            sp.dma_start(state[:], k.ins["pool_state"]).then_inc(loaded, 16)
            sp.dma_start(w[:], k.ins["w_grp"]).then_inc(loaded, 16)
            sp.wait_ge(done, NPC)
            sp.dma_start(k.outs["pool"], tails[:]).then_inc(stored, 16)
            sp.wait_ge(stored, 16)

        def parts(buf, lo):
            s = buf[:, EP:W].rearrange("p (b n) -> p b n", b=B)
            return buf[:, lo:EP], s[:, :, lo:ES]

        @block.vector
        def _(dve):
            dve.wait_ge(loaded, 32)
            for ch in range(NPC):
                e = ext[:, ch % 2, :]
                pw = POOLW[ch // 2]
                ep, es = parts(e, 0)
                dve.memset(ep[:, 0:PST], 0.0)
                dve.tensor_copy(ep[:, PST:EP], z[0:PCH, ch, 0:SEQ])
                dve.tensor_copy(es[:, :, 0:PST], state[:, ch, :].rearrange("p (b n) -> p b n", b=B))
                dve.tensor_copy(es[:, :, PST:ES], samples(z[0:PCH, ch, :]))
                dve.drain()
                dve.tensor_copy(tails[:, ch, 0:PST], ep[:, SEQ:EP])
                dve.tensor_copy(tails[:, ch, PST:].rearrange("p (b n) -> p b n", b=B), es[:, :, L:ES])
                cur, span = e, 1
                while span < pw:
                    nxt = sa if cur is not sa else sb_
                    nxt_ap = nxt[:, :]
                    lo = 2 * span - 1
                    cp, cs = parts(cur if cur is e else cur[:, :], 0)
                    np_, ns = parts(nxt_ap, 0)
                    dve.tensor_tensor(np_[:, lo:EP], cp[:, lo:EP], cp[:, lo - span:EP - span], ALU.add)
                    dve.tensor_tensor(ns[:, :, lo:ES], cs[:, :, lo:ES], cs[:, :, lo - span:ES - span], ALU.add)
                    dve.drain()
                    cur, span = nxt, 2 * span
                cp, cs = parts(cur[:, :], 0)
                dve.tensor_tensor(cp[:, PST:PST + 16], cp[:, PST:PST + 16], c["pool_counts"][0:PCH, ch // 2, :], ALU.mult)
                dve.drain()
                dve.scalar_tensor_tensor(out=pooled[:, ch, 0:SEQ], in0=cp[:, PST:EP], scalar=1.0 / pw, in1=ep[:, PST:EP],
                                         op0=ALU.mult, op1=ALU.subtract)
                dve.scalar_tensor_tensor(out=samples(pooled[:, ch, :]), in0=cs[:, :, PST:ES], scalar=1.0 / pw, in1=es[:, :, PST:ES],
                                         op0=ALU.mult, op1=ALU.subtract)
                dve.drain().then_inc(done, 1)

        @block.tensor
        def _(pe):
            for m in range(NPC):
                g = m // 2
                pe.wait_ge(done, 2 * g + 2)
                if m >= 2:
                    pe.wait_ge(scaled, m - 1)
                for a, cols in NT:
                    for kk in range(2):
                        last = pe.matmul(bank_set(k, m % 2)[0:PCH, a:a + cols], w[:, 2 * g + kk, (m % 2) * PCH:(m % 2 + 1) * PCH],
                                         pooled[:, 2 * g + kk, a:a + cols], start=kk == 0, stop=kk == 1)
                last.then_inc(multiplied, 1)

        @block.scalar
        def _(act):
            for m in range(NPC):
                act.wait_ge(multiplied, m + 1)
                act.activation(mix[0:PCH, m, :], bank_set(k, m % 2)[0:PCH, :], ACT.Copy, scale=c["pool_scale"][0:PCH, m:m + 1]).then_inc(scaled, 1)


def conv_ffn(k, layer, xn, x):
    nc, c = k.nc, k.cst
    EP, ES = SEQ + 2, L + 2
    W = EP + B * ES
    most = max(PARTS)
    starts = [sum(PARTS[:p]) for p in range(len(PARTS))]

    def up_base(p):
        return 2 * starts[p] + p * KC

    def down_base(p):
        return 2 * starts[p] + 2 * PARTS[p] + p * KC + (2 if p + 1 < len(PARTS) else 0)

    with ExitStack() as ctx:
        load_constants(k, ctx, CONVOLUTION)
        gh = k.sb(ctx, "gated_high", [P, most, T], F32R)
        gl = k.sb(ctx, "gated_low", [P, most, T], F32R)
        tails = k.sb(ctx, "conv_tails", [P, 2 * FC, 2 * (1 + B)])
        ext = k.sb(ctx, "conv_ext", [P, 2, W])
        y = k.sb(ctx, "conv_out", [P, 2, T])
        w = Weights(k, ctx, "ffn", KC * P)
        taken = k.sem(ctx, "banks_taken")
        placed = k.sem(ctx, "products_placed")
        convolved = k.sem(ctx, "convolved")
        silued = k.sem(ctx, "silued")
        gated = k.sem(ctx, "gated")
        rounded = k.sem(ctx, "gated_rounded")
        finished = k.sem(ctx, "gated_split")
        stored = k.sem(ctx, "tails_stored")
        block = ctx.enter_context(nc.Block())
        up = [(xn[0][:, kk, :], xn[1][:, kk, :]) for kk in range(KC)]

        def stream(eng, up_step, down_step):
            for p, n in enumerate(PARTS):
                with eng.Fori(0 if p == 0 else 1, n) as m:
                    up_step(p, m, up_base(p))
                if p + 1 < len(PARTS):
                    up_step(p + 1, 0, up_base(p) + 2 * n)
                with eng.Fori(0, KC // 2) as m:
                    down_step(p, m, n)

        @block.sync
        def _(sp):
            def up_step(p, m, base):
                for av in range(2):
                    w.load(sp, m * 2 + (base + av), av, k.ins["w_up"][layer, m + (starts[p] + av * FC)], KC * P)

            def down_step(p, m, n):
                for s in range(2):
                    w.load(sp, m * 2 + (down_base(p) + s), s,
                           k.ins["w_down"][layer, m * 2 + s, :, starts[p] * P:(starts[p] + n) * P], n * P)
            stream(sp, up_step, down_step)
            sp.wait_ge(finished, FC + 1)
            sp.dma_start(k.outs["conv"][layer], tails[:]).then_inc(stored, 16)
            sp.wait_ge(stored, 16)

        @block.gpsimd
        def _(pool):
            pool.sem_inc(w.split, 2)

            def up_step(p, m, base):
                for av in range(2):
                    w.part(k, pool, m * 2 + (base + av), m + base // 2, av, KC * P)

            def down_step(p, m, n):
                for s in range(2):
                    w.part(k, pool, m * 2 + (down_base(p) + s), m + down_base(p) // 2, s, n * P)
            stream(pool, up_step, down_step)

        @block.tensor
        def _(pe):
            pe.sem_inc(w.multiplied, 2)

            def up_step(p, m, base):
                for av in range(2):
                    t = m * 2 + (base + av)
                    pe.wait_ge(taken, t + 1)
                    w.multiply(pe, t, av, [(P, h, l) for h, l in up], bank_set(k, av))

            def down_step(p, m, n):
                pe.wait_ge(finished, starts[p] + n + 1)
                for s in range(2):
                    t = m * 2 + (down_base(p) + s)
                    pe.wait_ge(taken, t + 1)
                    w.multiply(pe, t, s, [(P, gh[:, i, :], gl[:, i, :]) for i in range(n)], bank_set(k, s))
            stream(pe, up_step, down_step)

        def ext_parts(av):
            return ext[:, av, 0:EP], ext[:, av, EP:W].rearrange("p (b n) -> p b n", b=B)

        @block.scalar
        def _(act):
            def up_step(p, m, base):
                for av in range(2):
                    act.wait_ge(w.multiplied, m * 2 + (base + av + 3))
                    ep, es = ext_parts(av)
                    bs = bank_set(k, av)
                    ch = m + (starts[p] + av * FC)
                    act.wait_ge(finished, m + (starts[p] + 1))
                    act.activation(y[:, av, :], bs, ACT.Identity, bias=c["conv_b"][:, layer, bass.ds(ch, 1)],
                                   scale=c["conv_w"][:, layer, 2, bass.ds(ch, 1)])
                    act.activation(ep[:, 2:EP], bs[:, 0:SEQ], ACT.Copy)
                    act.activation(es[:, :, 2:ES], samples(bs), ACT.Copy).then_inc(placed, 1)
                act.wait_ge(convolved, m + (starts[p] + 1))
                act.activation(y[:, 0, :], y[:, 0, :], ACT.Silu).then_inc(silued, 1)
                act.wait_ge(gated, m + (starts[p] + 1))
                if p and isinstance(m, int):
                    act.wait_ge(w.multiplied, down_base(p - 1) + KC + 2)
                act.activation(gh[:, bass.ds(m, 1), :].rearrange("p a n -> p (a n)"), y[:, 1, :], ACT.Copy).then_inc(rounded, 1)
            stream(act, up_step, lambda p, m, n: None)

        @block.vector
        def _(dve):
            dve.sem_inc(taken, 2)
            dve.sem_inc(finished, 1)
            dve.memset(ext[:, :, 0:2], 0.0)

            def convolve(p, m, base):
                for av in range(2):
                    ep, es = ext_parts(av)
                    ch = m + (starts[p] + av * FC)
                    dve.tensor_copy(es[:, :, 0:2], c["conv_state"][:, layer, bass.ds(ch, 1), :].rearrange("p a (b n) -> p (a b) n", b=B))
                    wait_apart(k, dve, placed, m * 2 + (2 * starts[p] + av + 1))
                    dve.drain().then_inc(taken, 1)
                    tail = tails[:, bass.ds(ch, 1), :].rearrange("p a n -> p (a n)")
                    dve.tensor_copy(tail[:, 0:2], ep[:, SEQ:EP])
                    dve.tensor_copy(tail[:, 2:].rearrange("p (b n) -> p b n", b=B), es[:, :, L:ES])
                    for tap in (1, 0):
                        wt = c["conv_w"][:, layer, tap, bass.ds(ch, 1)]
                        dve.scalar_tensor_tensor(out=y[:, av, 0:SEQ], in0=ep[:, tap:tap + SEQ], scalar=wt, in1=y[:, av, 0:SEQ],
                                                 op0=ALU.mult, op1=ALU.add)
                        dve.scalar_tensor_tensor(out=samples(y[:, av, :]), in0=es[:, :, tap:tap + L], scalar=wt, in1=samples(y[:, av, :]),
                                                 op0=ALU.mult, op1=ALU.add)
                        last = dve.drain()
                    if av == 0:
                        last.then_inc(convolved, 1)
                dve.wait_ge(silued, m + (starts[p] + 1))
                dve.tensor_tensor(y[:, 1, :], y[:, 0, :], y[:, 1, :], ALU.mult).then_inc(gated, 1)

            def finish(p, m):
                dve.wait_ge(rounded, m + (starts[p] + 1))
                low = gl[:, bass.ds(m, 1), :].rearrange("p a n -> p (a n)")
                high = gh[:, bass.ds(m, 1), :].bitcast(F32).rearrange("p a n -> p (a n)")
                dve.tensor_tensor(low, y[:, 1, :], high, ALU.subtract).then_inc(finished, 1)

            for p, n in enumerate(PARTS):
                with dve.Fori(0 if p == 0 else 1, n) as m:
                    convolve(p, m, None)
                    finish(p, m)
                if p + 1 < len(PARTS):
                    convolve(p + 1, 0, None)
                with dve.Fori(0, KC // 2) as m:
                    for s in range(2):
                        dve.wait_ge(w.multiplied, m * 2 + (down_base(p) + s + 3))
                        xm = x[:, m * 2 + s, :]
                        dve.tensor_tensor(xm, xm, bank_set(k, s), ALU.add).then_inc(taken, 1)
                dve.drain()
                if p + 1 < len(PARTS):
                    finish(p + 1, 0)


def store(k, pairs_):
    with ExitStack() as ctx:
        stored = k.sem(ctx, "stored")
        block = ctx.enter_context(k.nc.Block())

        @block.sync
        def _(sp):
            for dst, src in pairs_:
                sp.dma_start(dst, src).then_inc(stored, 16)
            sp.wait_ge(stored, 16 * len(pairs_))


CONSTANTS = dict(
    page_table=[1, B * PAGES],
    ident=[P, P], ones=[P, P], halves=[P, P], flip=[P, P], edge_mask=[P, P], block_mask=[P, 32],
    win_mask=[ROWS, L], sum_heads=[ROWS, G * L], spread_heads=[G * L, ROWS], diag=[P, H], branch=[P, 4],
    shift=[P, G, 2, P], norm_bias=[P, WHOLE + 1], norm_scale=[P, WHOLE + 1], onehot=[BUCKETS + 1, RW],
    relx=[BUCKETS + 1, H], gains=[P, NORMED + 2], xk_gain=[P, 2], g_mix=[P, 2, KC], g_mem=[P, 2, KC],
    g_ffn=[P, 2, KC], cmp_pos=[P, 2, L2], cmp_b1=[P, 2], cmp_w2=[P, 2, HD], cmp_b2k=[P, 1], cmp_b2v=[P, P],
    pool_scale=[P, NPC], pool_counts=[P, 4, 16], conv_b=[P, 2, 2 * FC], conv_w=[P, 2, 3, 2 * FC],
    conv_state=[P, 2, 2 * FC, 2 * B],
)


SMALL_INTEGERS = ("page_table",)
TABLES = ["onehot", "relx", "flip"]
COMPRESSION = ["shift", "cmp_pos", "cmp_b1", "cmp_w2", "cmp_b2k", "cmp_b2v"]
ATTENTION = ["edge_mask", "block_mask", "win_mask", "sum_heads", "spread_heads", "diag", "branch"]
POOLING = ["pool_scale", "pool_counts"]
CONVOLUTION = ["conv_b", "conv_w", "conv_state"]
COMMON = [n for n in CONSTANTS if n not in TABLES + COMPRESSION + ATTENTION + POOLING + CONVOLUTION]


def decoder(nc, ins, outs, n_pages):
    with ExitStack() as ctx:
        k = Kernel(nc, ctx, ins, outs)
        k.n_pages = n_pages
        k.ps = ctx.enter_context(nc.psum_tensor("banks", [P, 8, 512], F32))
        k.cst = {}
        k.passed = ctx.enter_context(nc.semaphore("passed"))
        k.row_dram = nc.dram_tensor("bias_row_scratch", [H, RW], F32, kind="Internal").ap()
        x = k.sb(ctx, "x", [P, KC, T])
        k.mem_k = k.sb(ctx, "mem_keys", [P, 2, 2, NMEM])
        k.mem_v = k.sb(ctx, "mem_values", [P, 2, 2, 2 * P])
        load_constants(k, ctx, COMMON)

        def two_parts(octx, name, n):
            return tuple(k.sb(octx, name + x, [P, n, T], F32R) for x in ("_high", "_low"))

        def whole_terms(parts, n):
            return [(P, parts[0][:, kk, :], parts[1][:, kk, :]) for kk in range(n)]

        def add(dve, m, banks):
            return dve.tensor_tensor(x[:, m, :], x[:, m, :], banks, ALU.add)

        def ffn(layer):
            with ExitStack() as f:
                xn = two_parts(f, "ffn_in", KC)
                rms_norm(k, x, xn, k.cst["g_ffn"][:, layer, :], T)
                conv_ffn(k, layer, xn, x)

        with ExitStack() as m:
            mem = k.sb(m, "memory", [P, KC, NMEM])
            memn = k.sb(m, "memory_normed", [P, KC, NMEM])
            load_x(k, mem, ins["mem"])
            for layer in range(2):
                memory_kv(k, layer, mem, memn)
        mix = x
        with ExitStack() as l0:
            comp_k = k.sb(l0, "compressed_keys", [P, B + 1, NCS])
            comp_v = k.sb(l0, "compressed_values", [NCS, B + 1, P])
            zs = k.sb(l0, "z_samples", [P, NZ, TS])
            load_constants(k, l0, ATTENTION)
            k.row_tail = k.sb(l0, "row_tail_bias", [ROWS, TAIL])
            k.row_far = k.sb(l0, "row_far_bias", [ROWS, 2])
            k.row_blocks = k.sb(l0, "row_block_bias", [ROWS, NCS])
            k.row_select = k.sb(l0, "row_select_bias", [ROWS, NBS])
            k.row_window = k.sb(l0, "row_window_bias", [ROWS, WINDOW + L])
            lz = l0.enter_context(ExitStack())
            z = k.sb(lz, "z", [P, NZ, T])
            with ExitStack() as n:
                x0 = z[:, NZ - KC:NZ, :]
                xn = two_parts(n, "in0", KC)
                load_x(k, x0, ins["x"])
                rms_norm(k, x0, xn, k.cst["g_mix"][:, 0, :], T)
                project(k, "w_in0", ins["w_in0"], NZ, whole_terms(xn, KC),
                        lambda dve, m, banks: dve.tensor_copy(z[:, m, :], banks))
            head_norms(k, z, NORMED, 0)
            store(k, [(outs["rows"], z[:, Z_KS:Z_GATE, :]),
                      (outs["win_k"][:, :, 0:WINDOW - L], ins["win_k"][:, :, L:WINDOW]),
                      (outs["win_v"][:, 0:WINDOW - L, :], ins["win_v"][:, L:WINDOW, :])])
            compress(k, z, mix, comp_k, comp_v)
            with ExitStack() as n:
                k.near_bias = k.sb(n, "near_bias", [P, H, 256])
                k.block_bias = k.sb(n, "block_bias", [P, H, 32])
                bias_tables(k)
                vals = k.sb(n, "prompt_values", [P, 2, QT, P])
                token_major_values(k, z, vals)
                prompt_attention(k, z, zs, vals, comp_k, comp_v, mix)
            memory_attention(k, 0, z[:, Z_XQ:Z_XQ + 2, :], mix[:, R:R + 2, :])
            lz.close()
            sample_attention(k, zs, comp_k, comp_v, mix)
        with ExitStack() as n:
            parts = two_parts(n, "mixed0", KC)
            split_tokens(k, mix, parts, [(P, i) for i in range(KC)])
            load_x(k, x, ins["x"])
            project(k, "w_out0", ins["w_out0"], KC, whole_terms(parts, KC), add)
        ffn(0)
        with ExitStack() as l1:
            mix = k.sb(l1, "mixed", [P, NPC + 2, T])
            with ExitStack() as lz:
                z = k.sb(lz, "z_pool", [P, NPC + 2, T])
                with ExitStack() as n:
                    xn = two_parts(n, "in1", KC)
                    rms_norm(k, x, xn, k.cst["g_mix"][:, 1, :], T)
                    project(k, "w_in1", ins["w_in1"], NPC + 2, whole_terms(xn, KC),
                            lambda dve, m, banks: dve.tensor_copy(z[:, m, :], banks))
                head_norms(k, z[:, NPC:NPC + 2, :], 2, NORMED)
                pool_mixer(k, z, mix)
                memory_attention(k, 1, z[:, NPC:NPC + 2, :], mix[:, NPC:NPC + 2, :])
            parts = two_parts(l1, "mixed1", NPC + 2)
            rows = [PCH] * NPC + [P] * 2
            split_tokens(k, mix, parts, [(r, i) for i, r in enumerate(rows)])
            project(k, "w_out1", ins["w_out1"], KC, [(r, parts[0][0:r, i, :], parts[1][0:r, i, :]) for i, r in enumerate(rows)], add)
        ffn(1)
        store(k, [(outs["y"], x[:])])


def rel_buckets(dist):
    exact = BUCKETS // 2
    n = np.maximum(dist, 0)
    nf = np.maximum(n, 1).astype(np.float32)
    large = exact + (np.log(nf / np.float32(exact)) / np.float32(np.log(128 / exact)) * np.float32(BUCKETS - exact)).astype(np.int32)
    return np.where(n < exact, n, np.minimum(large, BUCKETS - 1))


def shape_constants():
    f = np.float32
    eye = np.eye(P, dtype=f)
    out = dict(ident=eye, ones=np.ones((P, P), f), halves=np.kron(np.eye(2), np.ones((HD, HD))).astype(f),
               flip=eye[::-1].copy())
    q, kk = np.arange(P)[:, None], np.arange(P)[None, :]
    out["edge_mask"] = np.where(kk >= q, 0, NEG).astype(f)
    m = np.arange(32)[None, :] - 16
    out["block_mask"] = (q - 63 - CB * m >= 0).astype(f)
    row_q = (np.arange(ROWS) % L)[:, None]
    out["win_mask"] = np.where(np.arange(L)[None, :] >= row_q, 0, NEG).astype(f)
    rows = np.arange(ROWS)
    gq = rows // GR * L + rows % L
    out["sum_heads"] = (gq[:, None] == np.arange(G * L)[None, :]).astype(f)
    out["spread_heads"] = out["sum_heads"].T.copy()
    diag = np.zeros((P, H), f)
    for j in range(3):
        diag[32 * j + np.arange(H), np.arange(H)] = 1
    out["diag"] = diag
    out["branch"] = np.zeros((P, 4), f)
    for j in range(3):
        out["branch"][32 * j:32 * j + H, j] = 1
    shift = np.zeros((P, G, 2, P), f)
    for g in range(G):
        for lp in range(2):
            shift[g * HD + np.arange(HD), g, lp, lp * HD + np.arange(HD)] = 1
    out["shift"] = shift
    eps = 1e-6
    is_q = np.array([i not in (Z_KS, Z_KW) for i in range(WHOLE)])
    scale = np.where(is_q, 1.0 / HD / SCALE ** 2, 1.0 / HD)
    bias = np.where(is_q, eps / SCALE ** 2, eps)
    out["norm_scale"] = np.broadcast_to(np.append(scale, 1.0 / D_MODEL), (P, WHOLE + 1)).astype(f)
    out["norm_bias"] = np.broadcast_to(np.append(bias, eps), (P, WHOLE + 1)).astype(f)
    dist = 255 - np.arange(RW)
    onehot = np.zeros((BUCKETS + 1, RW), f)
    onehot[np.where(dist >= 0, rel_buckets(dist), BUCKETS), np.arange(RW)] = 1
    out["onehot"] = onehot
    pos = np.arange(16)
    counts = np.stack([w / np.minimum(w, pos + 1) for w in POOLW])
    out["pool_counts"] = np.broadcast_to(counts, (P, 4, 16)).astype(f)
    return out


def lay_out(a):
    f = np.float32
    con = np.ascontiguousarray
    d = shape_constants()

    def chunks(w, cols=None, m=P, kchunks=None):
        kk = w.shape[0] // P
        return con(w.reshape(kk, P, -1, m).transpose(2, 1, 0, 3).reshape(-1, P, kk * m))

    def feature(g):
        return con(g.reshape(g.shape[0], -1, P).transpose(2, 0, 1))

    x = np.concatenate([a["x_prompt"][0], a["x_sample"].reshape(TS, D_MODEL)], 0)
    d["x"] = con(x.T.reshape(KC, P, T))
    d["mem"] = con(a["mem_prompt"][0].T.reshape(KC, P, NMEM))
    d["relx"] = np.concatenate([a["rel_bias"], np.full((1, H), NEG, f)], 0)
    wi = a["w_in_nsa"][0]
    qw = wi[:, :H * HD].reshape(D_MODEL, G, R, HD).transpose(0, 2, 1, 3).reshape(D_MODEL, H * HD)
    kvw = wi[:, H * HD:H * HD + 6 * P].reshape(D_MODEL, 6, P)
    gw = wi[:, H * HD + 6 * P:H * HD + 6 * P + 3 * H].reshape(D_MODEL, H, 3)
    gate = np.zeros((D_MODEL, 4, 32), f)
    gate[:, 0:3, 0:H] = gw.transpose(0, 2, 1)
    xq = wi[:, H * HD + 6 * P + 3 * H:]
    w0 = np.concatenate([qw, kvw[:, 2], kvw[:, 4], xq, kvw[:, 0], kvw[:, 1], kvw[:, 3], kvw[:, 5], gate.reshape(D_MODEL, P)], 1)
    d["w_in0"] = chunks(w0)
    w1 = a["w_in_pool"][0]
    pool = np.zeros((D_MODEL, NPC, P), f)
    pool[:, :, 0:PCH] = w1[:, :NPC * PCH].reshape(D_MODEL, NPC, PCH)
    d["w_in1"] = chunks(np.concatenate([pool.reshape(D_MODEL, NPC * P), w1[:, NPC * PCH:]], 1))
    wo = a["w_out"][0]
    wo0 = np.concatenate([wo[:H * HD].reshape(G, R, HD, D_MODEL).transpose(1, 0, 2, 3).reshape(H * HD, D_MODEL), wo[H * HD:]], 0)
    d["w_out0"] = chunks(wo0)
    wo = a["w_out"][1]
    wp = np.zeros((NPC, P, D_MODEL), f)
    wp[:, 0:PCH] = wo[:NPC * PCH].reshape(NPC, PCH, D_MODEL)
    d["w_out1"] = chunks(np.concatenate([wp.reshape(NPC * P, D_MODEL), wo[NPC * PCH:]], 0))
    d["w_mem"] = con(a["w_mem_kv"].reshape(2, KC, P, 4 * P).transpose(0, 2, 1, 3))
    d["w_up"] = con(a["w_up"].reshape(2, KC, P, 2 * FC, P).transpose(0, 3, 2, 1, 4).reshape(2, 2 * FC, P, KC * P))
    d["w_down"] = con(a["w_down"].reshape(2, FC, P, KC, P).transpose(0, 3, 2, 1, 4).reshape(2, KC, P, FC * P))
    twice = lambda g: np.concatenate([g, g], -1)
    qg, kg, xqg = twice(a["q_gain_nsa"][0]), twice(a["k_gain_nsa"][0]), twice(a["xq_gain"])
    d["gains"] = con(np.stack([qg] * R + [kg] * 2 + [xqg[0]] * 2 + [xqg[1]] * 2, 1))
    d["xk_gain"] = con(twice(a["xk_gain"]).T)
    for n in ("g_mix", "g_mem", "g_ffn"):
        d[n] = feature(a[n])
    d["cmp_pos"] = con(a["cmp_pos"][0].reshape(2, L2, 2, HD).transpose(2, 3, 0, 1).reshape(P, 2, L2))
    d["cmp_w1"] = con(a["cmp_w1"][0].reshape(2, L2, 2, HD, P).transpose(2, 3, 0, 1, 4).reshape(P, 2, L2, P))
    d["cmp_b1"] = con(a["cmp_b1"][0].T)
    d["cmp_w2"] = con(a["cmp_w2"][0].transpose(1, 0, 2))
    d["cmp_b2k"] = con(twice(a["cmp_b2"][0, 0])[:, None])
    d["cmp_b2v"] = con(np.broadcast_to(twice(a["cmp_b2"][0, 1]), (P, P)))
    ps = np.zeros((P, NPC), f)
    ps[0:PCH] = a["pool_scale"][0].reshape(NPC, PCH).T
    d["pool_scale"] = ps
    d["conv_b"] = feature(a["conv_b"])
    d["conv_w"] = con(a["conv_w"].reshape(2, 3, 2 * FC, P).transpose(3, 0, 1, 2))
    d["conv_state"] = con(a["state_ffn_conv"].reshape(2, B, 2, 2 * FC, P).transpose(4, 0, 3, 1, 2).reshape(P, 2, 2 * FC, 2 * B))
    d["pool_state"] = con(a["state_pool"][0].reshape(B, PST, NPC, PCH).transpose(3, 2, 0, 1).reshape(PCH, NPC, B * PST))
    d["w_grp"] = con(a["w_pool_grp"][0].reshape(4, 2, PCH, PG).transpose(2, 0, 1, 3).reshape(PCH, NPC, PG))
    cache = a["cache_nsa_kv"][0]
    n = cache.shape[0]
    cmp_rows = cache[:, :, 0:2].reshape(n, 2, L2, 2, 2, G, HD)
    d["cmp_pages"] = con(cmp_rows.transpose(0, 3, 6, 4, 2, 5, 1).reshape(n, P, 2 * L2 * G * 2))
    d["kv_pages"] = np.concatenate([cache[:, :, 2].reshape(n, PAGE, P).transpose(0, 2, 1), cache[:, :, 3].reshape(n, PAGE, P)], 2)
    win = a["cache_nsa_win"][0]
    d["win_k"] = con(win[:, :, 0].reshape(B, WINDOW, P).transpose(0, 2, 1))
    d["win_v"] = con(win[:, :, 1].reshape(B, WINDOW, P))
    cm = a["cache_mem_kv"]
    d["cmem_k"] = con(cm[:, :, :, 0].reshape(2, B, NMEM, 2, P).transpose(0, 1, 4, 3, 2).reshape(2, B, P, 2 * NMEM))
    d["cmem_v"] = con(cm[:, :, :, 1].reshape(2, B, 2, P, 2 * P).transpose(0, 1, 3, 2, 4).reshape(2, B, P, 4 * P))
    d["page_table"] = con(a["page_table"].astype(np.int32).reshape(1, B * PAGES))
    return {name: con(v) for name, v in d.items()}


_OUTS = dict(y=[P, KC, T], rows=[P, Z_GATE - Z_KS, T], win_k=[B, P, WINDOW], win_v=[B, WINDOW, P],
             mem_k=[2, P, 2, NMEM], mem_v=[2, P, 2, 2 * P], pool=[PCH, NPC, PST * (1 + B)],
             conv=[2, P, 2 * FC, 2 * (1 + B)])


def kernel(**inputs):
    import concourse.bacc as bacc
    from concourse.bass_utils import run_bass_kernel_spmd

    a = {n: np.asarray(v) for n, v in inputs.items()}
    arrays = lay_out(a)
    nc = bacc.Bacc("TRN2", target_bir_lowering=False, num_devices=1, dynamic_dma_scratch_size=1024)
    ins = {n: nc.dram_tensor(f"in_{n}", v.shape, mybir.dt.from_np(v.dtype), kind="ExternalInput").ap() for n, v in arrays.items()}
    outs = {n: nc.dram_tensor(f"out_{n}", s, F32, kind="ExternalOutput").ap() for n, s in _OUTS.items()}
    decoder(nc, ins, outs, a["cache_nsa_kv"].shape[1])
    r = run_bass_kernel_spmd(nc, [{f"in_{n}": v for n, v in arrays.items()}], core_ids=[0]).results[0]
    o = {n: r[f"out_{n}"] for n in _OUTS}

    y = o["y"].transpose(2, 1, 0).reshape(T, D_MODEL)
    y_prompt, y_sample = y[None, :SEQ], y[SEQ:].reshape(B, L, D_MODEL)
    at = {s: c - Z_KS for s, c in enumerate((Z_KC, Z_VC, Z_KS, Z_VS, Z_KW, Z_VW))}
    rows = np.stack([o["rows"][:, at[s], :].T.reshape(T, G, HD) for s in range(6)], 1)
    kv_p = rows[None, None, :SEQ, 0:4]
    kv_s = rows[SEQ:, 0:4].reshape(1, B, L, 4, G, HD)
    win_p = rows[None, None, SEQ - WINDOW:SEQ, 4:6]
    new = rows[SEQ:, 4:6].reshape(B, L, 2, G, HD)
    old = np.stack([o["win_k"].transpose(0, 2, 1), o["win_v"]], 2)[:, :WINDOW - L].reshape(B, WINDOW - L, 2, G, HD)
    win_s = np.concatenate([old, new], 1)[None]
    mk = o["mem_k"].transpose(0, 3, 2, 1).reshape(2, NMEM, XH, HD)
    mv = o["mem_v"].transpose(0, 2, 1, 3).reshape(2, NMEM, XH, HD)
    mem_kv = np.stack([mk, mv], 2)[:, None]
    pool = o["pool"].reshape(PCH, NPC, 1 + B, PST).transpose(2, 3, 1, 0).reshape(1 + B, PST, NPC * PCH)
    conv = o["conv"].reshape(2, P, 2 * FC, 1 + B, 2).transpose(0, 3, 4, 2, 1).reshape(2, 1 + B, 2, 2 * DFF)
    got = (y_prompt, y_sample, kv_p, kv_s, win_p, win_s, mem_kv, pool[None, :1], pool[None, 1:], conv[:, :1], conv[:, 1:])
    return tuple(np.ascontiguousarray(v, dtype=np.float32) for v in got)
```

```python
from contextlib import ExitStack

import numpy as np
import concourse.bass as bass
from concourse import mybir

F32 = mybir.dt.float32
F32R = mybir.dt.float32r
I32 = mybir.dt.int32
ALU = mybir.AluOpType
ACT = mybir.ActivationFunctionType
X = mybir.AxisListType.X

P = 128
D_MODEL = 1024
KC = D_MODEL // P
SEQ = 1024
B, L = 8, 8
TS = B * L
T = SEQ + TS
QT = SEQ // P
PAST = 4096
PAGE = 128
PAGES = PAST // PAGE
HD = 64
G, R = 2, 6
H = G * R
ROWS = H * L
GR = R * L
CB = 64
L2 = CB // 2
NCP = SEQ // CB
NCS = PAST // CB
NBS = NCS + 1
WINDOW = 512
XH = 4
NMEM = 256
DFF = 2816
FC = DFF // P
PARTS = (6, 6, 5, 5)
PG = 192
PCH = 96
NPC = 8
POOLW = (2, 4, 8, 16)
PST = 15
BUCKETS = 32
RW = 384
NEG = -1e30
FORCED = 1e4
SCALE = HD ** -0.5
LOWEST = -3e38
TAIL = P + L
NT = ((0, 512), (512, 512), (1024, 64))
CUTS = 4
CUT = T // CUTS

Z_Q, Z_KS, Z_KW, Z_XQ, Z_KC, Z_VC, Z_VS, Z_VW, Z_GATE = 0, 6, 7, 8, 10, 11, 12, 13, 14
NZ = 15
NORMED = 10
WHOLE = NORMED + 2


def pairs(eng, n, body, between=None):
    if between:
        body(0, 0, 0)
        body(1, 0, 1)
        between()
    if n // 2:
        with eng.Fori(1 if between else 0, n // 2) as j:
            body(j * 2, j, 0)
            body(j * 2 + 1, j, 1)
    if n % 2:
        body(n - 1, n // 2, 0)


class Kernel:

    def __init__(self, nc, ctx, ins, outs):
        self.nc, self.ctx, self.ins, self.outs = nc, ctx, ins, outs
        self.made = 0
        self.sems_of, self.sems = None, []
        self.cleared = []

    def sb(self, ctx, name, shape, dtype=F32):
        self.made += 1
        return ctx.enter_context(self.nc.sbuf_tensor(f"{name}_{self.made}", shape, dtype))

    def retire(self, sems):
        for s in self.cleared:
            self.nc.release_semaphore(s)
        for s in sems:
            self.nc.gpsimd.sem_clear(s)
        self.cleared = sems

    def sem(self, ctx, name):
        if self.sems_of is not ctx:
            self.sems_of, self.sems = ctx, []
            ctx.callback(self.retire, self.sems)
        self.made += 1
        self.sems.append(self.nc.alloc_semaphore(f"{name}_{self.made}"))
        return self.sems[-1]


def wait_apart(k, eng, sem, value):
    eng.wait_ge(sem, value)
    eng.sem_inc(k.passed, 1)


LOOKUP = 32


def load_pages(k, sp, b, pages, dst, loaded):
    with sp.Fori(0, PAGES // LOOKUP) as i:
        _, found = k.nc.values_load_multi_w_load_instructions(
            k.cst["page_table"][0:1, bass.ds(b * PAGES + i * LOOKUP, LOOKUP)], engines=(mybir.EngineType.SP,),
            min_val=0, max_val=k.n_pages - 1)
        for x in range(LOOKUP):
            sp.dma_start(dst[:, bass.ds(i * LOOKUP + x, 1), :].rearrange("p a n -> p (a n)"), pages[found[x]]).then_inc(loaded, 16)


def bank_set(k, s):
    return k.ps[:, 3 * s:3 * s + 3, :].rearrange("p b n -> p (b n)")[:, 0:T]


def cut_set(k, s):
    return k.ps[:, 4 * s:4 * s + 4, 0:CUT]


def in_cuts(ap):
    return ap.rearrange("p (b n) -> p b n", b=CUTS)


def samples(ap):
    return ap[:, SEQ:T].rearrange("p (b q) -> p b q", b=B)


def load_constants(k, octx, names, others=()):
    for n in names:
        k.cst[n] = k.sb(octx, n, CONSTANTS[n], I32 if n in SMALL_INTEGERS else F32)
    with ExitStack() as ctx:
        loaded = k.sem(ctx, "constants_loaded")
        block = ctx.enter_context(k.nc.Block())

        @block.sync
        def _(sp):
            for n in names:
                sp.dma_start(k.cst[n][:], k.ins[n]).then_inc(loaded, 16)
            for dst, src in others:
                sp.dma_start(dst, src).then_inc(loaded, 16)
            sp.wait_ge(loaded, 16 * (len(names) + len(others)))


def bias_tables(k):
    nc, c = k.nc, k.cst
    with ExitStack() as ctx:
        load_constants(k, ctx, TABLES)
        row = k.sb(ctx, "bias_row", [H, RW])
        hank = k.sb(ctx, "bias_hankel", [P, H, 256])
        row_ready = k.sem(ctx, "bias_row_product")
        row_read = k.sem(ctx, "bias_row_read")
        row_stored = k.sem(ctx, "bias_row_stored")
        tables_loaded = k.sem(ctx, "tables_loaded")
        flipped = k.sem(ctx, "tables_flipped")
        block = ctx.enter_context(nc.Block())

        @block.tensor
        def _(pe):
            pe.matmul(k.ps[0:H, 0, 0:RW], c["relx"][:, :], c["onehot"][:, :], start=True, stop=True).then_inc(row_ready, 1)
            pe.wait_ge(tables_loaded, 16 * (1 + 2 * L))
            for i in range(6):
                last = pe.matmul(k.ps[:, i, :], c["flip"][:, :], hank[:, 2 * i:2 * i + 2, :], start=True, stop=True)
            last.then_inc(flipped, 1)

        @block.vector
        def _(dve):
            dve.wait_ge(row_ready, 1)
            dve.tensor_copy(row[:], k.ps[0:H, 0, 0:RW]).then_inc(row_read, 1)
            dve.wait_ge(flipped, 1)
            dve.tensor_copy(k.near_bias[:], k.ps[:, 0:6, :].rearrange("p i (h n) -> p (i h) n", h=2))
            dve.memset(k.block_bias[:], NEG)
            dve.drain()
            dve.tensor_copy(k.block_bias[:, :, 14:18], k.near_bias[:, :, CB - 1:256:CB])
            dve.tensor_copy(k.block_bias[:, :, 0:14], k.near_bias[:, :, 0:1].broadcast_to([P, H, 14]))
            far = k.row_far[:, 0:1]
            dve.tensor_copy(k.row_blocks[:, 0:NCS - 2], far.broadcast_to([ROWS, NCS - 2]))
            dve.tensor_copy(k.row_blocks[:, NCS - 2:NCS - 1], k.row_tail[:, 63:64])
            dve.tensor_copy(k.row_blocks[:, NCS - 1:NCS], k.row_tail[:, 127:128])
            dve.memset(k.row_select[:], 0.0)
            dve.drain()
            dve.tensor_copy(k.row_select[:, 0:NCS - 2], far.broadcast_to([ROWS, NCS - 2]))
            dve.tensor_copy(k.row_window[:, 0:WINDOW - P], far.broadcast_to([ROWS, WINDOW - P]))
            dve.tensor_copy(k.row_window[:, WINDOW - P:WINDOW + L], k.row_tail[:, :])
            dve.drain()
            dve.tensor_tensor(k.row_window[:, 0:L], k.row_window[:, 0:L], c["win_mask"][:, :], ALU.add)

        @block.sync
        def _(sp):
            sp.wait_ge(row_read, 1)
            sp.dma_start(k.row_dram, row[:]).then_inc(row_stored, 16)
            sp.wait_ge(row_stored, 16)
            sp.dma_start(hank[:], bass.AP(k.row_dram.tensor, 0, [[1, P], [RW, H], [1, 256]])).then_inc(tables_loaded, 16)
            for q in range(L):
                sp.dma_start(k.row_tail[q:ROWS:L, :], k.row_dram[:, 127 - q:127 - q + TAIL]).then_inc(tables_loaded, 16)
                sp.dma_start(k.row_far[q:ROWS:L, :], k.row_dram[:, 0:2]).then_inc(tables_loaded, 16)
            sp.wait_ge(tables_loaded, 16 * (1 + 2 * L))


class Norm:

    def __init__(self, k, ctx, x, out, gain, n, room, loaded=None):
        self.k, self.x, self.gain, self.n, self.loaded = k, x, gain, n, loaded
        self.parts = isinstance(out, tuple)
        self.out = out
        self.sq, self.acc, self.rms = room
        self.whole = self.sq
        self.squared = k.sem(ctx, "squared")
        self.added = k.sem(ctx, "squares_added")
        self.summed = k.sem(ctx, "squares_summed")
        self.rooted = k.sem(ctx, "rooted")
        self.normed = k.sem(ctx, "normed")
        self.rounded = k.sem(ctx, "rounded")
        self.split = [k.sem(ctx, f"split_by_{e}") for e in ("vector", "gpsimd")]
        self.total = k.ps[:, 0:3, :].rearrange("p b n -> p (b n)")[:, 0:n]

    def act(self, act):
        c = self.k.cst
        for i in range(KC):
            if self.loaded and i % 2 == 0:
                act.wait_ge(self.loaded[i // 2], 16)
            if i >= 2:
                act.wait_ge(self.added, i - 1)
            act.activation(self.sq[:, i % 2, :], self.x[:, i, :], ACT.Square).then_inc(self.squared, 1)
        act.wait_ge(self.summed, 1)
        act.activation(self.rms, self.total, ACT.Sqrt, bias=c["norm_bias"][:, WHOLE:WHOLE + 1],
                       scale=c["norm_scale"][:, WHOLE:WHOLE + 1]).then_inc(self.rooted, 1)
        if self.parts:
            for i in range(KC):
                act.wait_ge(self.normed, i + 1)
                act.activation(self.out[0][:, i, :], self.whole[:, i % 2, :], ACT.Copy).then_inc(self.rounded, 1)

    def low(self, eng, i):
        eng.wait_ge(self.rounded, i + 1)
        eng.tensor_tensor(self.out[1][:, i, :], self.whole[:, i % 2, :], self.out[0][:, i, :].bitcast(F32),
                          ALU.subtract).then_inc(self.split[i % 2], 1)

    def pe(self, pe):
        pe.wait_ge(self.added, KC)
        for a in range(0, self.n, 512):
            w = min(512, self.n - a)
            last = pe.matmul(self.total[:, a:a + w], self.k.cst["ones"][:, :], self.acc[:, a:a + w], start=True, stop=True)
        last.then_inc(self.summed, 1)

    def dve(self, dve):
        for i in range(KC):
            dve.wait_ge(self.squared, i + 1)
            if i == 1:
                dve.tensor_tensor(self.acc, self.sq[:, 0, :], self.sq[:, 1, :], ALU.add).then_inc(self.added, 2)
            elif i > 1:
                dve.tensor_tensor(self.acc, self.acc, self.sq[:, i % 2, :], ALU.add).then_inc(self.added, 1)
            dve.drain()
        dve.wait_ge(self.rooted, 1)
        dve.reciprocal(self.rms, self.rms)
        dve.drain()
        for i in range(KC):
            if self.parts and i % 2 and i >= 3:
                dve.wait_ge(self.split[1], i // 2)
            dst = self.whole[:, i % 2, :] if self.parts else self.out[:, i, :]
            dve.scalar_tensor_tensor(out=dst, in0=self.x[:, i, :], scalar=self.gain[:, i:i + 1], in1=self.rms,
                                     op0=ALU.mult, op1=ALU.mult).then_inc(self.normed, 1)
            if self.parts and i % 2:
                self.low(dve, i - 1)
                dve.drain()

    def pool(self, pool):
        if self.parts:
            for i in range(1, KC, 2):
                self.low(pool, i)

    def wait_ready(self, pe):
        for s in self.split:
            pe.wait_ge(s, KC // 2)

    def wait_chunk(self, pe, i):
        pe.wait_ge(self.split[i % 2], i // 2 + 1)


class Split:

    def __init__(self, k, ctx, src, out, chunks):
        self.src, self.out, self.chunks = src, out, chunks
        self.rounded = k.sem(ctx, "rounded")
        self.split = k.sem(ctx, "split")

    def act(self, act):
        for rows, i in self.chunks:
            act.activation(self.out[0][0:rows, i, :], self.src[0:rows, i, :], ACT.Copy).then_inc(self.rounded, 1)

    def dve(self, dve):
        for n, (rows, i) in enumerate(self.chunks):
            dve.wait_ge(self.rounded, n + 1)
            dve.tensor_tensor(self.out[1][0:rows, i, :], self.src[0:rows, i, :], self.out[0][0:rows, i, :].bitcast(F32),
                              ALU.subtract).then_inc(self.split, 1)

    def pe(self, pe):
        pass

    def pool(self, pool):
        pass

    def wait_ready(self, eng):
        eng.wait_ge(self.split, len(self.chunks))

    def wait_chunk(self, pe, i):
        pe.wait_ge(self.split, i + 1)


def rms_norm(k, x, out, gain, n):
    with ExitStack() as ctx:
        room = (k.sb(ctx, "squares", [P, 2, n])[:, :, :], k.sb(ctx, "squares_added", [P, n])[:, :], k.sb(ctx, "rms", [P, n])[:, :])
        norm = Norm(k, ctx, x, out, gain, n, room)
        block = ctx.enter_context(k.nc.Block())

        @block.scalar
        def _(act):
            norm.act(act)

        @block.tensor
        def _(pe):
            norm.pe(pe)

        @block.vector
        def _(dve):
            norm.dve(dve)


class Weights:

    def __init__(self, k, ctx, name, cols):
        self.whole = k.sb(ctx, name + "_whole", [P, 2, cols])
        self.high = k.sb(ctx, name + "_high", [P, 2, cols], F32R)
        self.low = k.sb(ctx, name + "_low", [P, 2, cols], F32R)
        self.loaded = [k.sem(ctx, f"{name}_loaded{s}") for s in range(2)]
        self.split = k.sem(ctx, name + "_split")
        self.multiplied = k.sem(ctx, name + "_multiplied")

    def load(self, sp, t, s, src, cols):
        sp.wait_ge(self.split, t + 1)
        sp.dma_start(self.whole[:, s, 0:cols], src).then_inc(self.loaded[s], 16)

    def part(self, k, pool, t, j, s, cols):
        whole, high, low = (x[:, s, 0:cols] for x in (self.whole, self.high, self.low))
        pool.wait_ge(self.loaded[s], j * 16 + 16)
        wait_apart(k, pool, self.multiplied, t + 1)
        pool.tensor_scalar(high, whole, 1.0, None, ALU.mult)
        pool.drain()
        pool.tensor_tensor(low, whole, high.bitcast(F32), ALU.subtract).then_inc(self.split, 1)

    def multiply(self, pe, t, s, terms, out, ready=None):
        pe.wait_ge(self.split, t + 3)
        for kk, (rows, high, low) in enumerate(terms):
            if ready:
                ready(kk)
            wh = self.high[0:rows, s, kk * P:(kk + 1) * P]
            wl = self.low[0:rows, s, kk * P:(kk + 1) * P]
            for cut in range(CUTS):
                o, at = out[:, cut, :], slice(cut * CUT, (cut + 1) * CUT)
                pe.matmul(o, wh, high[:, at], start=kk == 0, stop=False)
                pe.matmul(o, wh, low[:, at], start=False, stop=False)
                last = pe.matmul(o, wl, high[:, at], start=False, stop=kk == len(terms) - 1)
        last.then_inc(self.multiplied, 1)


def project(k, name, w_src, n, terms, make_tokens, read, load=None, late_load=None):
    cols = len(terms) * P
    with ExitStack() as ctx:
        w = Weights(k, ctx, name, cols)
        taken = k.sem(ctx, name + "_taken")
        x_loaded = [k.sem(ctx, f"x_loaded{i}") for i in range(KC // 2)] if load else None
        late_loaded = k.sem(ctx, "late_loaded")
        tokens = make_tokens(ctx, x_loaded)
        block = ctx.enter_context(k.nc.Block())

        @block.sync
        def _(sp):
            if load:
                for i in range(KC // 2):
                    sp.dma_start(load[0][:, 2 * i:2 * i + 2, :], load[1][2 * i:2 * i + 2].rearrange("k p t -> p k t")).then_inc(x_loaded[i], 16)

            def late():
                if late_load:
                    tokens.wait_ready(sp)
                    sp.dma_start(late_load[0][:], late_load[1].rearrange("k p t -> p k t")).then_inc(late_loaded, 16)
            pairs(sp, n, lambda m, j, s: w.load(sp, m, s, w_src[m], cols), late)

        @block.gpsimd
        def _(pool):
            pool.sem_inc(w.split, 2)
            pairs(pool, n, lambda m, j, s: w.part(k, pool, m, j, s, cols), lambda: tokens.pool(pool))

        @block.tensor
        def _(pe):
            pe.sem_inc(w.multiplied, 2)
            tokens.pe(pe)

            def multiply(m, j, s):
                ready = (lambda i: tokens.wait_chunk(pe, i)) if isinstance(m, int) and m == 0 else None
                pe.wait_ge(taken, m + 1)
                w.multiply(pe, m, s, terms, cut_set(k, s), ready)
            pairs(pe, n, multiply, lambda: None)

        @block.scalar
        def _(act):
            tokens.act(act)

        @block.vector
        def _(dve):
            dve.sem_inc(taken, 2)
            tokens.dve(dve)
            if late_load:
                dve.wait_ge(late_loaded, 16)

            def take(m, j, s):
                dve.wait_ge(w.multiplied, m + 3)
                read(dve, m, cut_set(k, s)).then_inc(taken, 1)
            pairs(dve, n, take)


def head_norms(k, z, n, first, layer):
    c = k.cst
    rows = 2 * n
    with ExitStack() as ctx:
        for name in HEADS:
            c[name] = k.sb(ctx, name, CONSTANTS[name])
        sq = k.sb(ctx, "head_squares", [P, 2, T])
        rstd = k.sb(ctx, "head_rstd", [rows, T])
        loaded = k.sem(ctx, "head_constants_loaded")
        squared = k.sem(ctx, "head_squared")
        summed = k.sem(ctx, "head_summed")
        rooted = k.sem(ctx, "head_rooted")
        inverted = k.sem(ctx, "head_inverted")
        spread = k.sem(ctx, "head_spread")
        normed = k.sem(ctx, "head_normed")
        block = ctx.enter_context(k.nc.Block())

        @block.sync
        def _(sp):
            for name in HEADS:
                sp.dma_start(c[name][:], k.ins[name]).then_inc(loaded, 16)

        @block.scalar
        def _(act):
            for m in range(n):
                if m >= 2:
                    act.wait_ge(summed, m - 1)
                act.activation(sq[:, m % 2, :], z[:, m, :], ACT.Square).then_inc(squared, 1)
            act.wait_ge(summed, n)
            act.activation(rstd[:], bank_set(k, 0)[0:rows, :], ACT.Sqrt, bias=c["head_bias"][0:rows, layer:layer + 1],
                           scale=c["head_scale"][0:rows, layer:layer + 1]).then_inc(rooted, 1)

        @block.tensor
        def _(pe):
            pe.wait_ge(loaded, 16 * len(HEADS))
            for m in range(n):
                pe.wait_ge(squared, m + 1)
                for a, cols in NT:
                    last = pe.matmul(bank_set(k, 0)[0:rows, a:a + cols], c["head_pick"][:, m, 0:rows], sq[:, m % 2, a:a + cols],
                                     start=m == 0, stop=m == n - 1)
                last.then_inc(summed, 1)
            pe.wait_ge(inverted, 1)
            for m in range(n):
                if m >= 2:
                    pe.wait_ge(normed, m - 1)
                for a, cols in NT:
                    last = pe.matmul(bank_set(k, (m + 1) % 2)[:, a:a + cols], c["head_spread"][0:rows, m, :], rstd[:, a:a + cols],
                                     start=True, stop=True)
                last.then_inc(spread, 1)

        @block.vector
        def _(dve):
            dve.wait_ge(rooted, 1)
            dve.reciprocal(rstd[:], rstd[:]).then_inc(inverted, 1)
            for m in range(n):
                dve.wait_ge(spread, m + 1)
                dve.scalar_tensor_tensor(out=z[:, m, :], in0=z[:, m, :], scalar=c["gains"][:, m + first:m + first + 1],
                                         in1=bank_set(k, (m + 1) % 2), op0=ALU.mult, op1=ALU.mult).then_inc(normed, 1)


def memory_kv(k, layer, mem, memn, w):
    c = k.cst
    rms_norm(k, mem, memn, c["g_mem"][:, layer, :], NMEM)
    with ExitStack() as ctx:
        sq = k.sb(ctx, "mem_squares", [P, 2, NMEM])
        rms = k.sb(ctx, "mem_rms", [P, 2 * NMEM])
        keys = k.mem_k[:, layer, :, :]
        multiplied = k.sem(ctx, "mem_multiplied")
        squared = k.sem(ctx, "mem_squared")
        summed = k.sem(ctx, "mem_summed")
        rooted = k.sem(ctx, "mem_rooted")
        written = k.sem(ctx, "mem_written")
        stored = k.sem(ctx, "mem_stored")
        block = ctx.enter_context(k.nc.Block())

        @block.sync
        def _(sp):
            sp.wait_ge(written, 1)
            sp.dma_start(k.outs["mem_k"][layer], keys).then_inc(stored, 16)
            sp.dma_start(k.outs["mem_v"][layer], k.mem_v[:, layer, :, :]).then_inc(stored, 16)
            sp.wait_ge(stored, 32)

        @block.tensor
        def _(pe):
            for ch in range(2):
                for kk in range(KC):
                    pe.matmul(k.ps[:, ch, 0:NMEM], w[:, kk, ch * P:(ch + 1) * P], memn[:, kk, :],
                              start=kk == 0, stop=kk == KC - 1)
            for mt in range(2):
                for kk in range(KC):
                    last = pe.matmul(k.ps[:, 2 + mt, 0:NMEM], memn[:, kk, mt * P:(mt + 1) * P], w[:, kk, 2 * P:4 * P],
                                     start=kk == 0, stop=kk == KC - 1)
            last.then_inc(multiplied, 1)
            pe.wait_ge(squared, 1)
            pe.matmul(k.ps[:, 4, :], c["halves"][:, :], sq[:, :, :], start=True, stop=True).then_inc(summed, 1)

        @block.scalar
        def _(act):
            act.wait_ge(multiplied, 1)
            act.activation(sq[:, :, :], k.ps[:, 0:2, 0:NMEM], ACT.Square).then_inc(squared, 1)
            act.wait_ge(summed, 1)
            act.activation(rms[:], k.ps[:, 4, :], ACT.Sqrt, bias=c["norm_bias"][:, Z_KS:Z_KS + 1],
                           scale=c["norm_scale"][:, Z_KS:Z_KS + 1]).then_inc(rooted, 1)

        @block.vector
        def _(dve):
            dve.wait_ge(multiplied, 1)
            dve.tensor_copy(k.mem_v[:, layer, :, :], k.ps[:, 2:4, 0:NMEM])
            dve.wait_ge(rooted, 1)
            dve.reciprocal(rms[:], rms[:])
            dve.drain()
            dve.scalar_tensor_tensor(out=keys, in0=k.ps[:, 0:2, 0:NMEM], scalar=c["xk_gain"][:, layer:layer + 1],
                                     in1=rms[:].rearrange("p (c n) -> p c n", c=2), op0=ALU.mult, op1=ALU.mult)
            dve.drain().then_inc(written, 1)


def token_major_values(k, z, vals):
    with ExitStack() as ctx:
        turned = k.sem(ctx, "values_turned")
        copied = k.sem(ctx, "values_copied")
        block = ctx.enter_context(k.nc.Block())

        @block.tensor
        def _(pe):
            for i in range(4):
                if i >= 2:
                    pe.wait_ge(copied, i - 1)
                for t in range(4):
                    last = pe.transpose(k.ps[:, i % 2, t * P:(t + 1) * P],
                                        z[:, Z_VS + i // 2, (4 * (i % 2) + t) * P:(4 * (i % 2) + t + 1) * P],
                                        k.cst["ident"][:, :])
                last.then_inc(turned, 1)

        @block.vector
        def _(dve):
            for i in range(4):
                dve.wait_ge(turned, i + 1)
                dve.tensor_copy(vals[:, i // 2, 4 * (i % 2):4 * (i % 2) + 4, :],
                                k.ps[:, i % 2, :].rearrange("p (t n) -> p t n", t=4)).then_inc(copied, 1)


def compress(k, z, spare, comp_k, comp_v):
    nc, c = k.nc, k.cst
    QP = PAGES * 2 * G
    with ExitStack() as ctx:
        load_constants(k, ctx, COMPRESSION)
        w1 = k.sb(ctx, "cmp_w1", [P, 2, L2, P])
        row_len = 2 * L2 * G * 2
        rows = [spare[:, :, :].rearrange("p a n -> p (a n)")[:, 0:PAGES * row_len].rearrange("p (a n) -> p a n", a=PAGES),
                k.sb(ctx, "cmp_rows", [P, PAGES, row_len])[:, :, :]]
        own = rows[0][:, 0:8, :].rearrange("p a n -> p (a n)")
        bias = k.sb(ctx, "cmp_bias", [P, 2])
        hid = k.sb(ctx, "cmp_hidden", [P, 2, QP])
        kc = k.sb(ctx, "cmp_keys", [P, NCS])
        sq = k.sb(ctx, "cmp_squares", [P, NCS])
        rms = k.sb(ctx, "cmp_rms", [P, NCS])
        w_loaded = k.sem(ctx, "cmp_weights_loaded")
        rows_loaded = [k.sem(ctx, f"cmp_rows_loaded{s}") for s in range(2)]
        pos_summed = k.sem(ctx, "cmp_pos_summed")
        bias_ready = k.sem(ctx, "cmp_bias_ready")
        hidden = k.sem(ctx, "cmp_hidden_summed")
        active = k.sem(ctx, "cmp_activated")
        mapped = k.sem(ctx, "cmp_mapped")
        squared = k.sem(ctx, "cmp_squared")
        summed = k.sem(ctx, "cmp_squares_summed")
        rooted = k.sem(ctx, "cmp_rooted")
        own_moved = k.sem(ctx, "cmp_own_moved")
        own_written = k.sem(ctx, "cmp_own_written")
        block = ctx.enter_context(nc.Block())

        def row_view(s, kv, l2, n):
            v = rows[s][:, 0:n // (2 * G), :].rearrange("p a (k l c) -> p k l a c", k=2, l=L2)
            return v[:, kv, l2, :, :]

        @block.sync
        def _(sp):
            sp.dma_start(w1[:], k.ins["cmp_w1"]).then_inc(w_loaded, 16)

            def load(b, j, s):
                wait_apart(k, sp, hidden, b + 1)
                load_pages(k, sp, b, k.ins["cmp_pages"], rows[s], rows_loaded[s])
            pairs(sp, B, load)

        def second(pe, kv, b, cols):
            v = hid[:, kv, 0:cols].rearrange("p (g n) -> p g n", g=G)
            for g in range(G):
                if kv == 0:
                    last = pe.matmul(k.ps[g * HD:(g + 1) * HD, 2, 0:cols // G], c["cmp_w2"][:, 0, :], v[:, g, :],
                                     start=True, stop=True)
                else:
                    last = pe.matmul(k.ps[0:cols // G, 4, g * HD:(g + 1) * HD], v[:, g, :], c["cmp_w2"][:, 1, :],
                                     start=True, stop=True)
            return last

        def hidden_layer(pe, b, s, cols, view):
            for kv in range(2):
                for l2 in range(L2):
                    last = pe.matmul(k.ps[:, 5 * s + kv, 0:cols], w1[:, kv, l2, :], view(kv, l2), start=l2 == 0, stop=l2 == L2 - 1)
            last.then_inc(hidden, 1)

        def rest(pe, b, cols):
            pe.wait_ge(active, b + 1)
            second(pe, 0, b, cols)
            second(pe, 1, b, cols).then_inc(mapped, 1)
            pe.wait_ge(squared, b + 1)
            pe.matmul(k.ps[:, 3, 0:cols // G], c["halves"][:, :], sq[:, 0:cols // G], start=True, stop=True).then_inc(summed, 1)

        @block.tensor
        def _(pe):
            pe.sem_inc(hidden, 2)
            pe.wait_ge(w_loaded, 16)
            for kv in range(2):
                for l2 in range(L2):
                    last = pe.matmul(k.ps[:, 5 + kv, 0:1], w1[:, kv, l2, :], c["cmp_pos"][:, kv, l2:l2 + 1],
                                     start=l2 == 0, stop=l2 == L2 - 1)
            last.then_inc(pos_summed, 1)

            def sample(b, j, s):
                pe.wait_ge(rows_loaded[s], (j + 1) * (16 * PAGES))
                hidden_layer(pe, b, s, QP, lambda kv, l2: row_view(s, kv, l2, QP))

            sample(0, 0, 0)
            pe.wait_ge(bias_ready, 1)
            sample(1, 0, 1)
            rest(pe, 0, QP)
            with pe.Fori(1, B // 2) as j:
                for s in range(2):
                    sample(j * 2 + s, j, s)
                    rest(pe, j * 2 + (s - 1), QP)
            for kv in range(2):
                for g in range(G):
                    if kv or g:
                        pe.wait_ge(own_written, 2 * kv + g)
                    for lp in range(2):
                        src = z[:, Z_KC + kv, 0:SEQ].rearrange("p (n l) -> p l n", l=2)[:, lp, :]
                        last = pe.matmul(k.ps[:, 7, :], c["shift"][:, g, lp, :], src, start=lp == 0, stop=lp == 1)
                    last.then_inc(own_moved, 1)
            rest(pe, B - 1, QP)
            pe.wait_ge(own_written, 4)
            ov = own.rearrange("p (k l n) -> p k l n", k=2, l=L2)
            hidden_layer(pe, B, 0, NCP * G, lambda kv, l2: ov[:, kv, l2, :])
            rest(pe, B, NCP * G)

        def finish(dve, b, cols):
            n = cols // G
            dve.wait_ge(mapped, b + 1)
            dve.tensor_scalar(kc[:, 0:n], k.ps[:, 2, 0:n], c["cmp_b2k"][:, 0:1], None, ALU.add)
            dve.tensor_tensor(comp_v[0:n, b, :], k.ps[0:n, 4, 0:P], c["cmp_b2v"][0:n, :], ALU.add)
            dve.drain()
            dve.tensor_tensor(sq[:, 0:n], kc[:, 0:n], kc[:, 0:n], ALU.mult).then_inc(squared, 1)
            dve.wait_ge(rooted, b + 1)
            dve.reciprocal(rms[:, 0:n], rms[:, 0:n])
            dve.drain()
            dve.scalar_tensor_tensor(out=comp_k[:, b, 0:n], in0=kc[:, 0:n], scalar=c["gains"][:, Z_KS:Z_KS + 1],
                                     in1=rms[:, 0:n], op0=ALU.mult, op1=ALU.mult)
            dve.drain()

        @block.vector
        def _(dve):
            dve.wait_ge(pos_summed, 1)
            dve.tensor_tensor(bias[:, 0:2], k.ps[:, 5:7, 0:1].rearrange("p a b -> p (a b)"), c["cmp_b1"][:, :], ALU.add).then_inc(bias_ready, 1)
            with dve.Fori(0, B - 1) as b:
                finish(dve, b, QP)
            ov = own.rearrange("p (k l a g c) -> p k l a g c", k=2, l=L2, g=G, c=2)
            for kv in range(2):
                for g in range(G):
                    dve.wait_ge(own_moved, 2 * kv + g + 1)
                    dve.tensor_copy(ov[:, kv, :, :, g, :], k.ps[:, 7, :].rearrange("p (a c l) -> p l a c", l=L2, c=2)).then_inc(own_written, 1)
            finish(dve, B - 1, QP)
            finish(dve, B, NCP * G)

        @block.scalar
        def _(act):
            act.wait_ge(bias_ready, 1)

            def gelu(b, s, cols):
                act.wait_ge(hidden, b + 3)
                for kv in range(2):
                    last = act.activation(hid[:, kv, 0:cols].rearrange("p (g a c) -> p a g c", g=G, c=2),
                                          k.ps[:, 5 * s + kv, 0:cols].rearrange("p (a g c) -> p a g c", g=G, c=2), ACT.Gelu_apprx_tanh, bias=bias[:, kv:kv + 1])
                last.then_inc(active, 1)
                act.wait_ge(summed, b + 1)
                act.activation(rms[:, 0:cols // G], k.ps[:, 3, 0:cols // G], ACT.Sqrt,
                               bias=c["norm_bias"][:, Z_KS:Z_KS + 1], scale=c["norm_scale"][:, Z_KS:Z_KS + 1]).then_inc(rooted, 1)
            pairs(act, B, lambda b, j, s: gelu(b, s, QP))
            gelu(B, 0, NCP * G)


def prompt_attention(k, z, zs, vals, comp_k, comp_v, mix):
    nc, c = k.nc, k.cst
    UN = QT * G
    WK = WINDOW + P
    SLOTS = 4
    AHEAD = SLOTS - 1
    assert UN % SLOTS == 0
    with ExitStack() as ctx:
        q = k.sb(ctx, "pair_queries", [P, SEQ])
        far = k.sb(ctx, "pair_bias", [P, G, SEQ])
        win = k.sb(ctx, "pair_window_bias", [P, G, WK])
        cbias = k.sb(ctx, "pair_block_bias", [P, G, 32])
        gates = k.sb(ctx, "gates", [P, QT, 3, H])
        gate_x = z[:, Z_GATE, :]
        ls = k.sb(ctx, "logits_selected", [P, SLOTS, SEQ])
        lw = k.sb(ctx, "logits_window", [P, SLOTS, WK])
        lc = k.sb(ctx, "logits_blocks", [P, SLOTS, NCP])
        mx = k.sb(ctx, "maxima", [P, SLOTS, 4])
        nmx = k.sb(ctx, "negated_maxima", [P, SLOTS, 4])
        sums = k.sb(ctx, "sums", [P, SLOTS, 4])
        coef = k.sb(ctx, "coefficients", [P, SLOTS, 4])
        pt = k.sb(ctx, "probs_turned", [P, 4, 512])
        stored = k.sem(ctx, "rows_stored")
        gates_turned = k.sem(ctx, "gates_turned")
        gates_on = k.sem(ctx, "gates_sigmoid")
        gates_read = k.sem(ctx, "gates_read")
        pair_ready = k.sem(ctx, "pair_ready")
        scored = k.sem(ctx, "scored")
        biased = k.sem(ctx, "biased")
        exped = k.sem(ctx, "exped")
        scaled = k.sem(ctx, "probs_scaled")
        turned = k.sem(ctx, "turned")
        copied = k.sem(ctx, "turned_copied")
        valued = k.sem(ctx, "valued")
        placed = k.sem(ctx, "outputs_placed")
        block = ctx.enter_context(nc.Block())

        tiles = [t for x in range(QT // 2) for t in (x, QT - 1 - x)]
        units = [(t, g) for x in range(0, QT, 2) for g in range(G) for t in tiles[x:x + 2]]

        def turns(t):
            sel = [("s", i * P, P, i) for i in range(t + 1)]
            w = [("w", (i - t + 4) * P, P, i) for i in range(max(0, t - 4), t + 1)]
            allt = sel + w + [("c", 0, NCP, 0)]
            return [allt[i:i + 4] for i in range(0, len(allt), 4)]

        banks_before = [0]
        for t, g in units:
            banks_before.append(banks_before[-1] + len(turns(t)))
        BANKS = banks_before[-1]
        assert BANKS % 4 == 0

        S_SEL = k.ps[:, 0:2, :].rearrange("p b n -> p (b n)")
        S_WIN = k.ps[:, 2:4, :].rearrange("p b n -> p (b n)")
        S_CMP = k.ps[:, 3, 256:256 + NCP]

        def extent(t):
            return (t + 1) * P, (max(0, t - 4) - t + 4) * P

        def out(u):
            g = units[u][1]
            return k.ps[g * HD:(g + 1) * HD, 6 + u % 2, 0:P]

        def passes(eng, one_pass):
            with eng.Fori(0, R - 1) as i:
                one_pass(i, True)
            one_pass(R - 1, False)

        def ahead(i, u, n, more, step, between=None):
            if u + n < UN:
                step(i, u + n)
            elif more:
                if u + n == UN and between:
                    between()
                step(i + 1, u + n - UN)

        @block.sync
        def _(sp):
            for dst, src in ((k.outs["rows"], z[:, Z_KS:Z_GATE, :]),
                             (k.outs["win_k"][:, :, 0:WINDOW - L], k.ins["win_k"][:, :, L:WINDOW]),
                             (k.outs["win_v"][:, 0:WINDOW - L, :], k.ins["win_v"][:, L:WINDOW, :])):
                sp.dma_start(dst, src).then_inc(stored, 16)
            sp.wait_ge(stored, 3 * 16)

        @block.tensor
        def _(pe):
            pe.wait_ge(gates_on, 1)
            for t in range(QT):
                last = pe.transpose(k.ps[:, t // 4, (t % 4) * P:(t % 4 + 1) * P], gate_x[:, t * P:(t + 1) * P], c["ident"][:, :])
            last.then_inc(gates_turned, 1)
            pe.wait_ge(gates_read, 1)
            pe.wait_ge(pair_ready, 1)

            def score(i, u):
                t, g = units[u]
                rows = slice(g * HD, (g + 1) * HD)
                w_sel, off = extent(t)
                pe.wait_ge(biased, i * UN + u + 1)
                lhs = q[rows, t * P:(t + 1) * P]
                for a in range(0, w_sel, 512):
                    b_ = min(a + 512, w_sel)
                    pe.matmul(S_SEL[:, a:b_], lhs, z[rows, Z_KS, a:b_], start=True, stop=True)
                for a, b_ in ((off, 512), (512, WK)):
                    if a < b_:
                        pe.matmul(S_WIN[:, a:b_], lhs, z[rows, Z_KW, (t - 4) * P + a:(t - 4) * P + b_], start=True, stop=True)
                pe.matmul(S_CMP, lhs, comp_k[rows, B, 0:NCP], start=True, stop=True).then_inc(scored, 1)

            for u in range(AHEAD):
                score(0, u)

            def one_pass(i, more):
                for u, (t, g) in enumerate(units):
                    ahead(i, u, AHEAD, more, score, lambda: pe.wait_ge(pair_ready, i + 2))
                    pe.wait_ge(scaled, i * UN + u + 1)
                    groups = turns(t)
                    for n in range(len(groups) + 1):
                        if n < len(groups):
                            at = banks_before[u] + n
                            pe.wait_ge(copied, i * BANKS + (at + 1))
                            for s, (what, col, w, tile) in enumerate(groups[n]):
                                src = {"s": ls, "w": lw, "c": lc}[what]
                                last = pe.transpose(k.ps[0:w, 4 + at % 2, s * P:(s + 1) * P], src[:, u % SLOTS, col:col + w], c["ident"][:, :])
                            last.then_inc(turned, 1)
                        if n >= 1:
                            at = banks_before[u] + n - 1
                            pe.wait_ge(copied, i * BANKS + (at + 3))
                            if n == 1:
                                pe.wait_ge(placed, i * UN + u + 1)
                            for s, (what, col, w, tile) in enumerate(groups[n - 1]):
                                values = {"s": vals[:, 0, tile, g * HD:(g + 1) * HD],
                                          "w": vals[:, 1, tile, g * HD:(g + 1) * HD],
                                          "c": comp_v[0:NCP, B, g * HD:(g + 1) * HD]}[what]
                                last = pe.matmul(out(u), values, pt[0:w, at % 4, s * P:(s + 1) * P],
                                                 start=n == 1 and s == 0, stop=what == "c")
                    last.then_inc(valued, 1)
            passes(pe, one_pass)

        @block.vector
        def _(dve):
            dve.sem_inc(biased, 1)
            dve.wait_ge(gates_turned, 1)
            for j in range(3):
                last = dve.tensor_copy(gates[:, :, j, :], k.ps[:, 0:2, :].rearrange("p b (t n) -> p (b t) n", t=4)[:, :, 32 * j:32 * j + H])
            last.then_inc(gates_read, 1)
            dve.drain()

            def prepare(i):
                dve.tensor_copy(q[:], z[:, i, 0:SEQ])
                for g in range(G):
                    h = i + g * R
                    b31 = k.near_bias[:, h, 0:1]
                    table = k.near_bias[:, h, :]
                    dve.tensor_copy(far[:, g, 0:SEQ - 256], b31.broadcast_to([P, SEQ - 256]))
                    dve.tensor_copy(far[:, g, SEQ - 256:SEQ], table)
                    dve.tensor_copy(win[:, g, P:WK - 256], b31.broadcast_to([P, WK - 256 - P]))
                    dve.tensor_copy(win[:, g, WK - 256:WK], table)
                    dve.tensor_scalar(win[:, g, 0:P], c["edge_mask"][:, :], b31, None, ALU.add)
                    dve.tensor_copy(cbias[:, g, :], k.block_bias[:, h, :])
                dve.drain().then_inc(pair_ready, 1)

            def logits(i, u):
                t, g = units[u]
                s = u % SLOTS
                w, off = extent(t)
                wait_apart(k, dve, scored, i * UN + (u + 1))
                if u >= SLOTS or not isinstance(i, int):
                    wait_apart(k, dve, valued, i * UN + (u + 1 - SLOTS))
                dve.tensor_tensor_reduce(ls[:, s, 0:w], S_SEL[:, 0:w], far[:, g, SEQ - w:SEQ], 1.0, LOWEST, ALU.add, ALU.max, mx[:, s, 0:1])
                dve.tensor_tensor_reduce(lw[:, s, off:WK], S_WIN[:, off:WK], win[:, g, off:WK], 1.0, LOWEST, ALU.add, ALU.max, mx[:, s, 1:2])
                dve.tensor_tensor_reduce(lc[:, s, :], S_CMP, cbias[:, g, 16 - 2 * t:32 - 2 * t], 1.0, LOWEST, ALU.add, ALU.max, mx[:, s, 2:3])
                dve.drain()
                dve.tensor_scalar(nmx[:, s, 0:3], mx[:, s, 0:3], -1.0, None, ALU.mult).then_inc(biased, 1)

            def weigh(i, u):
                t, g = units[u]
                s = u % SLOTS
                dve.wait_ge(exped, i * UN + (u + 1))
                dve.reciprocal(coef[:, s, 0:3], sums[:, s, 0:3])
                dve.drain()
                for col, j in ((0, 1), (1, 2), (2, 0)):
                    dve.tensor_tensor(coef[:, s, col:col + 1], coef[:, s, col:col + 1], gates[:, t, j, bass.ds(i + g * R, 1)], ALU.mult)
                dve.drain()
                dve.scalar_tensor_tensor(out=lc[:, s, :], in0=lc[:, s, :], scalar=coef[:, s, 2:3], in1=c["block_mask"][:, 16 - 2 * t:32 - 2 * t],
                                         op0=ALU.mult, op1=ALU.mult)
                w, off = extent(t)
                dve.tensor_scalar(ls[:, s, 0:w], ls[:, s, 0:w], coef[:, s, 0:1], None, ALU.mult)
                dve.tensor_scalar(lw[:, s, off:WK], lw[:, s, off:WK], coef[:, s, 1:2], None, ALU.mult).then_inc(scaled, 1)

            prepare(0)
            for u in range(AHEAD):
                logits(0, u)
                if u:
                    weigh(0, u - 1)

            def one_pass(i, more):
                for u in range(UN):
                    ahead(i, u, AHEAD, more, logits)
                    if more and u + AHEAD == UN - 1:
                        prepare(i + 1)
                    ahead(i, u, AHEAD - 1, more, weigh)
            passes(dve, one_pass)

        @block.gpsimd
        def _(pool):
            pool.wait_ge(gates_on, 1)
            pool.tensor_copy(zs[:, :, :], z[:, :, SEQ:T])

        @block.scalar
        def _(act):
            act.activation(gate_x, gate_x, ACT.Sigmoid).then_inc(gates_on, 1)
            act.sem_inc(copied, 2)
            act.sem_inc(placed, 2)

            def exponentials(i, u):
                s = u % SLOTS
                w, off = extent(units[u][0])
                act.wait_ge(biased, i * UN + (u + 2))
                act.activation(ls[:, s, 0:w], ls[:, s, 0:w], ACT.Exp, bias=nmx[:, s, 0:1], accum_out=sums[:, s, 0:1])
                act.activation(lw[:, s, off:WK], lw[:, s, off:WK], ACT.Exp, bias=nmx[:, s, 1:2], accum_out=sums[:, s, 1:2])
                act.activation(lc[:, s, :], lc[:, s, :], ACT.Exp, bias=nmx[:, s, 2:3], accum_out=sums[:, s, 2:3])
                act.drain().then_inc(exped, 1)

            def place(i, u):
                t, g = units[u]
                act.wait_ge(valued, i * UN + (u + 1))
                act.activation(mix[g * HD:(g + 1) * HD, i, t * P:(t + 1) * P], out(u), ACT.Copy).then_inc(placed, 1)

            for u in range(AHEAD - 1):
                exponentials(0, u)

            def one_pass(i, more):
                for u, (t, g) in enumerate(units):
                    ahead(i, u, AHEAD - 1, more, exponentials)
                    if u:
                        place(i, u - 1)
                    for n, group in enumerate(turns(t)):
                        at = banks_before[u] + n
                        act.wait_ge(turned, i * BANKS + (at + 1))
                        full = sum(x[0] != "c" for x in group) * P
                        if full:
                            last = act.activation(pt[:, at % 4, 0:full], k.ps[:, 4 + at % 2, 0:full], ACT.Copy)
                        if full < len(group) * P:
                            last = act.activation(pt[0:NCP, at % 4, full:full + P], k.ps[0:NCP, 4 + at % 2, full:full + P], ACT.Copy)
                        last.then_inc(copied, 1)
                place(i, UN - 1)
            passes(act, one_pass)


def sample_attention(k, zs, comp_k, comp_v, mix):
    nc, c = k.nc, k.cst
    WIN = WINDOW + L
    KEYS = PAST + L
    KCH = PAGES + 1
    groups = [list(range(a, min(a + 4, KCH))) for a in range(0, KCH, 4)]
    with ExitStack() as ctx:
        kv = k.sb(ctx, "past_rows", [P, 2, PAGES, 2 * P])
        wk = k.sb(ctx, "window_keys", [P, 2, WINDOW])
        wv = k.sb(ctx, "window_values", [P, 2, 4, P])
        qd = k.sb(ctx, "block_diagonal_queries", [P, ROWS])
        new = k.sb(ctx, "new_rows", [P, 4, L])
        newv = k.sb(ctx, "new_values", [L, 2, P])
        ls = k.sb(ctx, "row_logits", [ROWS, KEYS])
        lw = k.sb(ctx, "row_window_logits", [ROWS, WIN])
        lc = k.sb(ctx, "row_block_logits", [ROWS, NCS])
        mx = k.sb(ctx, "row_maxima", [ROWS, 16])
        mm = k.sb(ctx, "row_max", [ROWS, 4])
        nm = k.sb(ctx, "row_neg_max", [ROWS, 4])
        sums = k.sb(ctx, "row_sums", [ROWS, 4])
        halves = k.sb(ctx, "row_part_sums", [ROWS, 2])
        rs = k.sb(ctx, "row_rsums", [ROWS, 4])
        co = k.sb(ctx, "row_coef", [ROWS, 4])
        imp = k.sb(ctx, "importance", [G * L, 4, NBS])
        top = k.sb(ctx, "top8", [G * L, 2, 8])
        neg = k.sb(ctx, "unselected", [G * L, NBS])
        negr = k.sb(ctx, "row_unselected", [ROWS, NBS])
        pt = k.sb(ctx, "row_probs_turned", [P, 4, 4, ROWS])
        gd = k.sb(ctx, "gate_diagonals", [P, H, L])
        os_ = k.sb(ctx, "row_out", [ROWS, P])
        s_kv = [k.sem(ctx, f"past_loaded{s}") for s in range(2)]
        s_new = k.sem(ctx, "new_rows_copied")
        s_newt = k.sem(ctx, "new_values_turned")
        s_newv = k.sem(ctx, "new_values_copied")
        s_cs = k.sem(ctx, "block_scores")
        s_cb = k.sem(ctx, "block_logits")
        s_ce = k.sem(ctx, "block_probs")
        s_cn = k.sem(ctx, "block_probs_normed")
        s_imp = k.sem(ctx, "importance_summed")
        s_sel = k.sem(ctx, "blocks_selected")
        s_neg = k.sem(ctx, "mask_spread")
        s_negc = k.sem(ctx, "mask_copied")
        s_ks = k.sem(ctx, "key_scores")
        s_kb = k.sem(ctx, "key_logits")
        s_wb = k.sem(ctx, "window_logits")
        s_we = k.sem(ctx, "window_probs")
        s_lm = k.sem(ctx, "logit_max")
        s_e = k.sem(ctx, "key_probs")
        s_t = k.sem(ctx, "turned")
        s_tc = [k.sem(ctx, f"turned_copied{x}") for x in range(2)]
        s_o = k.sem(ctx, "outputs_summed")
        s_os = k.sem(ctx, "outputs_combined")
        s_ot = k.sem(ctx, "outputs_turned")
        s_mix = k.sem(ctx, "outputs_placed")
        block = ctx.enter_context(nc.Block())

        turn_list = [[("w", a * P, P, KCH + 1 + a) for a in range(4)],
                     [("w", 4 * P, L, KCH + 5), ("c", 0, NCS, KCH)]]
        turn_list += [[("s", a * P, P if a < PAGES else L, a) for a in g] for g in groups]
        if len(turn_list) % 2:
            turn_list[2:4] = [turn_list[2][:2], turn_list[2][2:], turn_list[3]]
        NTURN = len(turn_list)
        assert NTURN % 2 == 0
        SECOND = next(n for n, g in enumerate(turn_list) if n >= 2 and g[0][1] >= KEYS // 4)
        cut = turn_list[SECOND][0][1]
        HALVES = ((0, cut), (cut, KEYS - cut))
        OC, OS, OW = (k.ps[0:ROWS, 7, x * P:(x + 1) * P] for x in range(3))
        NKS = 9

        def tokens(b):
            return bass.ds(b * L + SEQ, L)

        @block.sync
        def _(sp):
            def load(b, j, s):
                wait_apart(k, sp, s_o, b + 1)
                sp.dma_start(wk[:, s, :], k.ins["win_k"][b]).then_inc(s_kv[s], 16)
                sp.dma_start(wv[:, s, :, :], k.ins["win_v"][b].rearrange("(a p) n -> p a n", p=P)).then_inc(s_kv[s], 16)
                load_pages(k, sp, b, k.ins["kv_pages"], kv[:, s, :, :], s_kv[s])
            pairs(sp, B, load)

        @block.tensor
        def _(pe):
            ident = c["ident"]
            pe.sem_inc(s_o, 2)

            def sample(b, j, slot):
                pe.wait_ge(s_new, b + 1)
                pe.transpose(k.ps[0:L, 2, 0:P], new[:, 2, :], ident[:, :])
                pe.transpose(k.ps[0:L, 2, P:2 * P], new[:, 3, :], ident[:, :]).then_inc(s_newt, 1)
                pe.matmul(k.ps[0:ROWS, 3, 0:NCS], qd[:, :], comp_k[:, b, :], start=True, stop=True)
                pe.matmul(k.ps[0:ROWS, 3, 256:260], gd[:, :, :].rearrange("p h q -> p (h q)"), c["branch"][:, :], start=True, stop=True)
                pe.wait_ge(s_kv[slot], (j + 1) * (16 * (PAGES + 2)))
                pe.matmul(k.ps[0:ROWS, 6, 0:WINDOW], qd[:, :], wk[:, slot, :], start=True, stop=True)
                pe.matmul(k.ps[0:ROWS, 3, 128:128 + L], qd[:, :], new[:, 1, :], start=True, stop=True).then_inc(s_cs, 1)
                pe.wait_ge(s_cn, b + 1)
                pe.matmul(k.ps[0:G * L, 2, 256:256 + NCS], c["sum_heads"][:, :], lc[:, :], start=True, stop=True).then_inc(s_imp, 1)
                pe.wait_ge(s_sel, b + 1)
                pe.matmul(k.ps[0:ROWS, 2, 384:384 + NBS], c["spread_heads"][:, :], neg[:, :], start=True, stop=True).then_inc(s_neg, 1)
                for n in range(NKS):
                    pe.wait_ge(s_kb, b * NKS + (n + 1))
                    if n < NKS - 1:
                        last = pe.matmul(k.ps[0:ROWS, n % 2, :], qd[:, :], kv[:, slot, 4 * n:4 * n + 4, 0:P], start=True, stop=True)
                    else:
                        last = pe.matmul(k.ps[0:ROWS, n % 2, 0:L], qd[:, :], new[:, 0, :], start=True, stop=True)
                    last.then_inc(s_ks, 1)
                pe.wait_ge(s_os, b + 1)
                for n in range(NTURN + 1):
                    if n < NTURN:
                        if n == 0:
                            pe.wait_ge(s_we, b + 1)
                        if n == 2:
                            pe.wait_ge(s_e, b * len(HALVES) + 1)
                        if n == SECOND:
                            pe.wait_ge(s_e, b * len(HALVES) + 2)
                        pe.wait_ge(s_tc[n % 2], b * (NTURN // 2) + (n // 2 + 1))
                        for s, (what, col, w, tile) in enumerate(turn_list[n]):
                            src = {"s": ls, "w": lw, "c": lc}[what]
                            last = pe.transpose(k.ps[0:w, 4 + n % 2, s * ROWS:(s + 1) * ROWS], src[:, col:col + w], ident[0:ROWS, 0:ROWS])
                        last.then_inc(s_t, 1)
                    if n >= 1:
                        pe.wait_ge(s_tc[(n - 1) % 2], b * (NTURN // 2) + ((n - 1) // 2 + 2))
                        if n == 1:
                            pe.wait_ge(s_newv, b + 1)
                        for s, (what, col, w, tile) in enumerate(turn_list[n - 1]):
                            if what == "c":
                                o, mv, st, sp_ = OC, comp_v[:, b, :], True, True
                            elif what == "w":
                                a = tile - KCH - 1
                                o, st, sp_ = OW, a == 0, a == 4
                                mv = wv[:, slot, a, :] if a < 4 else newv[:, 1, :]
                            else:
                                o, st, sp_ = OS, tile == 0, tile == PAGES
                                mv = kv[:, slot, tile, P:2 * P] if tile < PAGES else newv[:, 0, :]
                            last = pe.matmul(o, pt[0:w, (n - 1) % 4, s, :], mv, start=st, stop=sp_)
                last.then_inc(s_o, 1)
                pe.wait_ge(s_os, b + 2)
                pe.wait_ge(s_mix, b + 1)
                pe.transpose(k.ps[:, 3, 384:384 + ROWS], os_[:, :], ident[0:ROWS, 0:ROWS]).then_inc(s_ot, 1)
            pairs(pe, B, sample)

        def copies(eng, b, parity):
            for n in range(parity, NTURN, 2):
                eng.wait_ge(s_t, b * NTURN + (n + 1))
                group = turn_list[n]
                runs = []
                for s, (what, col, w, tile) in enumerate(group):
                    if runs and runs[-1][2] == w and runs[-1][1] + runs[-1][3] == tile:
                        runs[-1][3] += 1
                    else:
                        runs.append([s, tile, w, 1])
                for s, tile, w, count in runs:
                    dst = pt[0:w, n % 4, s:s + count, :]
                    src = k.ps[0:w, 4 + n % 2, s * ROWS:(s + count) * ROWS].rearrange("p (a n) -> p a n", a=count)
                    if eng is k.nc.scalar:
                        last = eng.activation(dst, src, ACT.Copy)
                    else:
                        last = eng.tensor_copy(dst, src)
                last.then_inc(s_tc[n % 2], 1)

        @block.scalar
        def _(act):
            act.sem_inc(s_tc[1], 1)
            with act.Fori(0, B) as b:
                act.wait_ge(s_cb, b + 1)
                act.activation(lc[:, :], lc[:, :], ACT.Exp, bias=nm[:, 0:1], accum_out=sums[:, 0:1]).then_inc(s_ce, 1)
                act.wait_ge(s_wb, b + 1)
                act.activation(lw[:, :], lw[:, :], ACT.Exp, bias=nm[:, 2:3], accum_out=sums[:, 2:3]).then_inc(s_we, 1)
                act.wait_ge(s_lm, b + 1)
                for x, (a, w) in enumerate(HALVES):
                    act.activation(ls[:, a:a + w], ls[:, a:a + w], ACT.Exp, bias=nm[:, 1:2], accum_out=halves[:, x:x + 1]).then_inc(s_e, 1)
                copies(act, b, 1)

        @block.vector
        def _(dve):
            dve.sem_inc(s_tc[0], 1)
            dve.sem_inc(s_kb, 2)
            dve.sem_inc(s_os, 1)
            dve.sem_inc(s_mix, 1)
            dve.memset(qd[:], 0.0)
            dve.memset(imp[:], FORCED)
            dve.drain()
            with dve.Fori(0, B) as b:
                for g in range(G):
                    rows = slice(g * HD, (g + 1) * HD)
                    dve.tensor_copy(qd[rows, g * GR:(g + 1) * GR].rearrange("p (r q) -> p r q", r=R), zs[rows, 0:R, bass.ds(b * L, L)])
                for n, ch in enumerate((Z_KS, Z_KW, Z_VS, Z_VW)):
                    dve.tensor_copy(new[:, n, :], zs[:, ch, bass.ds(b * L, L)])
                dve.tensor_tensor(gd[:, :, :], c["diag"][:, :].rearrange("p (h o) -> p h o", o=1).broadcast_to([P, H, L]),
                                  zs[:, bass.ds(Z_GATE, 1), bass.ds(b * L, L)].broadcast_to([P, H, L]), ALU.mult)
                dve.drain().then_inc(s_new, 1)
                dve.wait_ge(s_newt, b + 1)
                dve.tensor_copy(newv[:, :, :], k.ps[0:L, 2, 0:2 * P].rearrange("p (a n) -> p a n", a=2)).then_inc(s_newv, 1)
                wait_apart(k, dve, s_cs, b + 1)
                dve.tensor_tensor_reduce(lc[:, :], k.ps[0:ROWS, 3, 0:NCS], k.row_blocks[:, :], 1.0, LOWEST, ALU.add, ALU.max, mm[:, 0:1])
                dve.drain()
                dve.tensor_scalar(nm[:, 0:1], mm[:, 0:1], -1.0, None, ALU.mult).then_inc(s_cb, 1)
                dve.tensor_tensor_reduce(lw[:, 0:WINDOW], k.ps[0:ROWS, 6, 0:WINDOW], k.row_window[:, 0:WINDOW], 1.0, LOWEST, ALU.add, ALU.max, mx[:, 12:13])
                dve.tensor_tensor_reduce(lw[:, WINDOW:WIN], k.ps[0:ROWS, 3, 128:128 + L], k.row_window[:, WINDOW:WIN], 1.0, LOWEST, ALU.add, ALU.max, mx[:, 13:14])
                dve.tensor_copy(co[:, 0:3], k.ps[0:ROWS, 3, 256:259])
                dve.drain()
                dve.tensor_tensor(mm[:, 2:3], mx[:, 12:13], mx[:, 13:14], ALU.max)
                dve.drain()
                dve.tensor_scalar(nm[:, 2:3], mm[:, 2:3], -1.0, None, ALU.mult).then_inc(s_wb, 1)
                dve.wait_ge(s_ce, b + 1)
                dve.reciprocal(rs[:, 0:1], sums[:, 0:1])
                dve.drain()
                dve.tensor_scalar(lc[:, :], lc[:, :], rs[:, 0:1], None, ALU.mult).then_inc(s_cn, 1)
                dve.wait_ge(s_imp, b + 1)
                dve.tensor_copy(imp[:, 0, 1:NCS - 1], k.ps[0:G * L, 2, 257:256 + NCS - 1])
                dve.drain()
                for step in range(2):
                    dve.max(top[:, step, :], imp[:, step, :])
                    dve.drain()
                    dve.match_replace(imp[:, step + 1, :], top[:, step, :], imp[:, step, :], -5.0)
                    dve.drain()
                dve.tensor_scalar(neg[:, :], imp[:, 2, :], -1.0, NEG, ALU.is_ge, ALU.mult).then_inc(s_sel, 1)
                dve.wait_ge(s_neg, b + 1)
                dve.tensor_tensor(negr[:, :], k.ps[0:ROWS, 2, 384:384 + NBS], k.row_select[:, :], ALU.add)
                dve.drain()
                for n in range(NKS):
                    wait_apart(k, dve, s_ks, b * NKS + (n + 1))
                    if n < NKS - 2:
                        dve.tensor_tensor_reduce(ls[:, n * 512:(n + 1) * 512].rearrange("p (a n) -> p a n", n=CB),
                                                 k.ps[0:ROWS, n % 2, :].rearrange("p (a n) -> p a n", n=CB),
                                                 negr[:, 8 * n:8 * n + 8].rearrange("p (a o) -> p a o", o=1).broadcast_to([ROWS, 8, CB]),
                                                 1.0, LOWEST, ALU.add, ALU.max, mx[:, n:n + 1]).then_inc(s_kb, 1)
                    elif n == NKS - 2:
                        dve.tensor_tensor(ls[:, n * 512:(n + 1) * 512].rearrange("p (a n) -> p a n", n=CB),
                                          k.ps[0:ROWS, n % 2, :].rearrange("p (a n) -> p a n", n=CB),
                                          negr[:, 8 * n:8 * n + 8].rearrange("p (a o) -> p a o", o=1).broadcast_to([ROWS, 8, CB]),
                                          ALU.add).then_inc(s_kb, 1)
                    else:
                        dve.tensor_scalar(ls[:, PAST:KEYS], k.ps[0:ROWS, n % 2, 0:L], negr[:, NCS:NBS], None, ALU.add).then_inc(s_kb, 1)
                dve.drain()
                dve.tensor_tensor(ls[:, KEYS - TAIL:KEYS], ls[:, KEYS - TAIL:KEYS], k.row_tail[:, :], ALU.add)
                dve.drain()
                dve.tensor_reduce(mx[:, 7:8], ls[:, (NKS - 2) * 512:KEYS], X, ALU.max)
                dve.drain()
                dve.tensor_reduce(mm[:, 1:2], mx[:, 0:8], X, ALU.max)
                dve.drain()
                dve.tensor_scalar(nm[:, 1:2], mm[:, 1:2], -1.0, None, ALU.mult).then_inc(s_lm, 1)
                copies(dve, b, 0)
                dve.wait_ge(s_e, b * len(HALVES) + 2)
                dve.tensor_tensor(sums[:, 1:2], halves[:, 0:1], halves[:, 1:2], ALU.add)
                dve.drain()
                dve.wait_ge(s_o, b + 3)
                dve.reciprocal(rs[:, 1:3], sums[:, 1:3])
                dve.drain()
                dve.tensor_tensor(co[:, 1:3], co[:, 1:3], rs[:, 1:3], ALU.mult)
                dve.drain()
                dve.tensor_scalar(os_[:, :], OC, co[:, 0:1], None, ALU.mult)
                dve.drain()
                dve.scalar_tensor_tensor(out=os_[:, :], in0=OS, scalar=co[:, 1:2], in1=os_[:, :], op0=ALU.mult, op1=ALU.add)
                dve.drain()
                dve.scalar_tensor_tensor(out=os_[:, :], in0=OW, scalar=co[:, 2:3], in1=os_[:, :], op0=ALU.mult, op1=ALU.add).then_inc(s_os, 1)
                dve.wait_ge(s_ot, b + 1)
                for g in range(G):
                    rows = slice(g * HD, (g + 1) * HD)
                    last = dve.tensor_copy(mix[rows, 0:R, tokens(b)],
                                           k.ps[rows, 3, 384 + g * GR:384 + (g + 1) * GR].rearrange("p (r q) -> p r q", r=R))
                last.then_inc(s_mix, 1)


def memory_attention(k, layer, xq, mix_out):
    nc, c = k.nc, k.cst
    NB4 = 4
    STEPS = QT + B // NB4
    with ExitStack() as ctx:
        keys = k.sb(ctx, "sample_mem_keys", [P, B, 2, NMEM])
        vals = k.sb(ctx, "sample_mem_values", [P, B, 2, 2 * P])
        qd = k.sb(ctx, "mem_queries_diagonal", [P, 2, B, XH, L])
        pr = k.sb(ctx, "mem_probs", [P, 2, XH * NMEM])
        mx = k.sb(ctx, "mem_maxima", [P, 2, XH])
        sums = k.sb(ctx, "mem_sums", [P, 2, XH])
        rs = k.sb(ctx, "mem_rsums", [P, 2, XH])
        pt = k.sb(ctx, "mem_probs_turned", [P, 2, 512])
        o = k.sb(ctx, "mem_out", [P, 2 * P])
        loaded = k.sem(ctx, "mem_rows_loaded")
        placed = k.sem(ctx, "mem_queries_placed")
        scored = k.sem(ctx, "mem_scored")
        maxed = k.sem(ctx, "mem_maxed")
        exped = k.sem(ctx, "mem_exped")
        turned = k.sem(ctx, "mem_turned")
        copied = k.sem(ctx, "mem_copied")
        valued = k.sem(ctx, "mem_valued")
        normed = k.sem(ctx, "mem_normed")
        back = k.sem(ctx, "mem_turned_back")
        stored = k.sem(ctx, "mem_mixed")
        block = ctx.enter_context(nc.Block())

        @block.sync
        def _(sp):
            sp.dma_start(keys[:], k.ins["cmem_k"][layer].rearrange("b p n -> p b n").rearrange("p b (c n) -> p b c n", c=2)).then_inc(loaded, 16)
            sp.dma_start(vals[:], k.ins["cmem_v"][layer].rearrange("b p n -> p b n").rearrange("p b (c n) -> p b c n", c=2)).then_inc(loaded, 16)

        def score_view(n):
            return k.ps[:, 2 * (n % 2):2 * (n % 2) + 2, :].rearrange("p b n -> p (b n)")

        def head_at(y):
            return 2 * (y % 2) + y // 2

        def n_turn(n):
            return 2 if n < QT else 1

        turn_before = [0]
        for n in range(STEPS):
            turn_before.append(turn_before[-1] + n_turn(n))

        @block.tensor
        def _(pe):
            pe.wait_ge(placed, 1)
            pe.wait_ge(loaded, 32)

            def score(n):
                if n >= 2:
                    pe.wait_ge(exped, n - 1)
                sv = score_view(n)
                if n < QT:
                    for y in range(XH):
                        h = head_at(y)
                        rows = slice((h % 2) * HD, (h % 2 + 1) * HD)
                        last = pe.matmul(sv[:, y * NMEM:(y + 1) * NMEM], xq[rows, h // 2, n * P:(n + 1) * P],
                                         k.mem_k[rows, layer, h // 2, :], start=True, stop=True)
                else:
                    for x in range(NB4):
                        b = (n - QT) * NB4 + x
                        for ch in range(2):
                            last = pe.matmul(sv[32 * x:32 * x + 32, 0:NMEM], qd[:, ch, b, :, :].rearrange("p h q -> p (h q)"),
                                             keys[:, b, ch, :], start=ch == 0, stop=ch == 1)
                last.then_inc(scored, 1)
            score(0)
            for n in range(STEPS):
                if n + 1 < STEPS:
                    score(n + 1)
                pe.wait_ge(exped, n + 1)
                for x in range(n_turn(n)):
                    at = turn_before[n] + x
                    if at >= 1:
                        pe.wait_ge(copied, at)
                    cols = 4 if n < QT else 2
                    for y in range(cols):
                        last = pe.transpose(k.ps[:, 4, y * P:(y + 1) * P], pr[:, n % 2, (4 * x + y) * P:(4 * x + y + 1) * P], c["ident"][:, :])
                    last.then_inc(turned, 1)
                    pe.wait_ge(copied, at + 1)
                    if x == 0 and n >= 1:
                        pe.wait_ge(normed, n)
                    if n < QT:
                        for hh in range(2):
                            h = head_at(2 * x + hh)
                            for mt in range(2):
                                last = pe.matmul(k.ps[:, 5, h * HD:(h + 1) * HD], pt[:, at % 2, (2 * hh + mt) * P:(2 * hh + mt + 1) * P],
                                                 k.mem_v[:, layer, mt, h * HD:(h + 1) * HD], start=mt == 0, stop=mt == 1)
                    else:
                        for xx in range(NB4):
                            b = (n - QT) * NB4 + xx
                            for mt in range(2):
                                last = pe.matmul(k.ps[32 * xx:32 * xx + 32, 5, 0:2 * P], pt[:, at % 2, mt * P + 32 * xx:mt * P + 32 * xx + 32],
                                                 vals[:, b, mt, :], start=mt == 0, stop=mt == 1)
                last.then_inc(valued, 1)
                pe.wait_ge(normed, n + 1)
                if n >= 1:
                    pe.wait_ge(stored, n)
                for ch in range(2):
                    last = pe.transpose(k.ps[:, 6, ch * P:(ch + 1) * P], o[:, ch * P:(ch + 1) * P], c["ident"][:, :])
                last.then_inc(back, 1)

        @block.vector
        def _(dve):
            dve.memset(qd[:], 0.0)
            dve.drain()
            for h in range(XH):
                rows = slice((h % 2) * HD, (h % 2 + 1) * HD)
                dve.tensor_copy(qd[rows, h // 2, :, h, :], samples(xq[rows, h // 2, :]))
            dve.drain().then_inc(placed, 1)

            def maximum(n):
                dve.wait_ge(scored, n + 1)
                heads = XH if n < QT else 1
                if n >= 2:
                    dve.wait_ge(exped, n - 1)
                dve.tensor_reduce(mx[:, n % 2, 0:heads], score_view(n)[:, 0:heads * NMEM].rearrange("p (h n) -> p h n", h=heads), X, ALU.max)
                dve.drain()
                dve.tensor_scalar(mx[:, n % 2, 0:heads], mx[:, n % 2, 0:heads], -1.0, None, ALU.mult).then_inc(maxed, 1)
            maximum(0)
            for n in range(STEPS):
                heads = XH if n < QT else 1
                if n + 1 < STEPS:
                    maximum(n + 1)
                dve.wait_ge(exped, n + 1)
                dve.reciprocal(rs[:, n % 2, 0:heads], sums[:, n % 2, 0:heads])
                for x in range(n_turn(n)):
                    at = turn_before[n] + x
                    w = 512 if n < QT else 256
                    dve.wait_ge(turned, at + 1)
                    dve.tensor_copy(pt[:, at % 2, 0:w], k.ps[:, 4, 0:w]).then_inc(copied, 1)
                dve.drain()
                dve.wait_ge(valued, n + 1)
                if n >= 1:
                    dve.wait_ge(back, n)
                if n < QT:
                    dve.tensor_tensor(o[:, :].rearrange("p (a b d) -> p a b d", a=2, b=2), k.ps[:, 5, 0:2 * P].rearrange("p (a b d) -> p a b d", a=2, b=2),
                                      rs[:, n % 2, :].rearrange("p (b a o) -> p a b o", a=2, o=1).broadcast_to([P, 2, 2, HD]), ALU.mult).then_inc(normed, 1)
                else:
                    dve.tensor_scalar(o[:, :], k.ps[:, 5, 0:2 * P], rs[:, n % 2, 0:1], None, ALU.mult).then_inc(normed, 1)

        @block.scalar
        def _(act):
            def place(n):
                act.wait_ge(back, n + 1)
                if n < QT:
                    last = act.activation(mix_out[:, :, n * P:(n + 1) * P], k.ps[:, 6, 0:2 * P].rearrange("p (c n) -> p c n", c=2), ACT.Copy)
                else:
                    for h in range(XH):
                        rows = slice((h % 2) * HD, (h % 2 + 1) * HD)
                        src = k.ps[rows, 6, (h // 2) * P:(h // 2 + 1) * P].rearrange("p (b h q) -> p b h q", b=NB4, h=XH)[:, :, h, :]
                        b0 = (n - QT) * NB4
                        last = act.activation(samples(mix_out[rows, h // 2, :])[:, b0:b0 + NB4, :], src, ACT.Copy)
                last.then_inc(stored, 1)

            for n in range(STEPS):
                heads = XH if n < QT else 1
                act.wait_ge(maxed, n + 1)
                if n >= 2:
                    act.wait_ge(normed, n - 1)
                for h in range(heads):
                    last = act.activation(pr[:, n % 2, h * NMEM:(h + 1) * NMEM], score_view(n)[:, h * NMEM:(h + 1) * NMEM],
                                          ACT.Exp, bias=mx[:, n % 2, h:h + 1], accum_out=sums[:, n % 2, h:h + 1])
                last.then_inc(exped, 1)
                if n >= 1:
                    place(n - 1)
            place(STEPS - 1)


def pool_mixer(k, z, mix):
    nc, c = k.nc, k.cst
    EP, ES = PST + SEQ, PST + L
    W = EP + B * ES
    with ExitStack() as ctx:
        load_constants(k, ctx, POOLING)
        ext = k.sb(ctx, "pool_ext", [PCH, 2, W])
        sa = k.sb(ctx, "pool_sums_a", [PCH, W])
        sb_ = k.sb(ctx, "pool_sums_b", [PCH, W])
        state = k.sb(ctx, "pool_state", [PCH, NPC, B * PST])
        pooled = k.sb(ctx, "pooled", [PCH, NPC, T])
        tails = k.sb(ctx, "pool_tails", [PCH, NPC, PST * (1 + B)])
        w = k.sb(ctx, "pool_weights", [PCH, NPC, PG])
        loaded = k.sem(ctx, "pool_loaded")
        done = k.sem(ctx, "pooled_ready")
        multiplied = k.sem(ctx, "pool_multiplied")
        scaled = k.sem(ctx, "pool_scaled")
        stored = k.sem(ctx, "pool_stored")
        block = ctx.enter_context(nc.Block())

        @block.sync
        def _(sp):
            sp.dma_start(state[:], k.ins["pool_state"]).then_inc(loaded, 16)
            sp.dma_start(w[:], k.ins["w_grp"]).then_inc(loaded, 16)
            sp.wait_ge(done, NPC)
            sp.dma_start(k.outs["pool"], tails[:]).then_inc(stored, 16)
            sp.wait_ge(stored, 16)

        def parts(buf, lo):
            s = buf[:, EP:W].rearrange("p (b n) -> p b n", b=B)
            return buf[:, lo:EP], s[:, :, lo:ES]

        @block.vector
        def _(dve):
            dve.wait_ge(loaded, 32)
            for ch in range(NPC):
                e = ext[:, ch % 2, :]
                pw = POOLW[ch // 2]
                ep, es = parts(e, 0)
                dve.memset(ep[:, 0:PST], 0.0)
                dve.tensor_copy(ep[:, PST:EP], z[0:PCH, ch, 0:SEQ])
                dve.tensor_copy(es[:, :, 0:PST], state[:, ch, :].rearrange("p (b n) -> p b n", b=B))
                dve.tensor_copy(es[:, :, PST:ES], samples(z[0:PCH, ch, :]))
                dve.drain()
                dve.tensor_copy(tails[:, ch, 0:PST], ep[:, SEQ:EP])
                dve.tensor_copy(tails[:, ch, PST:].rearrange("p (b n) -> p b n", b=B), es[:, :, L:ES])
                cur, span = e, 1
                while span < pw:
                    nxt = sa if cur is not sa else sb_
                    nxt_ap = nxt[:, :]
                    lo = 2 * span - 1
                    cp, cs = parts(cur if cur is e else cur[:, :], 0)
                    np_, ns = parts(nxt_ap, 0)
                    dve.tensor_tensor(np_[:, lo:EP], cp[:, lo:EP], cp[:, lo - span:EP - span], ALU.add)
                    dve.tensor_tensor(ns[:, :, lo:ES], cs[:, :, lo:ES], cs[:, :, lo - span:ES - span], ALU.add)
                    dve.drain()
                    cur, span = nxt, 2 * span
                cp, cs = parts(cur[:, :], 0)
                dve.tensor_tensor(cp[:, PST:PST + 16], cp[:, PST:PST + 16], c["pool_counts"][0:PCH, ch // 2, :], ALU.mult)
                dve.drain()
                dve.scalar_tensor_tensor(out=pooled[:, ch, 0:SEQ], in0=cp[:, PST:EP], scalar=1.0 / pw, in1=ep[:, PST:EP],
                                         op0=ALU.mult, op1=ALU.subtract)
                dve.scalar_tensor_tensor(out=samples(pooled[:, ch, :]), in0=cs[:, :, PST:ES], scalar=1.0 / pw, in1=es[:, :, PST:ES],
                                         op0=ALU.mult, op1=ALU.subtract)
                dve.drain().then_inc(done, 1)

        @block.tensor
        def _(pe):
            for m in range(NPC):
                g = m // 2
                pe.wait_ge(done, 2 * g + 2)
                if m >= 2:
                    pe.wait_ge(scaled, m - 1)
                for a, cols in NT:
                    for kk in range(2):
                        last = pe.matmul(bank_set(k, m % 2)[0:PCH, a:a + cols], w[:, 2 * g + kk, (m % 2) * PCH:(m % 2 + 1) * PCH],
                                         pooled[:, 2 * g + kk, a:a + cols], start=kk == 0, stop=kk == 1)
                last.then_inc(multiplied, 1)

        @block.scalar
        def _(act):
            for m in range(NPC):
                act.wait_ge(multiplied, m + 1)
                act.activation(mix[0:PCH, m, :], bank_set(k, m % 2)[0:PCH, :], ACT.Copy, scale=c["pool_scale"][0:PCH, m:m + 1]).then_inc(scaled, 1)


def conv_ffn(k, layer, xn, x):
    nc, c = k.nc, k.cst
    EP, ES = SEQ + 2, L + 2
    W = EP + B * ES
    most = max(PARTS)
    starts = [sum(PARTS[:p]) for p in range(len(PARTS))]

    def up_base(p):
        return 2 * starts[p] + p * KC

    def down_base(p):
        return 2 * starts[p] + 2 * PARTS[p] + p * KC + (2 if p + 1 < len(PARTS) else 0)

    with ExitStack() as ctx:
        for name in CONVOLUTION:
            k.cst[name] = k.sb(ctx, name, CONSTANTS[name])
        constants_loaded = k.sem(ctx, "conv_constants_loaded")
        gh = k.sb(ctx, "gated_high", [P, most, T], F32R)
        gl = k.sb(ctx, "gated_low", [P, most, T], F32R)
        tails = k.sb(ctx, "conv_tails", [P, 2 * FC, 2 * (1 + B)])
        ext = k.sb(ctx, "conv_ext", [P, 2, W])
        y = k.sb(ctx, "conv_out", [P, 2, T])
        w = Weights(k, ctx, "ffn", KC * P)
        taken = k.sem(ctx, "banks_taken")
        placed = k.sem(ctx, "products_placed")
        convolved = k.sem(ctx, "convolved")
        silued = k.sem(ctx, "silued")
        gated = k.sem(ctx, "gated")
        rounded = k.sem(ctx, "gated_rounded")
        finished = k.sem(ctx, "gated_split")
        stored = k.sem(ctx, "tails_stored")
        norm = Norm(k, ctx, x, xn, k.cst["g_ffn"][:, layer, :], T, (y[:, :, :], ext[:, 0, 0:T], ext[:, 1, 0:T]))
        block = ctx.enter_context(nc.Block())
        up = [(xn[0][:, kk, :], xn[1][:, kk, :]) for kk in range(KC)]

        def stream(eng, up_step, down_step, between=None):
            if between:
                up_step(0, 0, 0)
                between()
            for p, n in enumerate(PARTS):
                with eng.Fori(0 if p == 0 and not between else 1, n) as m:
                    up_step(p, m, up_base(p))
                if p + 1 < len(PARTS):
                    up_step(p + 1, 0, up_base(p) + 2 * n)
                with eng.Fori(0, KC // 2) as m:
                    down_step(p, m, n)

        @block.sync
        def _(sp):
            def up_step(p, m, base):
                for av in range(2):
                    w.load(sp, m * 2 + (base + av), av, k.ins["w_up"][layer, m + (starts[p] + av * FC)], KC * P)

            def down_step(p, m, n):
                for s in range(2):
                    w.load(sp, m * 2 + (down_base(p) + s), s,
                           k.ins["w_down"][layer, m * 2 + s, :, starts[p] * P:(starts[p] + n) * P], n * P)
            def constants():
                for name in CONVOLUTION:
                    sp.dma_start(c[name][:], k.ins[name]).then_inc(constants_loaded, 16)
            stream(sp, up_step, down_step, constants)
            sp.wait_ge(finished, FC + 1)
            sp.dma_start(k.outs["conv"][layer], tails[:]).then_inc(stored, 16)
            sp.wait_ge(stored, 16)

        @block.gpsimd
        def _(pool):
            pool.sem_inc(w.split, 2)

            def up_step(p, m, base):
                for av in range(2):
                    w.part(k, pool, m * 2 + (base + av), m + base // 2, av, KC * P)

            def down_step(p, m, n):
                for s in range(2):
                    w.part(k, pool, m * 2 + (down_base(p) + s), m + down_base(p) // 2, s, n * P)
            stream(pool, up_step, down_step, lambda: norm.pool(pool))

        @block.tensor
        def _(pe):
            pe.sem_inc(w.multiplied, 2)
            norm.pe(pe)

            def up_step(p, m, base):
                for av in range(2):
                    t = m * 2 + (base + av)
                    pe.wait_ge(taken, t + 1)
                    ready = (lambda i: norm.wait_chunk(pe, i)) if isinstance(t, int) and t == 0 else None
                    w.multiply(pe, t, av, [(P, h, l) for h, l in up], cut_set(k, av), ready)

            def down_step(p, m, n):
                pe.wait_ge(finished, starts[p] + n + 1)
                for s in range(2):
                    t = m * 2 + (down_base(p) + s)
                    pe.wait_ge(taken, t + 1)
                    w.multiply(pe, t, s, [(P, gh[:, i, :], gl[:, i, :]) for i in range(n)], cut_set(k, s))
            stream(pe, up_step, down_step, lambda: None)

        def ext_parts(av):
            return ext[:, av, 0:EP], ext[:, av, EP:W].rearrange("p (b n) -> p b n", b=B)

        @block.scalar
        def _(act):
            norm.act(act)
            act.wait_ge(constants_loaded, 16 * len(CONVOLUTION))

            def up_step(p, m, base):
                for av in range(2):
                    act.wait_ge(w.multiplied, m * 2 + (base + av + 3))
                    ep, es = ext_parts(av)
                    bs = cut_set(k, av)
                    ch = m + (starts[p] + av * FC)
                    act.wait_ge(finished, m + (starts[p] + 1))
                    act.activation(in_cuts(y[:, av, :]), bs, ACT.Identity, bias=c["conv_b"][:, layer, bass.ds(ch, 1)],
                                   scale=c["conv_w"][:, layer, 2, bass.ds(ch, 1)])
                    head = (CUTS - 1) * CUT
                    act.activation(ep[:, 2:2 + head].rearrange("p (b n) -> p b n", n=CUT), bs[:, 0:CUTS - 1, :], ACT.Copy)
                    act.activation(ep[:, 2 + head:EP], bs[:, CUTS - 1, 0:SEQ - head], ACT.Copy)
                    act.activation(es[:, :, 2:ES], bs[:, CUTS - 1, SEQ - head:].rearrange("p (b n) -> p b n", b=B), ACT.Copy).then_inc(placed, 1)
                act.wait_ge(convolved, m + (starts[p] + 1))
                act.activation(y[:, 0, :], y[:, 0, :], ACT.Silu).then_inc(silued, 1)
                act.wait_ge(gated, m + (starts[p] + 1))
                if p and isinstance(m, int):
                    act.wait_ge(w.multiplied, down_base(p - 1) + KC + 2)
                act.activation(gh[:, bass.ds(m, 1), :].rearrange("p a n -> p (a n)"), y[:, 1, :], ACT.Copy).then_inc(rounded, 1)
            stream(act, up_step, lambda p, m, n: None)

        @block.vector
        def _(dve):
            dve.sem_inc(taken, 2)
            dve.sem_inc(finished, 1)
            norm.dve(dve)
            dve.wait_ge(constants_loaded, 16 * len(CONVOLUTION))
            dve.memset(ext[:, :, 0:2], 0.0)

            def convolve(p, m, base):
                for av in range(2):
                    ep, es = ext_parts(av)
                    ch = m + (starts[p] + av * FC)
                    dve.tensor_copy(es[:, :, 0:2], c["conv_state"][:, layer, bass.ds(ch, 1), :].rearrange("p a (b n) -> p (a b) n", b=B))
                    wait_apart(k, dve, placed, m * 2 + (2 * starts[p] + av + 1))
                    dve.drain().then_inc(taken, 1)
                    tail = tails[:, bass.ds(ch, 1), :].rearrange("p a n -> p (a n)")
                    dve.tensor_copy(tail[:, 0:2], ep[:, SEQ:EP])
                    dve.tensor_copy(tail[:, 2:].rearrange("p (b n) -> p b n", b=B), es[:, :, L:ES])
                    for tap in (1, 0):
                        wt = c["conv_w"][:, layer, tap, bass.ds(ch, 1)]
                        dve.scalar_tensor_tensor(out=y[:, av, 0:SEQ], in0=ep[:, tap:tap + SEQ], scalar=wt, in1=y[:, av, 0:SEQ],
                                                 op0=ALU.mult, op1=ALU.add)
                        dve.scalar_tensor_tensor(out=samples(y[:, av, :]), in0=es[:, :, tap:tap + L], scalar=wt, in1=samples(y[:, av, :]),
                                                 op0=ALU.mult, op1=ALU.add)
                        last = dve.drain()
                    if av == 0:
                        last.then_inc(convolved, 1)
                dve.wait_ge(silued, m + (starts[p] + 1))
                dve.tensor_tensor(y[:, 1, :], y[:, 0, :], y[:, 1, :], ALU.mult).then_inc(gated, 1)

            def finish(p, m):
                dve.wait_ge(rounded, m + (starts[p] + 1))
                low = gl[:, bass.ds(m, 1), :].rearrange("p a n -> p (a n)")
                high = gh[:, bass.ds(m, 1), :].bitcast(F32).rearrange("p a n -> p (a n)")
                dve.tensor_tensor(low, y[:, 1, :], high, ALU.subtract).then_inc(finished, 1)

            for p, n in enumerate(PARTS):
                with dve.Fori(0 if p == 0 else 1, n) as m:
                    convolve(p, m, None)
                    finish(p, m)
                if p + 1 < len(PARTS):
                    convolve(p + 1, 0, None)
                with dve.Fori(0, KC // 2) as m:
                    for s in range(2):
                        dve.wait_ge(w.multiplied, m * 2 + (down_base(p) + s + 3))
                        xm = in_cuts(x[:, m * 2 + s, :])
                        dve.tensor_tensor(xm, xm, cut_set(k, s), ALU.add).then_inc(taken, 1)
                dve.drain()
                if p + 1 < len(PARTS):
                    finish(p + 1, 0)


def store(k, pairs_):
    with ExitStack() as ctx:
        stored = k.sem(ctx, "stored")
        block = ctx.enter_context(k.nc.Block())

        @block.sync
        def _(sp):
            for dst, src in pairs_:
                sp.dma_start(dst, src).then_inc(stored, 16)
            sp.wait_ge(stored, 16 * len(pairs_))


CONSTANTS = dict(
    page_table=[1, B * PAGES],
    ident=[P, P], ones=[P, P], halves=[P, P], flip=[P, P], edge_mask=[P, P], block_mask=[P, 32],
    win_mask=[ROWS, L], sum_heads=[ROWS, G * L], spread_heads=[G * L, ROWS], diag=[P, H], branch=[P, 4],
    shift=[P, G, 2, P], norm_bias=[P, WHOLE + 1], norm_scale=[P, WHOLE + 1], onehot=[BUCKETS + 1, RW],
    head_pick=[P, NORMED, 2 * NORMED], head_spread=[2 * NORMED, NORMED, P], head_scale=[2 * NORMED, 2], head_bias=[2 * NORMED, 2],
    relx=[BUCKETS + 1, H], gains=[P, NORMED + 2], xk_gain=[P, 2], g_mix=[P, 2, KC], g_mem=[P, 2, KC],
    g_ffn=[P, 2, KC], cmp_pos=[P, 2, L2], cmp_b1=[P, 2], cmp_w2=[P, 2, HD], cmp_b2k=[P, 1], cmp_b2v=[P, P],
    pool_scale=[P, NPC], pool_counts=[P, 4, 16], conv_b=[P, 2, 2 * FC], conv_w=[P, 2, 3, 2 * FC],
    conv_state=[P, 2, 2 * FC, 2 * B],
)


SMALL_INTEGERS = ("page_table",)
TABLES = ["onehot", "relx", "flip"]
COMPRESSION = ["shift", "cmp_pos", "cmp_b1", "cmp_w2", "cmp_b2k", "cmp_b2v"]
ATTENTION = ["edge_mask", "block_mask", "win_mask", "sum_heads", "spread_heads", "diag", "branch"]
HEADS = ["head_pick", "head_spread", "head_scale", "head_bias"]
POOLING = ["pool_scale", "pool_counts"]
CONVOLUTION = ["conv_b", "conv_w", "conv_state"]
COMMON = [n for n in CONSTANTS if n not in HEADS + TABLES + COMPRESSION + ATTENTION + POOLING + CONVOLUTION]


def decoder(nc, ins, outs, n_pages):
    with ExitStack() as ctx:
        k = Kernel(nc, ctx, ins, outs)
        k.n_pages = n_pages
        k.ps = ctx.enter_context(nc.psum_tensor("banks", [P, 8, 512], F32))
        k.cst = {}
        k.passed = ctx.enter_context(nc.semaphore("passed"))
        k.row_dram = nc.dram_tensor("bias_row_scratch", [H, RW], F32, kind="Internal").ap()
        x = k.sb(ctx, "x", [P, KC, T])
        k.mem_k = k.sb(ctx, "mem_keys", [P, 2, 2, NMEM])
        k.mem_v = k.sb(ctx, "mem_values", [P, 2, 2, 2 * P])
        load_constants(k, ctx, COMMON)

        def two_parts(octx, name, n):
            return tuple(k.sb(octx, name + x, [P, n, T], F32R) for x in ("_high", "_low"))

        def whole_terms(parts, n):
            return [(P, parts[0][:, kk, :], parts[1][:, kk, :]) for kk in range(n)]

        def add(dve, m, banks):
            return dve.tensor_tensor(in_cuts(x[:, m, :]), in_cuts(x[:, m, :]), banks, ALU.add)

        def copy_to(z):
            return lambda dve, m, banks: dve.tensor_copy(in_cuts(z[:, m, :]), banks)

        def norm_of(x, parts, gain, spare):
            room = (spare[:, 0:2, :], spare[:, 2, :], spare[:, 3, :])
            return lambda ctx, loaded: Norm(k, ctx, x, parts, gain, T, room, loaded)

        def ffn(layer):
            with ExitStack() as f:
                xn = two_parts(f, "ffn_in", KC)
                conv_ffn(k, layer, xn, x)

        with ExitStack() as m:
            mem = k.sb(m, "memory", [P, KC, NMEM])
            memn = k.sb(m, "memory_normed", [P, KC, NMEM])
            w = k.sb(m, "mem_weights", [P, 2, KC, 4 * P])
            load_constants(k, m, [], [(mem[:], ins["mem"].rearrange("k p t -> p k t"))] +
                           [(w[:, layer, :, :], ins["w_mem"][layer]) for layer in range(2)])
            for layer in range(2):
                memory_kv(k, layer, mem, memn, w[:, layer, :, :])
        mix = x
        with ExitStack() as l0:
            comp_k = k.sb(l0, "compressed_keys", [P, B + 1, NCS])
            comp_v = k.sb(l0, "compressed_values", [NCS, B + 1, P])
            zs = k.sb(l0, "z_samples", [P, NZ, TS])
            load_constants(k, l0, ATTENTION)
            k.row_tail = k.sb(l0, "row_tail_bias", [ROWS, TAIL])
            k.row_far = k.sb(l0, "row_far_bias", [ROWS, 2])
            k.row_blocks = k.sb(l0, "row_block_bias", [ROWS, NCS])
            k.row_select = k.sb(l0, "row_select_bias", [ROWS, NBS])
            k.row_window = k.sb(l0, "row_window_bias", [ROWS, WINDOW + L])
            lz = l0.enter_context(ExitStack())
            z = k.sb(lz, "z", [P, NZ, T])
            with ExitStack() as n:
                x0 = z[:, NZ - KC:NZ, :]
                xn = two_parts(n, "in0", KC)
                project(k, "w_in0", ins["w_in0"], NZ, whole_terms(xn, KC), norm_of(x0, xn, k.cst["g_mix"][:, 0, :], mix),
                        copy_to(z), load=(x0, ins["x"]))
            head_norms(k, z, NORMED, 0, 0)
            compress(k, z, mix, comp_k, comp_v)
            with ExitStack() as n:
                k.near_bias = k.sb(n, "near_bias", [P, H, 256])
                k.block_bias = k.sb(n, "block_bias", [P, H, 32])
                bias_tables(k)
                vals = k.sb(n, "prompt_values", [P, 2, QT, P])
                token_major_values(k, z, vals)
                prompt_attention(k, z, zs, vals, comp_k, comp_v, mix)
            memory_attention(k, 0, z[:, Z_XQ:Z_XQ + 2, :], mix[:, R:R + 2, :])
            lz.close()
            sample_attention(k, zs, comp_k, comp_v, mix)
        with ExitStack() as n:
            parts = two_parts(n, "mixed0", KC)
            project(k, "w_out0", ins["w_out0"], KC, whole_terms(parts, KC),
                    lambda ctx, loaded: Split(k, ctx, mix, parts, [(P, i) for i in range(KC)]), add, late_load=(x, ins["x"]))
        ffn(0)
        with ExitStack() as l1:
            mix = k.sb(l1, "mixed", [P, NPC + 2, T])
            with ExitStack() as lz:
                z = k.sb(lz, "z_pool", [P, NPC + 2, T])
                with ExitStack() as n:
                    xn = two_parts(n, "in1", KC)
                    project(k, "w_in1", ins["w_in1"], NPC + 2, whole_terms(xn, KC),
                            norm_of(x, xn, k.cst["g_mix"][:, 1, :], mix), copy_to(z))
                head_norms(k, z[:, NPC:NPC + 2, :], 2, NORMED, 1)
                pool_mixer(k, z, mix)
                memory_attention(k, 1, z[:, NPC:NPC + 2, :], mix[:, NPC:NPC + 2, :])
            parts = two_parts(l1, "mixed1", NPC + 2)
            rows = [PCH] * NPC + [P] * 2
            project(k, "w_out1", ins["w_out1"], KC, [(r, parts[0][0:r, i, :], parts[1][0:r, i, :]) for i, r in enumerate(rows)],
                    lambda ctx, loaded: Split(k, ctx, mix, parts, [(r, i) for i, r in enumerate(rows)]), add)
        ffn(1)
        store(k, [(outs["y"], x[:])])


def rel_buckets(dist):
    exact = BUCKETS // 2
    n = np.maximum(dist, 0)
    nf = np.maximum(n, 1).astype(np.float32)
    large = exact + (np.log(nf / np.float32(exact)) / np.float32(np.log(128 / exact)) * np.float32(BUCKETS - exact)).astype(np.int32)
    return np.where(n < exact, n, np.minimum(large, BUCKETS - 1))


def shape_constants():
    f = np.float32
    eye = np.eye(P, dtype=f)
    out = dict(ident=eye, ones=np.ones((P, P), f), halves=np.kron(np.eye(2), np.ones((HD, HD))).astype(f),
               flip=eye[::-1].copy())
    q, kk = np.arange(P)[:, None], np.arange(P)[None, :]
    out["edge_mask"] = np.where(kk >= q, 0, NEG).astype(f)
    m = np.arange(32)[None, :] - 16
    out["block_mask"] = (q - 63 - CB * m >= 0).astype(f)
    row_q = (np.arange(ROWS) % L)[:, None]
    out["win_mask"] = np.where(np.arange(L)[None, :] >= row_q, 0, NEG).astype(f)
    rows = np.arange(ROWS)
    gq = rows // GR * L + rows % L
    out["sum_heads"] = (gq[:, None] == np.arange(G * L)[None, :]).astype(f)
    out["spread_heads"] = out["sum_heads"].T.copy()
    diag = np.zeros((P, H), f)
    for j in range(3):
        diag[32 * j + np.arange(H), np.arange(H)] = 1
    out["diag"] = diag
    out["branch"] = np.zeros((P, 4), f)
    for j in range(3):
        out["branch"][32 * j:32 * j + H, j] = 1
    shift = np.zeros((P, G, 2, P), f)
    for g in range(G):
        for lp in range(2):
            shift[g * HD + np.arange(HD), g, lp, lp * HD + np.arange(HD)] = 1
    out["shift"] = shift
    eps = 1e-6
    is_q = np.array([i not in (Z_KS, Z_KW) for i in range(WHOLE)])
    scale = np.where(is_q, 1.0 / HD / SCALE ** 2, 1.0 / HD)
    bias = np.where(is_q, eps / SCALE ** 2, eps)
    out["norm_scale"] = np.broadcast_to(np.append(scale, 1.0 / D_MODEL), (P, WHOLE + 1)).astype(f)
    out["norm_bias"] = np.broadcast_to(np.append(bias, eps), (P, WHOLE + 1)).astype(f)
    pick = np.zeros((P, NORMED, 2 * NORMED), f)
    for m in range(NORMED):
        for y in range(2):
            pick[y * HD:(y + 1) * HD, m, 2 * m + y] = 1
    out["head_pick"] = pick
    out["head_spread"] = pick.transpose(2, 1, 0).copy()
    out["head_scale"] = np.stack([np.repeat(scale[:NORMED], 2), np.full(2 * NORMED, scale[0])], 1).astype(f)
    out["head_bias"] = np.stack([np.repeat(bias[:NORMED], 2), np.full(2 * NORMED, bias[0])], 1).astype(f)
    dist = 255 - np.arange(RW)
    onehot = np.zeros((BUCKETS + 1, RW), f)
    onehot[np.where(dist >= 0, rel_buckets(dist), BUCKETS), np.arange(RW)] = 1
    out["onehot"] = onehot
    pos = np.arange(16)
    counts = np.stack([w / np.minimum(w, pos + 1) for w in POOLW])
    out["pool_counts"] = np.broadcast_to(counts, (P, 4, 16)).astype(f)
    return out


def lay_out(a):
    f = np.float32
    con = np.ascontiguousarray
    d = shape_constants()

    def chunks(w, cols=None, m=P, kchunks=None):
        kk = w.shape[0] // P
        return con(w.reshape(kk, P, -1, m).transpose(2, 1, 0, 3).reshape(-1, P, kk * m))

    def feature(g):
        return con(g.reshape(g.shape[0], -1, P).transpose(2, 0, 1))

    x = np.concatenate([a["x_prompt"][0], a["x_sample"].reshape(TS, D_MODEL)], 0)
    d["x"] = con(x.T.reshape(KC, P, T))
    d["mem"] = con(a["mem_prompt"][0].T.reshape(KC, P, NMEM))
    d["relx"] = np.concatenate([a["rel_bias"], np.full((1, H), NEG, f)], 0)
    wi = a["w_in_nsa"][0]
    qw = wi[:, :H * HD].reshape(D_MODEL, G, R, HD).transpose(0, 2, 1, 3).reshape(D_MODEL, H * HD)
    kvw = wi[:, H * HD:H * HD + 6 * P].reshape(D_MODEL, 6, P)
    gw = wi[:, H * HD + 6 * P:H * HD + 6 * P + 3 * H].reshape(D_MODEL, H, 3)
    gate = np.zeros((D_MODEL, 4, 32), f)
    gate[:, 0:3, 0:H] = gw.transpose(0, 2, 1)
    xq = wi[:, H * HD + 6 * P + 3 * H:]
    w0 = np.concatenate([qw, kvw[:, 2], kvw[:, 4], xq, kvw[:, 0], kvw[:, 1], kvw[:, 3], kvw[:, 5], gate.reshape(D_MODEL, P)], 1)
    d["w_in0"] = chunks(w0)
    w1 = a["w_in_pool"][0]
    pool = np.zeros((D_MODEL, NPC, P), f)
    pool[:, :, 0:PCH] = w1[:, :NPC * PCH].reshape(D_MODEL, NPC, PCH)
    d["w_in1"] = chunks(np.concatenate([pool.reshape(D_MODEL, NPC * P), w1[:, NPC * PCH:]], 1))
    wo = a["w_out"][0]
    wo0 = np.concatenate([wo[:H * HD].reshape(G, R, HD, D_MODEL).transpose(1, 0, 2, 3).reshape(H * HD, D_MODEL), wo[H * HD:]], 0)
    d["w_out0"] = chunks(wo0)
    wo = a["w_out"][1]
    wp = np.zeros((NPC, P, D_MODEL), f)
    wp[:, 0:PCH] = wo[:NPC * PCH].reshape(NPC, PCH, D_MODEL)
    d["w_out1"] = chunks(np.concatenate([wp.reshape(NPC * P, D_MODEL), wo[NPC * PCH:]], 0))
    d["w_mem"] = con(a["w_mem_kv"].reshape(2, KC, P, 4 * P).transpose(0, 2, 1, 3))
    d["w_up"] = con(a["w_up"].reshape(2, KC, P, 2 * FC, P).transpose(0, 3, 2, 1, 4).reshape(2, 2 * FC, P, KC * P))
    d["w_down"] = con(a["w_down"].reshape(2, FC, P, KC, P).transpose(0, 3, 2, 1, 4).reshape(2, KC, P, FC * P))
    twice = lambda g: np.concatenate([g, g], -1)
    qg, kg, xqg = twice(a["q_gain_nsa"][0]), twice(a["k_gain_nsa"][0]), twice(a["xq_gain"])
    d["gains"] = con(np.stack([qg] * R + [kg] * 2 + [xqg[0]] * 2 + [xqg[1]] * 2, 1))
    d["xk_gain"] = con(twice(a["xk_gain"]).T)
    for n in ("g_mix", "g_mem", "g_ffn"):
        d[n] = feature(a[n])
    d["cmp_pos"] = con(a["cmp_pos"][0].reshape(2, L2, 2, HD).transpose(2, 3, 0, 1).reshape(P, 2, L2))
    d["cmp_w1"] = con(a["cmp_w1"][0].reshape(2, L2, 2, HD, P).transpose(2, 3, 0, 1, 4).reshape(P, 2, L2, P))
    d["cmp_b1"] = con(a["cmp_b1"][0].T)
    d["cmp_w2"] = con(a["cmp_w2"][0].transpose(1, 0, 2))
    d["cmp_b2k"] = con(twice(a["cmp_b2"][0, 0])[:, None])
    d["cmp_b2v"] = con(np.broadcast_to(twice(a["cmp_b2"][0, 1]), (P, P)))
    ps = np.zeros((P, NPC), f)
    ps[0:PCH] = a["pool_scale"][0].reshape(NPC, PCH).T
    d["pool_scale"] = ps
    d["conv_b"] = feature(a["conv_b"])
    d["conv_w"] = con(a["conv_w"].reshape(2, 3, 2 * FC, P).transpose(3, 0, 1, 2))
    d["conv_state"] = con(a["state_ffn_conv"].reshape(2, B, 2, 2 * FC, P).transpose(4, 0, 3, 1, 2).reshape(P, 2, 2 * FC, 2 * B))
    d["pool_state"] = con(a["state_pool"][0].reshape(B, PST, NPC, PCH).transpose(3, 2, 0, 1).reshape(PCH, NPC, B * PST))
    d["w_grp"] = con(a["w_pool_grp"][0].reshape(4, 2, PCH, PG).transpose(2, 0, 1, 3).reshape(PCH, NPC, PG))
    cache = a["cache_nsa_kv"][0]
    n = cache.shape[0]
    cmp_rows = cache[:, :, 0:2].reshape(n, 2, L2, 2, 2, G, HD)
    d["cmp_pages"] = con(cmp_rows.transpose(0, 3, 6, 4, 2, 5, 1).reshape(n, P, 2 * L2 * G * 2))
    d["kv_pages"] = np.concatenate([cache[:, :, 2].reshape(n, PAGE, P).transpose(0, 2, 1), cache[:, :, 3].reshape(n, PAGE, P)], 2)
    win = a["cache_nsa_win"][0]
    d["win_k"] = con(win[:, :, 0].reshape(B, WINDOW, P).transpose(0, 2, 1))
    d["win_v"] = con(win[:, :, 1].reshape(B, WINDOW, P))
    cm = a["cache_mem_kv"]
    d["cmem_k"] = con(cm[:, :, :, 0].reshape(2, B, NMEM, 2, P).transpose(0, 1, 4, 3, 2).reshape(2, B, P, 2 * NMEM))
    d["cmem_v"] = con(cm[:, :, :, 1].reshape(2, B, 2, P, 2 * P).transpose(0, 1, 3, 2, 4).reshape(2, B, P, 4 * P))
    d["page_table"] = con(a["page_table"].astype(np.int32).reshape(1, B * PAGES))
    return {name: con(v) for name, v in d.items()}


_OUTS = dict(y=[P, KC, T], rows=[P, Z_GATE - Z_KS, T], win_k=[B, P, WINDOW], win_v=[B, WINDOW, P],
             mem_k=[2, P, 2, NMEM], mem_v=[2, P, 2, 2 * P], pool=[PCH, NPC, PST * (1 + B)],
             conv=[2, P, 2 * FC, 2 * (1 + B)])


def kernel(**inputs):
    import concourse.bacc as bacc
    from concourse.bass_utils import run_bass_kernel_spmd

    a = {n: np.asarray(v) for n, v in inputs.items()}
    arrays = lay_out(a)
    nc = bacc.Bacc("TRN2", target_bir_lowering=False, num_devices=1, dynamic_dma_scratch_size=1024)
    ins = {n: nc.dram_tensor(f"in_{n}", v.shape, mybir.dt.from_np(v.dtype), kind="ExternalInput").ap() for n, v in arrays.items()}
    outs = {n: nc.dram_tensor(f"out_{n}", s, F32, kind="ExternalOutput").ap() for n, s in _OUTS.items()}
    decoder(nc, ins, outs, a["cache_nsa_kv"].shape[1])
    r = run_bass_kernel_spmd(nc, [{f"in_{n}": v for n, v in arrays.items()}], core_ids=[0]).results[0]
    o = {n: r[f"out_{n}"] for n in _OUTS}

    y = o["y"].transpose(2, 1, 0).reshape(T, D_MODEL)
    y_prompt, y_sample = y[None, :SEQ], y[SEQ:].reshape(B, L, D_MODEL)
    at = {s: c - Z_KS for s, c in enumerate((Z_KC, Z_VC, Z_KS, Z_VS, Z_KW, Z_VW))}
    rows = np.stack([o["rows"][:, at[s], :].T.reshape(T, G, HD) for s in range(6)], 1)
    kv_p = rows[None, None, :SEQ, 0:4]
    kv_s = rows[SEQ:, 0:4].reshape(1, B, L, 4, G, HD)
    win_p = rows[None, None, SEQ - WINDOW:SEQ, 4:6]
    new = rows[SEQ:, 4:6].reshape(B, L, 2, G, HD)
    old = np.stack([o["win_k"].transpose(0, 2, 1), o["win_v"]], 2)[:, :WINDOW - L].reshape(B, WINDOW - L, 2, G, HD)
    win_s = np.concatenate([old, new], 1)[None]
    mk = o["mem_k"].transpose(0, 3, 2, 1).reshape(2, NMEM, XH, HD)
    mv = o["mem_v"].transpose(0, 2, 1, 3).reshape(2, NMEM, XH, HD)
    mem_kv = np.stack([mk, mv], 2)[:, None]
    pool = o["pool"].reshape(PCH, NPC, 1 + B, PST).transpose(2, 3, 1, 0).reshape(1 + B, PST, NPC * PCH)
    conv = o["conv"].reshape(2, P, 2 * FC, 1 + B, 2).transpose(0, 3, 4, 2, 1).reshape(2, 1 + B, 2, 2 * DFF)
    got = (y_prompt, y_sample, kv_p, kv_s, win_p, win_s, mem_kv, pool[None, :1], pool[None, 1:], conv[:, :1], conv[:, 1:])
    return tuple(np.ascontiguousarray(v, dtype=np.float32) for v in got)
```
